# Optimizing a Trainium2 kernel written in Bass

```python
import math
import jax, jax.numpy as jnp
from jax import lax
import numpy as np

D_MODEL = 1024
BATCH = 1
SEQ = 512
DEPTH = 1

CTX_LEN = 256
GRID_W = 64
D_MIX = D_MODEL
D_CONV = D_MIX // 2
D_RWKV = D_MIX - D_CONV
RWKV_HEAD = 64
RWKV_HEADS = D_RWKV // RWKV_HEAD
W_LORA = 64
A_LORA = 64
G_LORA = 128
N_DIR = 2
D_FF = ((8 * D_MODEL // 3 + 127) // 128) * 128
PROJ = 3 * D_CONV + 3 * D_RWKV + W_LORA + A_LORA + G_LORA
RMS_EPS = 1e-6
GN_EPS = 64e-5
DECAY_SCALE = math.exp(-0.5)


def rms_norm(x, g):
    xf = x.astype(jnp.float32)
    y = xf * lax.rsqrt(jnp.mean(xf * xf, axis=-1, keepdims=True) + RMS_EPS)
    return (y * g.astype(jnp.float32)).astype(x.dtype)

def modulate(h, shift, scale):
    return h * (1 + scale) + shift

def split_proj(p):
    sizes = (D_CONV, D_CONV, D_CONV, D_RWKV, D_RWKV, D_RWKV, W_LORA, A_LORA, G_LORA)
    idx = [int(i) for i in np.cumsum(sizes)[:-1]]
    return jnp.split(p, idx, axis=-1)

def shortconv1d(u, w):
    up = jnp.pad(u, ((0, 0), (1, 1), (0, 0)))
    return up[:, :-2] * w[0] + up[:, 1:-1] * w[1] + up[:, 2:] * w[2]

def dwconv_grid(u, w, b, rows, cols):
    bsz, t, ch = u.shape
    img = u.reshape(bsz, rows, cols, ch)
    out = lax.conv_general_dilated(img, w[:, :, None, :].astype(u.dtype), (1, 1), "SAME",
                                   dimension_numbers=("NHWC", "HWIO", "NHWC"),
                                   feature_group_count=ch)
    return out.reshape(bsz, t, ch) + b

def to_heads(t):
    return t.astype(jnp.float32).reshape(t.shape[0], t.shape[1], RWKV_HEADS, RWKV_HEAD)

def wkv_scan(state0, r, decay, kk, b, v, k, reverse):
    def step(S, inp):
        r_t, w_t, kk_t, b_t, v_t, k_t = inp
        sa = jnp.einsum("bhvk,bhk->bhv", S, kk_t)
        S = (S * w_t[:, :, None, :] - sa[..., None] * b_t[:, :, None, :]
             + v_t[..., None] * k_t[:, :, None, :])
        return S, jnp.einsum("bhvk,bhk->bhv", S, r_t)
    xs = tuple(jnp.swapaxes(t, 0, 1) for t in (r, decay, kk, b, v, k))
    S, ys = lax.scan(step, state0, xs, reverse=reverse)
    return S, jnp.swapaxes(ys, 0, 1)

def rwkv_scans(r, k, v, w_lo, a_lo, lp, init):
    kk = to_heads(k * lp["k_k"])
    kk = kk * lax.rsqrt(jnp.maximum(jnp.sum(kk * kk, axis=-1, keepdims=True), 1e-24))
    rh, vh = to_heads(r), to_heads(v)
    y_sum = None
    finals = []
    for d in range(N_DIR):
        decay = jnp.exp(-DECAY_SCALE * jax.nn.sigmoid(lp["w0"][d] + jnp.tanh(w_lo) @ lp["w_up"][d]))
        a = jax.nn.sigmoid(lp["a0"][d] + a_lo @ lp["a_up"][d])
        k_d = k * (1 + (a - 1) * lp["k_a"])
        state, y = wkv_scan(init[d], rh, to_heads(decay), kk, kk * to_heads(a), vh, to_heads(k_d),
                            reverse=(d == 1))
        y_sum = y if y_sum is None else y_sum + y
        finals.append(state)
    return y_sum, finals

def rwkv_output(y, r, k, v, g_lo, lp):
    bsz, t = y.shape[:2]
    mu = jnp.mean(y, axis=-1, keepdims=True)
    var = jnp.mean(jnp.square(y - mu), axis=-1, keepdims=True)
    yn = ((y - mu) * lax.rsqrt(var + GN_EPS)).reshape(bsz, t, D_RWKV) * lp["ln_g"] + lp["ln_b"]
    bonus = jnp.sum(to_heads(r) * to_heads(k) * lp["r_k"].astype(jnp.float32), axis=-1, keepdims=True) * to_heads(v)
    gate = jax.nn.sigmoid(g_lo) @ lp["g_up"]
    return ((yn + bonus.reshape(bsz, t, D_RWKV)) * gate).astype(r.dtype)

def mixer_block(h, lp, init, need_output):
    cb, cc, cx, r, k, v, w_lo, a_lo, g_lo = split_proj(h @ lp["w_in"])
    y, finals = rwkv_scans(r, k, v, w_lo, a_lo, lp, init)
    if not need_output:
        return None, finals
    y_conv = cb * shortconv1d(cc * cx, lp["conv_a_w"])
    y_rwkv = rwkv_output(y, r, k, v, g_lo, lp)
    return jnp.concatenate([y_conv, y_rwkv], axis=-1) @ lp["w_out"], finals

def conv_ffn(h, lp, rows, cols):
    gate, val = jnp.split(h @ lp["ffn_w_up"], 2, axis=-1)
    gate = dwconv_grid(gate, lp["ffn_conv_w"], lp["ffn_conv_b"], rows, cols)
    return (jax.nn.silu(gate) * val) @ lp["ffn_w_down"]

def first_inputs(seed: int = 0) -> dict:
    key = jax.random.key(seed)
    ks = jax.random.split(key, 32)
    L, D = DEPTH, D_MODEL

    def nrm(k, shape, s):
        return jax.random.normal(k, shape, jnp.float32) * s

    return {
        "x": nrm(ks[0], (BATCH, SEQ, D), 1.0),
        "c": nrm(ks[1], (BATCH, D), 1.0),
        "ctx": nrm(ks[2], (BATCH, CTX_LEN, D), 1.0),
        "c_ctx": nrm(ks[3], (D,), 1.0),
        "ada_w": nrm(ks[4], (L, D, 6 * D), 0.5 * D ** -0.5),
        "ada_b": nrm(ks[5], (L, 6 * D), 0.01),
        "norm1_g": 1.0 + nrm(ks[6], (L, D), 0.1),
        "norm2_g": 1.0 + nrm(ks[7], (L, D), 0.1),
        "w_in": nrm(ks[8], (L, D, PROJ), D ** -0.5),
        "conv_a_w": nrm(ks[9], (L, 3, D_CONV), 3 ** -0.5),
        "rw_w0": nrm(ks[10], (L, N_DIR, D_RWKV), 0.5),
        "rw_w_up": nrm(ks[11], (L, N_DIR, W_LORA, D_RWKV), 0.5 * W_LORA ** -0.5),
        "rw_a0": nrm(ks[12], (L, N_DIR, D_RWKV), 0.5),
        "rw_a_up": nrm(ks[13], (L, N_DIR, A_LORA, D_RWKV), 0.5 * A_LORA ** -0.5),
        "rw_k_k": 0.85 + nrm(ks[14], (L, D_RWKV), 0.05),
        "rw_k_a": 1.0 + nrm(ks[15], (L, D_RWKV), 0.05),
        "rw_r_k": nrm(ks[16], (L, RWKV_HEADS, RWKV_HEAD), 0.1),
        "rw_g_up": nrm(ks[17], (L, G_LORA, D_RWKV), G_LORA ** -0.5),
        "rw_ln_g": 1.0 + nrm(ks[18], (L, D_RWKV), 0.1),
        "rw_ln_b": nrm(ks[19], (L, D_RWKV), 0.01),
        "w_out": nrm(ks[20], (L, D_MIX, D), D_MIX ** -0.5),
        "ffn_w_up": nrm(ks[21], (L, D, 2 * D_FF), D ** -0.5),
        "ffn_conv_w": nrm(ks[22], (L, 3, 3, D_FF), 1.0 / 3.0),
        "ffn_conv_b": nrm(ks[23], (L, D_FF), 0.01),
        "ffn_w_down": nrm(ks[24], (L, D_FF, D), D_FF ** -0.5),
        "final_g": 1.0 + nrm(ks[25], (D,), 0.1),
    }

def first_block(x, c, ctx, c_ctx, ada_w, ada_b, norm1_g, norm2_g, w_in, conv_a_w,
              rw_w0, rw_w_up, rw_a0, rw_a_up, rw_k_k, rw_k_a, rw_r_k, rw_g_up, rw_ln_g, rw_ln_b,
              w_out, ffn_w_up, ffn_conv_w, ffn_conv_b, ffn_w_down, final_g):
    bsz = x.shape[0]
    rows = x.shape[1] // GRID_W
    zero_state = jnp.zeros((bsz, RWKV_HEADS, RWKV_HEAD, RWKV_HEAD), jnp.float32)
    for l in range(DEPTH):
        last = l == DEPTH - 1
        lp = {
            "w_in": w_in[l], "conv_a_w": conv_a_w[l], "w0": rw_w0[l], "w_up": rw_w_up[l],
            "a0": rw_a0[l], "a_up": rw_a_up[l], "k_k": rw_k_k[l], "k_a": rw_k_a[l],
            "r_k": rw_r_k[l], "g_up": rw_g_up[l], "ln_g": rw_ln_g[l], "ln_b": rw_ln_b[l],
            "w_out": w_out[l], "ffn_w_up": ffn_w_up[l], "ffn_conv_w": ffn_conv_w[l],
            "ffn_conv_b": ffn_conv_b[l], "ffn_w_down": ffn_w_down[l],
        }
        mod = jax.nn.silu(c) @ ada_w[l] + ada_b[l]
        sh1, sc1, g1, sh2, sc2, g2 = [m[:, None, :] for m in jnp.split(mod, 6, axis=-1)]
        csh1, csc1, cg1, csh2, csc2, cg2 = jnp.split(jax.nn.silu(c_ctx) @ ada_w[l] + ada_b[l], 6, axis=-1)

        hc = modulate(rms_norm(ctx, norm1_g[l]), csh1, csc1)
        out_c, ctx_states = mixer_block(hc, lp, (zero_state, zero_state), not last)

        hx = modulate(rms_norm(x, norm1_g[l]), sh1, sc1)
        out_x, _ = mixer_block(hx, lp, ctx_states, True)
        x = x + g1 * out_x
        hx = modulate(rms_norm(x, norm2_g[l]), sh2, sc2)
        x = x + g2 * conv_ffn(hx, lp, rows, GRID_W)

        if not last:
            ctx = ctx + cg1 * out_c
            hc = modulate(rms_norm(ctx, norm2_g[l]), csh2, csc2)
            ctx = ctx + cg2 * conv_ffn(hc, lp, 1, ctx.shape[1])
    return rms_norm(x, final_g)


MIX_WIDTH = D_MODEL
HG_HEADS = 4
HG_DK = 128
HG_DV = 128
HG_KEY_WIDTH = HG_HEADS * HG_DK
HG_VAL_WIDTH = HG_HEADS * HG_DV
HG_CHUNK = 64
ATT_HEADS = 8
ATT_KV_HEADS = 2
ATT_GROUP = ATT_HEADS // ATT_KV_HEADS
ATT_HD = 64
ATT_Q_WIDTH = ATT_HEADS * ATT_HD
ATT_KV_WIDTH = ATT_KV_HEADS * ATT_HD
WINDOW = 128
ATT_BLOCK = 128
HG_COLS = 2 * HG_KEY_WIDTH + 2 * HG_VAL_WIDTH
ATT_COLS = ATT_Q_WIDTH + 2 * ATT_KV_WIDTH
IN_COLS = HG_COLS + ATT_COLS
D_FF_2 = 2816
CONV_W = 3
EPS = 1e-6


def rmsnorm(x, w, eps=EPS):
    xf = x.astype(jnp.float32)
    inv = lax.rsqrt(jnp.mean(xf * xf, axis=-1, keepdims=True) + eps)
    return (xf * inv * w.astype(jnp.float32)).astype(x.dtype)

def hgrn2_chunkwise(q, k, v, log_f):
    B, S, H, DK = q.shape
    DV = v.shape[-1]
    n = S // HG_CHUNK

    def to_chunks(a):
        return a.astype(jnp.float32).reshape(B, n, HG_CHUNK, H, a.shape[-1]).transpose(1, 0, 3, 2, 4)

    qc, kc, vc, gc = to_chunks(q), to_chunks(k), to_chunks(v), to_chunks(log_f)
    causal = jnp.tril(jnp.ones((HG_CHUNK, HG_CHUNK), dtype=bool))[:, :, None]

    def step(state, inp):
        qi, ki, vi, gi = inp
        b = jnp.cumsum(gi, axis=2)
        rel = b[:, :, :, None, :] - b[:, :, None, :, :]
        decay = jnp.exp(jnp.where(causal, rel, -jnp.inf))
        scores = jnp.einsum('bhtk,bhsk,bhtsk->bhts', qi, ki, decay)
        intra = jnp.einsum('bhts,bhsv->bhtv', scores, vi)
        inter = jnp.einsum('bhtk,bhkv->bhtv', qi * jnp.exp(b), state)
        b_last = b[:, :, -1:, :]
        new_state = state * jnp.exp(b_last)[:, :, 0, :, None] + jnp.einsum(
            'bhsk,bhsv->bhkv', ki * jnp.exp(b_last - b), vi)
        return new_state, intra + inter

    state0 = jnp.zeros((B, H, DK, DV), jnp.float32)
    _, out = lax.scan(step, state0, (qc, kc, vc, gc))
    return out.transpose(1, 0, 3, 2, 4).reshape(B, S, H, DV)

def sliding_window_attention_with_sinks(q, k, v, sinks):
    B, S = q.shape[0], q.shape[1]
    nb = S // ATT_BLOCK
    scale = 1.0 / math.sqrt(ATT_HD)
    qb = q.astype(jnp.float32).reshape(B, nb, ATT_BLOCK, ATT_KV_HEADS, ATT_GROUP, ATT_HD)

    def band_keys(a):
        ap = jnp.pad(a.astype(jnp.float32), ((0, 0), (ATT_BLOCK, 0), (0, 0), (0, 0)))
        ap = ap.reshape(B, nb + 1, ATT_BLOCK, ATT_KV_HEADS, ATT_HD)
        return jnp.concatenate([ap[:, :-1], ap[:, 1:]], axis=2)

    kb, vb = band_keys(k), band_keys(v)
    scores = jnp.einsum('bnqhgd,bnkhd->bnhgqk', qb, kb) * scale
    qi = jnp.arange(ATT_BLOCK)[:, None]
    kj = jnp.arange(2 * ATT_BLOCK)[None, :]
    dist = qi + ATT_BLOCK - kj
    band = (dist >= 0) & (dist < WINDOW)
    key_pos = jnp.arange(nb)[:, None] * ATT_BLOCK + jnp.arange(2 * ATT_BLOCK)[None, :] - ATT_BLOCK
    mask = band[None] & (key_pos >= 0)[:, None, :]
    scores = jnp.where(mask[None, :, None, None], scores, -jnp.inf)
    sink = sinks.astype(jnp.float32).reshape(ATT_KV_HEADS, ATT_GROUP)[None, None, :, :, None, None]
    m = jnp.maximum(jnp.max(scores, axis=-1, keepdims=True), sink)
    p = jnp.exp(scores - m)
    denom = jnp.sum(p, axis=-1, keepdims=True) + jnp.exp(sink - m)
    out = jnp.einsum('bnhgqk,bnkhd->bnqhgd', p / denom, vb)
    return out.reshape(B, S, ATT_HEADS * ATT_HD)

def causal_depthwise_conv(a, w, b):
    C = a.shape[-1]
    y = lax.conv_general_dilated(
        a, w[:, None, :].astype(a.dtype), window_strides=(1,), padding=[(CONV_W - 1, 0)],
        dimension_numbers=('NWC', 'WIO', 'NWC'), feature_group_count=C)
    return y + b.astype(a.dtype)

def second_inputs(seed: int = 0) -> dict:
    key = jax.random.key(seed)
    ks = jax.random.split(key, 16)
    f32 = jnp.float32
    nrm = lambda k, shape, s: jax.random.normal(k, shape, f32) * s
    return {
        "x": jax.random.normal(ks[0], (BATCH, SEQ, D_MODEL), f32),
        "norm_mix_w": 1.0 + nrm(ks[1], (DEPTH, D_MODEL), 0.02),
        "w_in": nrm(ks[2], (DEPTH, D_MODEL, IN_COLS), D_MODEL ** -0.5),
        "b_attn": nrm(ks[3], (DEPTH, ATT_COLS), 0.02),
        "lb_logits": nrm(ks[4], (DEPTH + 1, HG_KEY_WIDTH), 0.1),
        "hg_norm_w": 1.0 + nrm(ks[5], (DEPTH, HG_DV), 0.02),
        "sinks": nrm(ks[6], (DEPTH, ATT_HEADS), 0.5),
        "w_out": nrm(ks[7], (DEPTH, MIX_WIDTH, D_MODEL), MIX_WIDTH ** -0.5),
        "norm_ffn_w": 1.0 + nrm(ks[8], (DEPTH, D_MODEL), 0.02),
        "w_gate": nrm(ks[9], (DEPTH, D_MODEL, D_FF_2), D_MODEL ** -0.5),
        "w_up": nrm(ks[10], (DEPTH, D_MODEL, D_FF_2), D_MODEL ** -0.5),
        "conv_w": nrm(ks[11], (DEPTH, CONV_W, D_FF_2), CONV_W ** -0.5),
        "conv_b": nrm(ks[12], (DEPTH, D_FF_2), 0.02),
        "w_down": nrm(ks[13], (DEPTH, D_FF_2, D_MODEL), D_FF_2 ** -0.5),
        "final_norm_w": 1.0 + nrm(ks[14], (D_MODEL,), 0.02),
    }

def second_block(x, norm_mix_w, w_in, b_attn, lb_logits, hg_norm_w, sinks, w_out,
              norm_ffn_w, w_gate, w_up, conv_w, conv_b, w_down, final_norm_w):
    B, S, _ = x.shape
    lb_all = jnp.cumsum(jax.nn.softmax(lb_logits.astype(jnp.float32), axis=0), axis=0)[:DEPTH]
    h = x
    for l in range(DEPTH):
        u = rmsnorm(h, norm_mix_w[l])
        proj = u @ w_in[l]
        hq, hf, hi, hg, att = jnp.split(
            proj, [HG_KEY_WIDTH, 2 * HG_KEY_WIDTH, 2 * HG_KEY_WIDTH + HG_VAL_WIDTH, HG_COLS], axis=-1)
        lb = lb_all[l]
        f = lb + (1.0 - lb) * jax.nn.sigmoid(hf.astype(jnp.float32))
        log_f = jnp.log(f).reshape(B, S, HG_HEADS, HG_DK)
        k_hg = (1.0 - f).reshape(B, S, HG_HEADS, HG_DK)
        q_hg = hq.astype(jnp.float32).reshape(B, S, HG_HEADS, HG_DK) * (HG_DK ** -0.5)
        v_hg = hi.reshape(B, S, HG_HEADS, HG_DV)
        o_hg = hgrn2_chunkwise(q_hg, k_hg, v_hg, log_f)
        o_hg = rmsnorm(o_hg, hg_norm_w[l]).reshape(B, S, HG_VAL_WIDTH)
        o_hg = (o_hg * jax.nn.silu(hg.astype(jnp.float32))).astype(h.dtype)
        att = att + b_attn[l]
        aq, ak, av = jnp.split(att, [ATT_Q_WIDTH, ATT_Q_WIDTH + ATT_KV_WIDTH], axis=-1)
        o_att = sliding_window_attention_with_sinks(
            aq.reshape(B, S, ATT_HEADS, ATT_HD),
            ak.reshape(B, S, ATT_KV_HEADS, ATT_HD),
            av.reshape(B, S, ATT_KV_HEADS, ATT_HD),
            sinks[l]).astype(h.dtype)
        mix = jnp.concatenate([o_hg, o_att], axis=-1)
        h = h + mix @ w_out[l]
        v = rmsnorm(h, norm_ffn_w[l])
        gate = causal_depthwise_conv(v @ w_gate[l], conv_w[l], conv_b[l])
        h = h + (jax.nn.silu(gate) * (v @ w_up[l])) @ w_down[l]
    return rmsnorm(h, final_norm_w)


def setup_inputs(seed=0):
    out = dict(first_inputs(seed))
    for name, value in second_inputs(seed + 1).items():
        if name != "x":
            out[name + "_2"] = value
    return out


def reference(
    x, c, ctx, c_ctx, ada_w, ada_b, norm1_g, norm2_g, w_in, conv_a_w, rw_w0, rw_w_up, rw_a0,
    rw_a_up, rw_k_k, rw_k_a, rw_r_k, rw_g_up, rw_ln_g, rw_ln_b, w_out, ffn_w_up, ffn_conv_w,
    ffn_conv_b, ffn_w_down, final_g, norm_mix_w_2, w_in_2, b_attn_2, lb_logits_2, hg_norm_w_2,
    sinks_2, w_out_2, norm_ffn_w_2, w_gate_2, w_up_2, conv_w_2, conv_b_2, w_down_2,
    final_norm_w_2,
):
    x = first_block(
        x, c, ctx, c_ctx, ada_w, ada_b, norm1_g, norm2_g, w_in, conv_a_w, rw_w0, rw_w_up, rw_a0,
        rw_a_up, rw_k_k, rw_k_a, rw_r_k, rw_g_up, rw_ln_g, rw_ln_b, w_out, ffn_w_up, ffn_conv_w,
        ffn_conv_b, ffn_w_down, final_g,
    )
    return second_block(
        x, norm_mix_w_2, w_in_2, b_attn_2, lb_logits_2, hg_norm_w_2, sinks_2, w_out_2,
        norm_ffn_w_2, w_gate_2, w_up_2, conv_w_2, conv_b_2, w_down_2, final_norm_w_2,
    )


_drawn_inputs = setup_inputs


def setup_inputs(seed=0):
    import zlib

    import numpy as np

    out = dict(_drawn_inputs(seed))
    spreads = {}
    factors = {'ctx': 3.706,
     'c_ctx': 8.0,
     'rw_w_up': 3.573,
     'rw_k_k': 8.0,
     'rw_k_a': 5.677,
     'rw_ln_g': 3.886,
     'rw_ln_b': 8.0,
     'ffn_conv_b': 8.0,
     'b_attn_2': 3.978,
     'hg_norm_w_2': 5.973,
     'sinks_2': 8.0,
     'norm_ffn_w_2': 3.902,
     'conv_b_2': 5.795,
     'final_norm_w_2': 2.865}
    for name, (base, spread) in spreads.items():
        noise = np.random.default_rng([zlib.crc32(name.encode()), seed]).standard_normal(out[name].shape)
        drawn = base * np.exp(spread * noise) if base else spread * noise
        out[name] = __import__('jax').numpy.asarray(drawn.astype(out[name].dtype))
    for name, factor in factors.items():
        out[name] = (out[name] * factor).astype(out[name].dtype)
    return out
```

```python
from contextlib import ExitStack

import numpy as np
import concourse.bass as bass
from concourse import mybir

F32 = mybir.dt.float32
U32 = mybir.dt.uint32
ALU = mybir.AluOpType
ACT = mybir.ActivationFunctionType
AX = mybir.AxisListType

P = 128
D = 1024
KB = D // P
TX = 512
TC = 256
TT = TC + TX
DFF = 2816
FB = DFF // P
HALF = FB // 2
GRID_W = 64
GRID_H = TX // GRID_W
DECAY = float(np.exp(-0.5))
EPS = 1e-6
GN_EPS = 64e-5
L = 64
NJ = 4
NCC, NCX = TC // L, TX // L
NC = NCC + NCX
LEVELS = 6
HC = 128
NH = 4
NB = TX // HC
NQ = 8
HLEV = 7

VEC = {}
_n = 0
for _name, _w in (("n1", KB), ("n2", KB), ("fin", KB), ("cs", 2 * KB), ("adab", 6 * KB), ("conva", 3 * 4),
                  ("wa0", 2 * 8), ("kk", 4), ("ka", 4), ("rk", 4), ("lng", 4), ("lnb", 4), ("fcw", FB * 10),
                  ("nmix", KB), ("nffn", KB), ("batt", 6), ("lb", 8), ("hgn", 1), ("sinks", NQ),
                  ("cw2", FB * 4), ("fin2", KB)):
    VEC[_name] = (_n, _w)
    _n += _w
NVEC = _n

CON = {}
_n = 0
for _name, _w in (("ident", P), ("ident2", L), ("ones", P), ("headones", P), ("level", 2 * LEVELS * L),
                  ("strict", 2 * L), ("incl", 2 * L), ("reset", 2 * NJ * L)):
    CON[_name] = (_n, _w)
    _n += _w
NCON = _n


def constants():
    c = np.zeros((P, NCON), np.float32)

    def put(name, a):
        o, w = CON[name]
        c[:, o:o + w] = a.reshape(P, w)

    put("ident", np.eye(P))
    put("ident2", np.tile(np.eye(L), (2, 1)))
    put("ones", np.ones((P, P)))
    put("headones", np.kron(np.eye(2), np.ones((L, L))))
    t, s = np.arange(L)[:, None], np.arange(L)[None, :]
    level = np.stack([(t >> l == s >> l) & (t >> (l - 1) & 1 == 1) & (s >> (l - 1) & 1 == 0)
                      for l in range(1, LEVELS + 1)])
    level = np.stack([level, level.transpose(0, 2, 1)])
    put("level", np.tile(level.transpose(2, 0, 1, 3), (2, 1, 1, 1)))
    put("strict", np.tile(np.stack([t < s, t > s]).transpose(1, 0, 2), (2, 1, 1)))
    put("incl", np.tile(np.stack([t <= s, t >= s]).transpose(1, 0, 2), (2, 1, 1)))
    reset = np.ones((2, NJ, L))
    reset[0, :, 0] = 0
    reset[1, :, -1] = 0
    put("reset", np.broadcast_to(reset, (P, 2, NJ, L)))
    return c


def level_masks():
    s, t = np.arange(HC)[:, None], np.arange(HC)[None, :]
    m = [(t >> l == s >> l) & (t >> (l - 1) & 1 == 1) & (s >> (l - 1) & 1 == 0) for l in range(1, HLEV + 1)]
    m.append(s == t)
    return np.ascontiguousarray(np.stack(m).transpose(1, 0, 2).astype(np.uint32))


def band_masks():
    q, k = np.arange(HC)[:, None], np.arange(2 * HC)[None, :]
    band = (q + HC - k >= 0) & (q + HC - k < HC)
    m = np.stack([band & (k >= HC), band, band, band])
    return np.ascontiguousarray(np.where(m, 0.0, -3e38).transpose(1, 0, 2).astype(np.float32))


RING = 2
STAGES = (("ADA1", 8, 1), ("W_IN", 8, 2), ("W_INB", 1, 3), ("W_INC", 4, 4), ("ADA2", 16, 1), ("W_OUT", 4, 2),
          ("UP1", FB, 2), ("DOWN1", 16, 1), ("W_IN2", 11, 2), ("W_OUT2", 4, 2), ("UP2", FB, 2), ("DOWN2", 16, 1))
SLOT, DONE = {}, []
_n = _g = 0
for _name, _slots, _per in STAGES:
    SLOT[_name] = _g
    for _ in range(_slots):
        _n += _per
        DONE.append(_n)
    _g += _slots


def in_pairs(eng, n, body, peel=False):
    first = 0
    if peel:
        body(0, 0)
        body(0, 1)
        first = 1
    with eng.Fori(first, n // 2) as i:
        body(i, 0)
        body(i, 1)
    if n % 2:
        body(n // 2, 0)


def two_blocks(nc, xT, ctxT, vec, con, hmask, band, w8, w11, lora, gup, outT):
    with ExitStack() as ctx:
        def sb(name, shape, dt=F32):
            return ctx.enter_context(nc.sbuf_tensor(name, shape, dt))

        s = {}

        def sem(*names):
            for name in names:
                s[name] = ctx.enter_context(nc.semaphore(name))

        banks = [ctx.enter_context(nc.psum_tensor(f"bank{b}", [P, 512], F32)) for b in range(8)]

        x = sb("x", [P, KB, TX])
        v = sb("v", [P, NVEC])
        k_ = sb("k_", [P, NCON])
        ring = sb("ring", [P, RING, 2 * KB * P])
        mod = sb("mod", [P, 6 * KB, 2])
        gains = sb("gains", [P, 3, KB])
        siluc = sb("siluc", [P, 2 * KB])
        rstd = sb("rstd", [P, TX])
        gain2 = sb("gain2", [P, KB])
        rstd_c = sb("rstd_c", [P, TC])
        NARENA = 41300
        arena = sb("arena", [P, NARENA])

        class Area:

            def __init__(self, at=0):
                self.at = at

            def take(self, *shape):
                n = int(np.prod(shape))
                a = arena[:, self.at:self.at + n]
                self.at += n
                assert self.at <= NARENA, self.at
                names = " ".join(f"d{i}" for i in range(len(shape)))
                return a.rearrange(f"p ({names}) -> p {names}",
                                   **{f"d{i}": n for i, n in enumerate(shape)}) if len(shape) > 1 else a

        def vcol(name, *shape):
            o, w = VEC[name]
            a = v[:, o:o + w]
            if not shape:
                return a
            names = " ".join(f"d{i}" for i in range(len(shape)))
            return a.rearrange(f"p ({names}) -> p {names}", **{f"d{i}": n for i, n in enumerate(shape)})

        def kcol(name, *shape):
            o, w = CON[name]
            a = k_[:, o:o + w]
            if not shape:
                return a
            names = " ".join(f"d{i}" for i in range(len(shape)))
            return a.rearrange(f"p ({names}) -> p {names}", **{f"d{i}": n for i, n in enumerate(shape)})

        def spread(a, *shape):
            return a.unsqueeze(len(a.shape)).broadcast_to([P, *shape])

        ident, ident2, ones, headones = kcol("ident"), kcol("ident2"), kcol("ones"), kcol("headones")
        level = kcol("level", 2, LEVELS, L)
        strict, incl = kcol("strict", 2, L), kcol("incl", 2, L)
        reset = kcol("reset", 2, NJ * L)

        A1 = Area()
        kv = A1.take(9, TT)
        px = A1.take(17, TX)
        kk = A1.take(4, TT)
        y_conv, rT, g_lo = px[:, 0:4], px[:, 12:16], px[:, 16]
        y_dir = [px[:, 4:8], px[:, 8:12]]
        kT, vT, lowT = kv[:, 0:4], kv[:, 4:8], kv[:, 8]
        staged = A1.at
        h = A1.take(KB, TX)
        hc = A1.take(KB, TC)
        ctx_sb = px[:, 0:4].rearrange("p a (b t) -> p (a b) t", b=2)
        kk_sq = Area(staged + 2048 + 512).take(NJ, TT)
        A2 = Area(staged)
        up = A2.take(2, 2, 4, P)
        gup_sb = A2.take(4 * P)

        class Scan:
            def __init__(self):
                self.gate = A2.take(2, NJ, L)
                self.cum = A2.take(NJ, L)
                self.pin = A2.take(NJ, L)
                self.kd = A2.take(NJ, L)
                self.kt, self.bh, self.rt = (A2.take(NJ, L) for _ in range(3))
                self.kt_bd, self.bh_bd, self.kh_bd, self.v_bd = (A2.take(NJ, P) for _ in range(4))
                self.n_bd, self.ak_bd = A2.take(NJ, P), A2.take(NJ, P)
                self.rm = A2.take(2, NJ, L)
                self.w, self.X = A2.take(NJ, L), A2.take(NJ, L)
                self.X_bd, self.XT_bd = A2.take(NJ, P), A2.take(NJ, P)
                self.b_tok, self.k_tok, self.v_tok = (A2.take(NJ, P) for _ in range(3))
                self.v2, self.u, self.S = (A2.take(NJ, L) for _ in range(3))
                self.S_bd = A2.take(NJ, P)
                self.g, self.u_bd = self.w, self.n_bd

        scans = [Scan(), Scan()]

        A3 = Area(staged + 6144)
        ys, yc, ysq, yr, rkr, bonus, y_rwkv = (A3.take(4, TX) for _ in range(7))

        act = Area(0).take(FB, TX)
        A4 = Area(staged + KB * TX)
        pad = [A4.take(GRID_H + 2, GRID_W + 2) for _ in range(2)]
        pad1 = [A4.take(TX + 2) for _ in range(2)]
        conv = [A4.take(TX) for _ in range(2)]
        silu = [A4.take(TX) for _ in range(2)]

        A5 = Area(0)
        pr = A5.take(16, TX)
        aq = A5.take(4, TX)
        kz = [A5.take(HC + TX) for _ in range(2)]
        vp = A5.take(HC + TX)
        hreset, cumf = A5.take(NB, NH, HC), A5.take(NB, NH, HC)
        assert A5.at <= staged
        kh, qh = A5.take(NB, NH, HC), A5.take(NB, NH, HC)
        assert A5.at <= staged + KB * TX
        A6 = Area(staged + KB * TX)
        hmask_sb = A6.take(HLEV + 1, HC).bitcast(U32)
        band_sb = A6.take(NB, 2 * HC)
        v_ch, k_ch, sT, S2, qe, ec, ke, k_tok2, v_tok2 = (A6.take(NH, HC) for _ in range(9))
        de = [A6.take(NH * HC) for _ in range(2)]
        zz = [A6.take(NH * HC) for _ in range(2)]
        q_ch = A6.take(NH, HC)
        v_st = A6.take(2, HC)
        vz = A6.take(2, 2, HC)
        pp = A6.take(NQ, 2 * HC)
        pT = A6.take(2 * NQ, HC)
        mix = A6.take(KB, TX)
        lbv, oml = A6.take(4), A6.take(4)
        hi, nm, dsk, den, esk = (A6.take(NQ) for _ in range(5))
        sq2 = Area(0).take(4, TX)
        yr2 = pr[:, 4:8]

        sem("x_in", "ctx_in", "vec_in", "con_in", "lora_in", "slot_in0", "slot_in1")
        sem("product", "taken")
        sem("silu_c", "mod", "squares", "square_sum", "mean_sq", "root", "gain", "normed")
        sem("head_sq", "head_sum", "head_rec", "head_root", "kk_ready", "low_tanh", "conv_ready", "bd_clean")
        sem("y_rkr", "y_rkr_mm", "centred_bonus", "g_sig", "gate_mm", "mixed")
        per_scan = ("z_mm", "z_biased", "z_tanh", "decays", "exps", "keys", "bds", "rt", "m_mm", "m2_mm", "m_out",
                    "ak_bd", "rm", "tok_mm", "tok", "X", "X_bd", "XT_mm", "XT_bd", "level_mm", "w", "gu_mm", "gu",
                    "u_bd", "y_out", "ds_mm", "S", "S_bd")
        for d in range(2):
            sem(*(f"{n}{d}" for n in per_scan))
        sem("pads_clean", "gate_in", "conv", "silu", "val_free")
        sem("masks_in", "lb", "forget", "sig", "q_hg", "cum_f", "cum_scan", "f", "keys_hg", "g_silu", "pads2", "S_clean")
        sem("h_in", "h_d", "h_e", "h_z", "h_mm", "h_s", "h_ec", "h_qe", "h_ke", "h_ke_e", "h_kend", "h_v_mm",
            "h_v", "h_k_mm", "h_k", "h_o_mm", "h_o", "h_ds", "h_S")
        sem("a_in", "a_s_mm", "a_nm", "a_ds", "a_p", "a_es", "a_pn", "a_v_mm", "a_v", "a_t_mm", "a_t",
            "a_o_mm", "a_o")
        sem("mix2", "out")
        sem("dve_step", "act_step", "pool_step")

        class Steps:

            def __init__(self, eng, name):
                self.eng, self.sem, self.n, self.per, self.i = eng, s[name], 0, 0, 0

            def do(self, ins):
                ins.then_inc(self.sem, 1)
                self.n += 1

            def last(self):
                self.eng.wait_ge(self.sem, self.n + self.per * self.i)

            def loop(self, i, per):
                self.i, self.per, self.at = i, per, self.n

            def end(self, turns):
                assert self.n - self.at == self.per, (self.n - self.at, self.per)
                self.n = self.at + self.per * turns
                self.per = self.i = 0

        def slot_view(g, blocks=2 * KB):
            return ring[:, g % 2, 0:blocks * P].rearrange("p (k m) -> p k m", m=P)

        def slot_ready(pe, g, i):
            pe.wait_ge(s[f"slot_in{g % 2}"], 16 * (g // 2) + 16 + 16 * i)

        def chunk_at(d, n, isx):
            if d == 0:
                return (TC if isx else 0) + L * n
            return n * -L + (TT - L if isx else TC - L)

        def places(eng, i, isx):
            at = [chunk_at(d, i, isx) for d in range(2)]
            return at if isinstance(i, int) else [eng.snap(a) for a in at]

        TAKEN_IN = 35
        block = ctx.enter_context(nc.Block())

        @block.sync
        def _(sp):
            def load(g, i, src, at, used):
                if used is not None:
                    sp.wait_ge(s["product"], used)
                if src is w8:
                    to = ring[:, g % 2, :].rearrange("p (c n) -> p c n", c=2)
                    ap = w8[bass.ds(2 * at + 4 * i, 2)].rearrange("c p n -> p c n")
                else:
                    to = ring[:, g % 2, 0:HALF * P]
                    ap = w11[bass.ds(at + 2 * i, 1)].rearrange("c p n -> p (c n)")
                sp.dma_start(to, ap).then_inc(s[f"slot_in{g % 2}"], 16)

            def load_stage(name, src, at, skip=0):
                g = SLOT[name]
                _, n, per = next(st for st in STAGES if st[0] == name)
                for u in range(skip, min(2, n)):
                    load(g + u, 0, src, at + u, DONE[g + u - 2] if g + u >= 2 else None)
                if n > 3:
                    with sp.Fori(1, n // 2) as i:
                        for u in range(2):
                            load(g + u, i, src, at + u, DONE[g + u] - 2 * per + 2 * per * i)
                if n > 2 and n % 2:
                    load(g, n // 2, src, at, DONE[g + n - 3])

            sp.dma_start(v[:, :], vec).then_inc(s["vec_in"], 16)
            load(0, 0, w8, 0, None)
            load(1, 0, w8, 1, None)
            sp.dma_start(k_[:, :], con).then_inc(s["con_in"], 16)
            sp.dma_start(x[:, :, :], xT).then_inc(s["x_in"], 16)
            sp.dma_start(ctx_sb, ctxT).then_inc(s["ctx_in"], 16)
            load_stage("ADA1", w8, 0, skip=2)
            load_stage("W_IN", w8, 8)
            load_stage("W_INB", w8, 16)
            load_stage("W_INC", w8, 17)
            sp.wait_ge(s["product"], DONE[SLOT["ADA2"] - 1])
            sp.dma_start(up.rearrange("p a b c d -> p (a b c d)"), lora).then_inc(s["lora_in"], 16)
            sp.dma_start(gup_sb, gup).then_inc(s["lora_in"], 16)
            load_stage("ADA2", w8, 21)
            load_stage("W_OUT", w8, 37)
            load_stage("UP1", w8, 41)
            load_stage("DOWN1", w11, 0)
            sp.wait_ge(s["normed"], 5 * KB)
            sp.dma_start(hmask_sb, hmask).then_inc(s["masks_in"], 16)
            sp.dma_start(band_sb, band).then_inc(s["masks_in"], 16)
            load_stage("W_IN2", w8, 63)
            load_stage("W_OUT2", w8, 74)
            load_stage("UP2", w8, 78)
            load_stage("DOWN2", w11, 16)
            for k in range(0, KB, 2):
                sp.wait_ge(s["normed"], 6 * KB + k + 2)
                sp.dma_start(outT[:, k:k + 2], x[:, k:k + 2, :]).then_inc(s["out"], 16)
            sp.wait_ge(s["out"], 16 * KB // 2)

        @block.tensor
        def _(pe):
            mm = nc.tensor.matmul

            def ada(name, bank, col):
                g = SLOT[name]

                def body(i, u):
                    slot_ready(pe, g + u, i)
                    w = slot_view(g + u)
                    for c in range(2):
                        o = bank[:, bass.ds(col + 2 * (2 * u + c) + 8 * i, 2)]
                        for k in range(KB):
                            last = mm(o, w[:, c * KB + k, :], siluc[:, 2 * k:2 * k + 2], start=k == 0,
                                      stop=k == KB - 1)
                    last.then_inc(s["product"], 1)
                return body

            pe.wait_ge(s["silu_c"], 1)
            in_pairs(pe, 8, ada("ADA1", banks[7], 0))

            norms = [0]

            def sum_squares(sq, bank, t):
                for k in range(KB):
                    pe.wait_ge(s["squares"], norms[0] * KB + k + 1)
                    last = mm(bank[:, 0:t], ones, sq[:, k, :], start=k == 0, stop=k == KB - 1)
                last.then_inc(s["square_sum"], 1)
                norms[0] += 1

            def stage(name, prods, taken, free=None):
                g = SLOT[name]
                n = next(st[1] for st in STAGES if st[0] == name)
                q = len(prods)

                def body(i, u):
                    slot_ready(pe, g + u, i)
                    w = slot_view(g + u)
                    for c, (blk, src, t) in enumerate(prods):
                        if not (isinstance(i, int) and i == 0):
                            if free:
                                pe.wait_ge(s[free[c]], 2 * i + taken + u - 1)
                            else:
                                pe.wait_ge(s["taken"], 2 * q * i + taken + q * u + c + 1 - 2 * q)
                        bank = banks[q * u + c]
                        for k in range(KB):
                            last = mm(bank[:, 0:t], w[:, blk * KB + k, :], src(k), start=k == 0, stop=k == KB - 1)
                        last.then_inc(s["product"], 1)

                if n == 1:
                    body(0, 0)
                else:
                    in_pairs(pe, n, body, peel=True)

            def blocks(a):
                return lambda k: a[:, k, :]

            def down(name, taken):
                g = SLOT[name]
                with pe.Fori(0, KB // 2) as i:
                    for m in range(2):
                        pe.wait_ge(s["taken"], taken + 2 * i + m - 1)
                        for half in range(2):
                            slot_ready(pe, g + 2 * m + half, 2 * i)
                            w = slot_view(g + half, HALF)
                            for k in range(HALF):
                                last = mm(banks[m][:, :], w[:, k, :], act[:, HALF * half + k, :],
                                          start=half == 0 and k == 0, stop=half == 1 and k == HALF - 1)
                            last.then_inc(s["product"], 1)

            pe.wait_ge(s["con_in"], 16)
            sum_squares(hc, banks[0], TC)
            sum_squares(h, banks[1], TX)
            pe.wait_ge(s["normed"], 2 * KB)
            hb, hcb = blocks(h), blocks(hc)
            stage("W_IN", [(0, hb, TX), (1, hb, TX)], 0)
            pe.wait_ge(s["taken"], 16)
            stage("W_INB", [(0, hb, TX), (1, hb, TX), (1, hcb, TC)], 16)
            pe.wait_ge(s["taken"], 19)
            stage("W_INC", [(0, hb, TX), (0, hcb, TC), (1, hb, TX), (1, hcb, TC)], 19)

            pe.wait_ge(s["taken"], TAKEN_IN)
            for j in range(NJ):
                pe.wait_ge(s["head_sq"], j + 1)
                mm(banks[2 * j][:, 0:TX], headones, kk_sq[:, j, TC:TT], start=True, stop=True)
                mm(banks[2 * j + 1][:, 0:TC], headones, kk_sq[:, j, 0:TC], start=True,
                   stop=True).then_inc(s["head_sum"], 1)

            ada_g = SLOT["ADA2"]

            def chunk(i, isx):
                n = i + (NCC if isx else 0)
                bank = [banks[0:4], banks[4:8]]

                def done(name, d, per=1, at=0):
                    pe.wait_ge(s[f"{name}{d}"], per * n + (at or per))

                def pairs(d, out, lhs, rhs, name=None, start=True, stop=True):
                    for j in range(NJ):
                        last = mm(out[:, j, :], lhs[:, j, :], rhs if len(rhs.shape) == 2 else rhs[:, j, :],
                                  start=start, stop=stop)
                    if name:
                        last.then_inc(s[f"{name}{d}"], 1)

                def half(b, k):
                    return b[:, 256 * k:256 * k + 256].rearrange("p (j t) -> p j t", j=NJ)

                def whole(b):
                    return b[:, :].rearrange("p (j t) -> p j t", j=NJ)

                ats = places(pe, i, isx)
                for d, sc in enumerate(scans):
                    b0, b1, b2, b3 = bank[d]
                    at = ats[d]
                    if not (isinstance(i, int) and i == 0 and not isx):
                        pe.wait_ge(s[f"XT_bd{d}"], LEVELS * n)
                    z = b0[:, :].rearrange("p (q t) -> p q t", q=8)
                    for q in range(8):
                        last = mm(z[:, q, :], up[:, d, q // 4, q % 4, :], lowT[:, bass.ds(at, L)], start=True,
                                  stop=True)
                    last.then_inc(s[f"z_mm{d}"], 1)
                for d, sc in enumerate(scans):
                    b0, b1, b2, b3 = bank[d]
                    done("bds", d, 3, 2)
                    done("keys", d, 4, 2)
                    if not (isinstance(i, int) and i == 0 and not isx):
                        pe.wait_ge(s[f"X{d}"], LEVELS * n)
                    pairs(d, half(b3, 0), sc.kt_bd, sc.bh)
                    done("keys", d, 4)
                    pairs(d, half(b3, 1), sc.kh_bd, sc.kt, "m_mm")
                    done("bds", d, 3)
                    pairs(d, half(b1, 0), sc.bh_bd, sc.kt, "m_mm")
                    done("bds", d, 3, 1)
                    done("z_biased", d)
                    pairs(d, half(b0, 0), sc.v_bd, ident2, "m_mm")
                    if not (isinstance(i, int) and i == 0 and not isx):
                        pe.wait_ge(s[f"S{d}"], n)
                        pe.wait_ge(s["mod"], 1 + (NCC if isx else i))
                    if isx:
                        pe.wait_ge(s[f"rt{d}"], i + 1)
                        pairs(d, half(b2, 0), sc.bh_bd, sc.rt)
                        pairs(d, half(b2, 1), sc.kh_bd, sc.rt, "m2_mm")

                def turn(d, k):
                    sc = scans[d]
                    src = (sc.bh_bd, sc.kh_bd, sc.v_bd)[k]
                    if k == 0:
                        if isx:
                            pe.wait_ge(s[f"rm{d}"], i + 1)
                    else:
                        pe.wait_ge(s[f"tok{d}"], 3 * n + k)
                    for j in range(NJ):
                        last = nc.tensor.transpose(whole(bank[d][2])[:, j, :], src[:, j, :], ident)
                    last.then_inc(s[f"tok_mm{d}"], 1)

                for l in range(1, LEVELS + 1):
                    for d, sc in enumerate(scans):
                        b3 = bank[d][3]
                        if l > 1:
                            pe.wait_ge(s[f"X{d}"], LEVELS * n + l - 1)
                            if l == 2:
                                done("m_out", d, 3, 2)
                                done("ak_bd", d, 2)
                            pairs(d, half(b3, 0), sc.n_bd, sc.X, "level_mm")
                    if l <= 3:
                        for d in range(2):
                            turn(d, l - 1)
                    for d, sc in enumerate(scans):
                        b3 = bank[d][3]
                        if l > 1:
                            pe.wait_ge(s[f"w{d}"], (LEVELS - 1) * n + l - 1)
                            pe.wait_ge(s[f"XT_bd{d}"], LEVELS * n + l - 1)
                            pairs(d, half(b3, 1), sc.XT_bd, sc.w, "level_mm")
                    for d, sc in enumerate(scans):
                        if l == 1:
                            done("m_out", d, 3)
                        pe.wait_ge(s[f"X_bd{d}"], LEVELS * n + l)
                        for j in range(NJ):
                            last = nc.tensor.transpose(whole(bank[d][0])[:, j, :], sc.X_bd[:, j, :], ident)
                        last.then_inc(s[f"XT_mm{d}"], 1)

                for d, sc in enumerate(scans):
                    b1, b2 = bank[d][1], bank[d][2]
                    if not (isinstance(i, int) and i == 0 and not isx):
                        pe.wait_ge(s[f"S_bd{d}"], n)
                    g = half(b1, 0)
                    for j in range(NJ):
                        mm(g[:, j, :], sc.kt_bd[:, j, :], sc.S[:, j, :], start=True, stop=False)
                        last = mm(g[:, j, :], sc.ak_bd[:, j, :], sc.v2[:, j, :], start=False, stop=True)
                    last.then_inc(s[f"gu_mm{d}"], 1)
                for d, sc in enumerate(scans):
                    done("XT_bd", d, LEVELS)
                    done("gu", d, 2, 1)
                    pairs(d, half(bank[d][1], 1), sc.XT_bd, sc.g, "gu_mm")
                for d, sc in enumerate(scans):
                    b2 = bank[d][2]
                    pe.wait_ge(s[f"tok{d}"], 3 * n + 3)
                    if isx:
                        y = half(b2, 0)
                        pe.wait_ge(s[f"u_bd{d}"], 2 * i + 2)
                        for j in range(NJ):
                            mm(y[:, j, :], sc.S_bd[:, j, :], sc.rt[:, j, :], start=True, stop=False)
                            mm(y[:, j, :], sc.u_bd[:, j, :], sc.rm[:, 0, j, :], start=False, stop=False)
                            mm(y[:, j, :], sc.v_tok[:, j, :], sc.rm[:, 1, j, :], start=False, stop=True)
                    done("gu", d, 2)
                    ds = half(b2, 1)
                    for j in range(NJ):
                        mm(ds[:, j, :], sc.b_tok[:, j, :], sc.u[:, j, :], start=True, stop=False)
                        last = mm(ds[:, j, :], sc.k_tok[:, j, :], sc.v2[:, j, :], start=False, stop=True)
                    last.then_inc(s[f"ds_mm{d}"], 1)
                if not isx:
                    pe.wait_ge(s["S0"], n + 1)
                    for u in range(4):
                        slot_ready(pe, ada_g + u, 2 * i)
                        w = slot_view(ada_g + u)
                        for c in range(2):
                            o = bank[0][2][:, 2 * (2 * u + c):2 * (2 * u + c) + 2]
                            for k in range(KB):
                                last = mm(o, w[:, c * KB + k, :], siluc[:, 2 * k:2 * k + 2], start=k == 0,
                                          stop=k == KB - 1)
                        last.then_inc(s["product"], 1)

            pe.wait_ge(s["kk_ready"], NJ)
            pe.wait_ge(s["lora_in"], 32)
            pe.wait_ge(s["low_tanh"], 1)
            pe.wait_ge(s["bd_clean"], 10)
            chunk(0, False)
            with pe.Fori(1, NCC) as i:
                chunk(i, False)
            with pe.Fori(0, NCX) as i:
                chunk(i, True)

            for j in range(NJ):
                pe.wait_ge(s["y_rkr"], 2 * j + 1)
                mm(banks[j][:, :], headones, ys[:, j, :], start=True, stop=True).then_inc(s["y_rkr_mm"], 1)
                pe.wait_ge(s["y_rkr"], 2 * j + 2)
                mm(banks[4 + j][:, :], headones, rkr[:, j, :], start=True, stop=True).then_inc(s["y_rkr_mm"], 1)
            for j in range(NJ):
                pe.wait_ge(s["head_sq"], NJ + j + 1)
                mm(banks[j][:, :], headones, ysq[:, j, :], start=True, stop=True).then_inc(s["head_sum"], 1)
            pe.wait_ge(s["g_sig"], 1)
            for j in range(NJ):
                pe.wait_ge(s["centred_bonus"], 2 * j + 2)
                mm(banks[4 + j][:, :], gup_sb[:, j * P:(j + 1) * P], g_lo, start=True,
                   stop=True).then_inc(s["gate_mm"], 1)
            pe.wait_ge(s["mixed"], NJ)
            stage("W_OUT", [(c, lambda k: y_conv[:, k, :] if k < 4 else y_rwkv[:, k - 4, :], TX) for c in range(2)],
                  35)
            sum_squares(h, banks[6], TX)
            pe.wait_ge(s["normed"], 3 * KB)
            stage("UP1", [(0, hb, TX), (1, hb, TX)], 0, free=("gate_in", "val_free"))
            pe.wait_ge(s["val_free"], FB)
            down("DOWN1", 43)
            sum_squares(h, banks[6], TX)

            sum_squares(h, banks[7], TX)
            pe.wait_ge(s["normed"], 5 * KB)
            stage("W_IN2", [(0, hb, TX), (1, hb, TX)], 51)
            pe.wait_ge(s["taken"], 51 + 22)

            def mixer2(i):
                first = isinstance(i, int) and i == 0

                def heads(b):
                    return b[:, :].rearrange("p (h t) -> p h t", h=NH)

                pe.wait_ge(s["a_in"], 2 * i + 1)
                if not first:
                    pe.wait_ge(s["a_o"], i)
                for j in range(4):
                    for g in range(2):
                        last = mm(banks[4 + j][:, 256 * g:256 * g + 256], q_ch[:, j, :],
                                  kz[g][:, bass.ds(HC * i, 2 * HC)], start=True, stop=True)
                last.then_inc(s["a_s_mm"], 1)
                pe.wait_ge(s["h_in"], 2 * i + 2)
                if not first:
                    pe.wait_ge(s["h_k"], i)
                for hd in range(NH):
                    last = nc.tensor.transpose(heads(banks[2])[:, hd, :], v_ch[:, hd, :], ident)
                last.then_inc(s["h_v_mm"], 1)
                for l in range(1, HLEV + 2):
                    b = banks[l % 2]
                    if not first or l > 2:
                        pe.wait_ge(s["h_s"], 8 * i + l - 2)
                    if l <= HLEV:
                        pe.wait_ge(s["h_z"], 2 * HLEV * i + 2 * l)
                    for hd in range(NH):
                        zl = zz[l % 2].rearrange("p (h t) -> p h t", h=NH)
                        if l <= HLEV:
                            last = mm(heads(b)[:, hd, :], zl[:, hd, :], zl[:, hd, :], start=True, stop=True)
                        else:
                            last = mm(heads(b)[:, hd, :], k_ch[:, hd, :], q2d(i, hd), start=True, stop=True)
                    last.then_inc(s["h_mm"], 1)
                pe.wait_ge(s["h_kend"], i + 1)
                pe.wait_ge(s["h_v"], i + 1)
                for hd in range(NH):
                    last = nc.tensor.transpose(heads(banks[2])[:, hd, :], ke[:, hd, :], ident)
                last.then_inc(s["h_k_mm"], 1)
                pe.wait_ge(s["h_s"], 8 * i + 8)
                pe.wait_ge(s["h_qe"], i + 1)
                if not first:
                    pe.wait_ge(s["h_S"], i)
                for hd in range(NH):
                    mm(heads(banks[3])[:, hd, :], v_tok2[:, hd, :], sT[:, hd, :], start=True, stop=False)
                    last = mm(heads(banks[3])[:, hd, :], S2[:, hd, :], qe[:, hd, :], start=False, stop=True)
                last.then_inc(s["h_o_mm"], 1)
                pe.wait_ge(s["a_pn"], i + 1)
                for b in range(4):
                    for c in range(4):
                        last = nc.tensor.transpose(heads(banks[4 + b])[:, c, :],
                                                   pp[:, 2 * b + c // 2, HC * (c % 2):HC * (c % 2) + HC], ident)
                    last.then_inc(s["a_t_mm"], 1)
                pe.wait_ge(s["h_k"], i + 1)
                pe.wait_ge(s["h_o"], i + 1)
                for hd in range(NH):
                    last = mm(heads(banks[3])[:, hd, :], k_tok2[:, hd, :], v_tok2[:, hd, :], start=True, stop=True)
                last.then_inc(s["h_ds"], 1)
                pe.wait_ge(s["a_in"], 2 * i + 2)
                pe.wait_ge(s["a_t"], 4 * i + 4)
                for c in range(2):
                    last = nc.tensor.transpose(banks[4][:, HC * c:HC * c + HC], v_st[:, c, :], ident)
                last.then_inc(s["a_v_mm"], 1)
                pe.wait_ge(s["a_v"], 2 * i + 2)
                for j in range(4):
                    for n, (g, c) in enumerate(((0, 0), (0, 1), (1, 0), (1, 1))):
                        last = mm(heads(banks[5])[:, j, :], vz[:, g, c, :], pT[:, 4 * j + 2 * g + c, :],
                                  start=n == 0, stop=n == 3)
                last.then_inc(s["a_o_mm"], 1)

            def q2d(i, hd):
                return qh.rearrange("p n h t -> p (n h t)")[:, bass.ds(NH * HC * i + HC * hd, HC)]

            pe.wait_ge(s["q_hg"], NH)
            pe.wait_ge(s["S_clean"], 1)
            pe.wait_ge(s["pads2"], 4)
            mixer2(0)
            with pe.Fori(1, NB) as i:
                mixer2(i)
            pe.wait_ge(s["h_S"], NB)
            for hd in range(NH):
                pe.wait_ge(s["head_sq"], 2 * NJ + hd + 1)
                mm(banks[hd][:, :], ones, sq2[:, hd, :], start=True, stop=True).then_inc(s["head_sum"], 1)
            pe.wait_ge(s["mix2"], NH)
            pe.wait_ge(s["a_o"], NB)
            stage("W_OUT2", [(c, blocks(mix), TX) for c in range(2)], 73)
            sum_squares(h, banks[6], TX)

            pe.wait_ge(s["normed"], 6 * KB)
            stage("UP2", [(0, hb, TX), (1, hb, TX)], FB, free=("gate_in", "val_free"))
            pe.wait_ge(s["val_free"], 2 * FB)
            down("DOWN2", 81)
            sum_squares(h, banks[6], TX)

        @block.scalar
        def _(se):
            act_f = nc.scalar.activation
            steps = Steps(se, "act_step")
            se.wait_ge(s["vec_in"], 16)
            act_f(siluc[:, :], vcol("cs"), ACT.Silu).then_inc(s["silu_c"], 1)

            def squares(src, to, after=None):
                for k in range(KB):
                    if after:
                        se.wait_ge(s[after[0]], after[1] + k + 1)
                    act_f(to[:, k, :], src[:, k, :], ACT.Square).then_inc(s["squares"], 1)

            roots = [0]

            def root(r):
                roots[0] += 1
                se.wait_ge(s["mean_sq"], roots[0])
                act_f(r, r, ACT.Sqrt).then_inc(s["root"], 1)

            se.wait_ge(s["ctx_in"], 16)
            squares(ctx_sb, hc)
            se.wait_ge(s["x_in"], 16)
            squares(x, h)
            root(rstd_c[:, :])
            root(rstd[:, :])

            def take(to, bank, product, **kw):
                se.wait_ge(s["product"], product)
                act_f(to, bank, ACT.Copy, **kw).then_inc(s["taken"], 1)

            p_in = DONE[SLOT["W_IN"] - 1]

            def take_x(i, u):
                for c in range(2):
                    m = 4 * i + 2 * u + c
                    take(px[:, m, :] if isinstance(i, int) else px[:, bass.ds(m, 1), :], banks[2 * u + c][:, :],
                         p_in + 4 * i + 2 * u + c + 1)

            in_pairs(se, 8, take_x)
            take(px[:, 16, :], banks[0][:, :], p_in + 17)
            take(kv[:, 0, TC:TT], banks[1][:, :], p_in + 18)
            take(kv[:, 0, 0:TC], banks[2][:, 0:TC], p_in + 19)

            def take_xc(i, u):
                for c in range(4):
                    m = 1 + 4 * i + 2 * u + c // 2
                    to = kv[:, bass.ds(m, 1), TC:TT] if c % 2 == 0 else kv[:, bass.ds(m, 1), 0:TC]
                    take(to, banks[4 * u + c][:, 0:TX if c % 2 == 0 else TC], p_in + 20 + 8 * i + 4 * u + c)

            in_pairs(se, 4, take_xc)

            se.wait_ge(s["taken"], TAKEN_IN)
            for j in range(NJ):
                act_f(kk_sq[:, j, :], kT[:, j, :], ACT.Square, scale=vcol("kk")[:, j:j + 1]).then_inc(s["head_sq"], 1)
            act_f(lowT[0:64, :], lowT[0:64, :], ACT.Tanh).then_inc(s["low_tanh"], 1)
            for j in range(NJ):
                se.wait_ge(s["head_rec"], j + 1)
                act_f(kk[:, j, :], kk[:, j, :], ACT.Sqrt).then_inc(s["head_root"], 1)

            def chunk(i, isx):
                n = i + (NCC if isx else 0)
                bank = [banks[0:4], banks[4:8]]

                def done(name, d, per=1, at=0):
                    se.wait_ge(s[f"{name}{d}"], per * n + (at or per))

                def half(b, k):
                    return b[:, 256 * k:256 * k + 256].rearrange("p (j t) -> p j t", j=NJ)

                def diagonal(to, src, name, scale=1.0):
                    for q in range(2):
                        r = slice(64 * q, 64 * q + 64)
                        act_f(to[r, :, r], src[r, :, :], ACT.Copy, scale=scale).then_inc(s[name], 1)

                for d, sc in enumerate(scans):
                    done("z_biased", d)
                    act_f(sc.gate, sc.gate, ACT.Tanh, scale=0.5).then_inc(s[f"z_tanh{d}"], 1)
                for d, sc in enumerate(scans):
                    done("decays", d)
                    act_f(sc.gate[:, 0], sc.gate[:, 0], ACT.Exp).then_inc(s[f"exps{d}"], 1)
                    act_f(sc.pin, sc.cum, ACT.Exp).then_inc(s[f"exps{d}"], 1)
                    done("exps", d, 3, 2)
                    act_f(sc.cum, sc.cum, ACT.Exp, scale=-1.0).then_inc(s[f"exps{d}"], 1)
                for d, sc in enumerate(scans):
                    done("m_mm", d, 3, 2)
                    diagonal(sc.n_bd, half(bank[d][1], 0), f"m_out{d}", -1.0)
                    done("m_mm", d, 3)
                    act_f(sc.v2, half(bank[d][0], 0), ACT.Copy).then_inc(s[f"m_out{d}"], 1)
                for l in range(1, LEVELS + 1):
                    for d, sc in enumerate(scans):
                        whole = bank[d][2][:, :].rearrange("p (j t) -> p j t", j=NJ)
                        if l <= 3:
                            done("tok_mm", d, 3, l)
                            act_f((sc.b_tok, sc.k_tok, sc.v_tok)[l - 1], whole, ACT.Copy).then_inc(s[f"tok{d}"], 1)
                    for d, sc in enumerate(scans):
                        done("XT_mm", d, LEVELS, l)
                        act_f(sc.XT_bd, bank[d][0][:, :].rearrange("p (j t) -> p j t", j=NJ),
                              ACT.Copy).then_inc(s[f"XT_bd{d}"], 1)
                for d, sc in enumerate(scans):
                    done("gu_mm", d, 2, 1)
                    act_f(sc.g, half(bank[d][1], 0), ACT.Copy, scale=-1.0).then_inc(s[f"gu{d}"], 1)
                for d, sc in enumerate(scans):
                    done("gu_mm", d, 2)
                    act_f(sc.u, half(bank[d][1], 1), ACT.Copy).then_inc(s[f"gu{d}"], 1)
                    if isx:
                        diagonal(sc.u_bd, half(bank[d][1], 1), f"u_bd{d}")

            se.wait_ge(s["bd_clean"], 10)
            chunk(0, False)
            with se.Fori(1, NCC) as i:
                chunk(i, False)
            with se.Fori(0, NCX) as i:
                chunk(i, True)

            for d in range(2):
                se.wait_ge(s[f"S_bd{d}"], NC)
            act_f(g_lo, g_lo, ACT.Sigmoid).then_inc(s["g_sig"], 1)
            for j in range(NJ):
                se.wait_ge(s["centred_bonus"], 2 * j + 1)
                act_f(ysq[:, j, :], yc[:, j, :], ACT.Square).then_inc(s["head_sq"], 1)
            for j in range(NJ):
                se.wait_ge(s["head_rec"], NJ + j + 1)
                act_f(yr[:, j, :], yr[:, j, :], ACT.Sqrt).then_inc(s["head_root"], 1)
            squares(x, h, ("taken", 35))
            root(rstd[:, :])

            def ffn(first, p0, name):
                def body(i, u):
                    if not (isinstance(i, int) and i == 0 and first == 0):
                        se.wait_ge(s["conv"], first + 2 * i + u - 1)
                    se.wait_ge(s["product"], p0 + 4 * i + 2 * u + 1)
                    if name == 1:
                        act_f(pad[u][:, 1:1 + GRID_H, 1:1 + GRID_W],
                              banks[2 * u][:, :].rearrange("p (y x) -> p y x", y=GRID_H),
                              ACT.Copy).then_inc(s["gate_in"], 1)
                    else:
                        act_f(pad1[u][:, 2:2 + TX], banks[2 * u][:, :], ACT.Copy).then_inc(s["gate_in"], 1)
                    se.wait_ge(s["conv"], first + 2 * i + u + 1)
                    if not (isinstance(i, int) and i == 0):
                        se.wait_ge(s["val_free"], first + 2 * i + u - 1)
                    act_f(silu[u], conv[u], ACT.Silu).then_inc(s["silu"], 1)

                se.wait_ge(s["pads_clean"], 2 * name)
                in_pairs(se, FB, body, peel=True)

            ffn(0, DONE[SLOT["UP1"] - 1], 1)
            squares(x, h, ("taken", 43))
            root(rstd[:, :])

            squares(x, h, ("normed", 3 * KB))
            root(rstd[:, :])
            se.wait_ge(s["lb"], 1)
            act_f(lbv, lbv, ACT.Sigmoid).then_inc(s["sig"], 1)
            p_in2 = DONE[SLOT["W_IN2"] - 1]

            def take2(i, u):
                for c in range(2):
                    m = 4 * i + 2 * u + c
                    take(pr[:, m, :] if isinstance(i, int) else pr[:, bass.ds(m, 1), :], banks[2 * u + c][:, :],
                         p_in2 + 4 * i + 2 * u + c + 1)

            in_pairs(se, 8, take2)
            bias = vcol("batt")
            for j in range(4):
                se.wait_ge(s["product"], p_in2 + 17 + j)
                act_f(aq[:, j, :], banks[j][:, :], ACT.Identity, bias=bias[:, j:j + 1]).then_inc(s["taken"], 1)
            se.wait_ge(s["pads2"], 4)
            se.wait_ge(s["product"], p_in2 + 21)
            act_f(kz[0][0:64, HC:], banks[0][0:64, :], ACT.Identity, bias=bias[0:64, 4:5]).then_inc(s["act_step"], 1)
            act_f(kz[1][64:128, HC:], banks[0][64:128, :], ACT.Identity,
                  bias=bias[64:128, 4:5]).then_inc(s["taken"], 1)
            se.wait_ge(s["product"], p_in2 + 22)
            act_f(vp[:, HC:], banks[1][:, :], ACT.Identity, bias=bias[:, 5:6]).then_inc(s["taken"], 1)
            for hd in range(NH):
                act_f(pr[:, 4 + hd, :], pr[:, 4 + hd, :], ACT.Sigmoid).then_inc(s["forget"], 1)
            for hd in range(NH):
                act_f(pr[:, 12 + hd, :], pr[:, 12 + hd, :], ACT.Silu).then_inc(s["g_silu"], 1)
            for hd in range(NH):
                se.wait_ge(s["keys_hg"], hd + 1)
                act_f(cumf[:, :, hd, :], cumf[:, :, hd, :], ACT.Ln).then_inc(s["cum_f"], 1)

            def mixer2(i):
                first = isinstance(i, int) and i == 0
                chunk = bass.ds(NH * HC * i, NH * HC)
                cf = cumf.rearrange("p n h t -> p (n h t)")[:, chunk]

                def heads(b):
                    return b[:, :].rearrange("p (h t) -> p h t", h=NH)

                if not first:
                    se.wait_ge(s["h_S"], i)
                act_f(ec.rearrange("p h t -> p (h t)"), cf, ACT.Exp).then_inc(s["h_ec"], 1)
                se.wait_ge(s["h_v_mm"], i + 1)
                act_f(v_tok2, heads(banks[2]), ACT.Copy).then_inc(s["h_v"], 1)

                def level(l):
                    se.wait_ge(s["h_d"], 2 * HLEV * i + 2 * l)
                    act_f(de[l % 2], de[l % 2], ACT.Exp).then_inc(s["h_e"], 1)

                level(1)
                level(2)
                se.wait_ge(s["a_ds"], i + 1)
                for q in range(NQ):
                    act_f(pp[:, q, :], pp[:, q, :], ACT.Exp, bias=nm[:, q:q + 1],
                          accum_out=den[:, q:q + 1]).then_inc(s["a_p"], 1)
                act_f(esk, dsk, ACT.Exp).then_inc(s["a_es"], 1)
                for l in range(3, HLEV + 1):
                    level(l)
                se.wait_ge(s["h_ke"], i + 1)
                act_f(ke, ke, ACT.Exp).then_inc(s["h_ke_e"], 1)
                se.wait_ge(s["h_k_mm"], i + 1)
                act_f(k_tok2, heads(banks[2]), ACT.Copy).then_inc(s["h_k"], 1)
                se.wait_ge(s["h_o_mm"], i + 1)
                act_f(mix[:, 0:4, bass.ds(HC * i, HC)], heads(banks[3]), ACT.Copy).then_inc(s["h_o"], 1)
                for b in range(4):
                    se.wait_ge(s["a_t_mm"], 4 * i + b + 1)
                    act_f(pT[:, 4 * b:4 * b + 4, :], heads(banks[4 + b]), ACT.Copy).then_inc(s["a_t"], 1)
                se.wait_ge(s["a_v_mm"], i + 1)
                for g in range(2):
                    act_f(vz[:, g, :, 64 * g:64 * g + 64],
                          banks[4][:, 0:2 * HC].rearrange("p (c f) -> p c f", c=2)[:, :, 64 * g:64 * g + 64],
                          ACT.Copy).then_inc(s["a_v"], 1)
                se.wait_ge(s["a_o_mm"], i + 1)
                act_f(mix[:, 4:8, bass.ds(HC * i, HC)], heads(banks[5]), ACT.Copy).then_inc(s["a_o"], 1)

            se.wait_ge(s["cum_scan"], 1)
            mixer2(0)
            with se.Fori(1, NB) as i:
                mixer2(i)
            se.wait_ge(s["h_o"], NB)
            for hd in range(NH):
                act_f(sq2[:, hd, :], mix[:, hd, :], ACT.Square).then_inc(s["head_sq"], 1)
            for hd in range(NH):
                se.wait_ge(s["head_rec"], 2 * NJ + hd + 1)
                act_f(yr2[:, hd, :], yr2[:, hd, :], ACT.Sqrt).then_inc(s["head_root"], 1)
            squares(x, h, ("taken", 73))
            root(rstd[:, :])
            ffn(FB, DONE[SLOT["UP2"] - 1], 2)
            squares(x, h, ("taken", 81))
            root(rstd[:, :])

        @block.gpsimd
        def _(pool):
            pool.wait_ge(s["head_sum"], NJ)
            for sc in scans:
                for a in (sc.kh_bd, sc.n_bd, sc.ak_bd, sc.S_bd, sc.S):
                    nc.gpsimd.memset(a, 0.0).then_inc(s["bd_clean"], 1)

            def diagonal(to, src, name):
                nc.gpsimd.tensor_tensor(to.rearrange("p j (q t) -> p j q t", q=2),
                                        src.unsqueeze(2).broadcast_to([P, NJ, 2, L]),
                                        headones.rearrange("p (q t) -> p q t", q=2).unsqueeze(1)
                                        .broadcast_to([P, NJ, 2, L]), ALU.mult).then_inc(s[name], 1)

            def chunk(i, isx):
                n = i + (NCC if isx else 0)

                def done(name, d, per=1, at=0):
                    pool.wait_ge(s[f"{name}{d}"], per * n + (at or per))

                at = places(pool, i, isx)
                for d, sc in enumerate(scans):
                    if not (isinstance(i, int) and i == 0 and not isx):
                        pool.wait_ge(s[f"ds_mm{d}"], n)
                    diagonal(sc.v_bd, vT[:, :, bass.ds(at[d], L)], f"bds{d}")
                for d, sc in enumerate(scans):
                    done("keys", d, 4, 1)
                    diagonal(sc.kt_bd, sc.kt, f"bds{d}")
                    done("keys", d, 4, 2)
                    diagonal(sc.bh_bd, sc.bh, f"bds{d}")
                for l in range(1, LEVELS + 1):
                    for d, sc in enumerate(scans):
                        done("X", d, LEVELS, l)
                        diagonal(sc.X_bd, sc.X, f"X_bd{d}")
                for d, sc in enumerate(scans):
                    done("S", d)
                    diagonal(sc.S_bd, sc.S, f"S_bd{d}")

            chunk(0, False)
            with pool.Fori(1, NCC) as i:
                chunk(i, False)
            with pool.Fori(0, NCX) as i:
                chunk(i, True)
            pool.wait_ge(s["mixed"], NJ)
            for a in pad:
                nc.gpsimd.memset(a, 0.0).then_inc(s["pads_clean"], 1)
            pool.wait_ge(s["taken"], 51)
            nc.gpsimd.memset(hreset, 1.0).then_inc(s["pool_step"], 1)
            pool.wait_ge(s["pool_step"], 1)
            nc.gpsimd.memset(hreset[:, :, :, 0:1], 0.0).then_inc(s["pads2"], 1)
            for a in (kz[0], kz[1], vp[:, 0:HC]):
                nc.gpsimd.memset(a, 0.0).then_inc(s["pads2"], 1)
            nc.gpsimd.memset(vz, 0.0).then_inc(s["pads2"], 1)
            nc.gpsimd.memset(S2, 0.0).then_inc(s["S_clean"], 1)

            def mixer2(i):
                first = isinstance(i, int) and i == 0
                if not first:
                    pool.wait_ge(s["a_s_mm"], i)
                nc.gpsimd.tensor_copy(q_ch, aq[:, :, bass.ds(HC * i, HC)]).then_inc(s["a_in"], 1)
                if not first:
                    pool.wait_ge(s["h_mm"], 8 * i)
                    pool.wait_ge(s["h_v_mm"], i)
                nc.gpsimd.tensor_copy(v_ch, pr[:, 8:12, bass.ds(HC * i, HC)]).then_inc(s["h_in"], 1)
                nc.gpsimd.tensor_copy(k_ch.rearrange("p h t -> p (h t)"),
                                      kh.rearrange("p n h t -> p (n h t)")[:, bass.ds(NH * HC * i, NH * HC)]
                                      ).then_inc(s["h_in"], 1)
                if not first:
                    pool.wait_ge(s["a_v_mm"], i)
                nc.gpsimd.tensor_copy(v_st.rearrange("p c t -> p (c t)"),
                                      vp[:, bass.ds(HC * i, 2 * HC)]).then_inc(s["a_in"], 1)

            pool.wait_ge(s["taken"], 73)
            pool.wait_ge(s["keys_hg"], NH)
            mixer2(0)
            with pool.Fori(1, NB) as i:
                mixer2(i)
            pool.wait_ge(s["mix2"], NH)
            pool.wait_ge(s["a_o"], NB)
            for a in pad1:
                nc.gpsimd.memset(a[:, 0:2], 0.0).then_inc(s["pads_clean"], 1)

        @block.vector
        def _(dve):
            V = nc.vector
            steps = Steps(dve, "dve_step")
            norms = [0]

            def mean_square(r, bank, t):
                norms[0] += 1
                dve.wait_ge(s["square_sum"], norms[0])
                steps.do(V.tensor_scalar(r, bank[:, 0:t], 1.0 / D, EPS, ALU.mult, ALU.add))
                steps.last()
                V.reciprocal(r, r).then_inc(s["mean_sq"], 1)

            def norm(to, src, r, gain, shift=None):
                dve.wait_ge(s["root"], norms_done[0] + 1)
                norms_done[0] += 1
                for k in range(KB):
                    ins = V.scalar_tensor_tensor(to[:, k, :], src[:, k, :], gain[:, k:k + 1], r, ALU.mult, ALU.mult)
                    if shift is None:
                        ins.then_inc(s["normed"], 1)
                    else:
                        steps.do(ins)
                if shift is not None:
                    steps.last()
                    for k in range(KB):
                        V.tensor_scalar(to[:, k, :], to[:, k, :], shift[:, k:k + 1], None,
                                        ALU.add).then_inc(s["normed"], 1)

            norms_done = [0]
            dve.wait_ge(s["vec_in"], 16)
            mean_square(rstd_c[:, :], banks[0], TC)
            mean_square(rstd[:, :], banks[1], TX)
            dve.wait_ge(s["product"], DONE[SLOT["W_IN"] - 1])
            V.tensor_tensor(mod[:, 0:16, :], banks[7][:, 0:32].rearrange("p (m c) -> p m c", c=2),
                            spread(vcol("adab")[:, 0:16], 16, 2), ALU.add).then_inc(s["mod"], 1)
            dve.wait_ge(s["mod"], 1)
            for c in range(2):
                V.scalar_tensor_tensor(gains[:, c, :], mod[:, 8:16, c], 1.0, vcol("n1"), ALU.add,
                                       ALU.mult).then_inc(s["gain"], 1)
            dve.wait_ge(s["gain"], 2)
            norm(hc, ctx_sb, rstd_c[:, :], gains[:, 1], mod[:, 0:8, 1])
            norm(h, x, rstd[:, :], gains[:, 0], mod[:, 0:8, 0])

            for j in range(NJ):
                dve.wait_ge(s["head_sum"], j + 1)
                steps.do(V.tensor_scalar(kk[:, j, TC:TT], banks[2 * j][:, 0:TX], 1e-24, None, ALU.max))
                steps.do(V.tensor_scalar(kk[:, j, 0:TC], banks[2 * j + 1][:, 0:TC], 1e-24, None, ALU.max))
                steps.last()
                V.reciprocal(kk[:, j, :], kk[:, j, :]).then_inc(s["head_rec"], 1)
            for j in range(NJ):
                dve.wait_ge(s["head_root"], j + 1)
                V.scalar_tensor_tensor(kk[:, j, :], kT[:, j, :], vcol("kk")[:, j:j + 1], kk[:, j, :], ALU.mult,
                                       ALU.mult).then_inc(s["kk_ready"], 1)
            cw = vcol("conva", 3, 4)
            cb, u_, t_ = px[:, 0:4], px[:, 4:8], px[:, 8:12]
            steps.do(V.tensor_tensor(u_, u_, t_, ALU.mult))
            steps.last()
            for j in range(4):
                steps.do(V.tensor_scalar(t_[:, j, :], u_[:, j, :], cw[:, 1, j:j + 1], None, ALU.mult))
            steps.last()
            for j in range(4):
                steps.do(V.scalar_tensor_tensor(t_[:, j, 1:TX], u_[:, j, 0:TX - 1], cw[:, 0, j:j + 1],
                                                t_[:, j, 1:TX], ALU.mult, ALU.add))
            steps.last()
            for j in range(4):
                steps.do(V.scalar_tensor_tensor(t_[:, j, 0:TX - 1], u_[:, j, 1:TX], cw[:, 2, j:j + 1],
                                                t_[:, j, 0:TX - 1], ALU.mult, ALU.add))
            steps.last()
            V.tensor_tensor(cb, cb, t_, ALU.mult).then_inc(s["conv_ready"], 1)
            dve.wait_ge(s["conv_ready"], 1)

            kaS = spread(vcol("ka"), NJ, L)
            i2 = ident2.unsqueeze(1).broadcast_to([P, NJ, L])

            def chunk(i, isx):
                n = i + (NCC if isx else 0)
                bank = [banks[0:4], banks[4:8]]

                def done(name, d, per=1, at=0):
                    dve.wait_ge(s[f"{name}{d}"], per * n + (at or per))

                def half(b, k):
                    return b[:, 256 * k:256 * k + 256].rearrange("p (j t) -> p j t", j=NJ)

                def flat(a):
                    return a.rearrange("p a b -> p (a b)")

                def over(mask):
                    return mask.unsqueeze(1).broadcast_to([P, NJ, L])

                at = [bass.ds(chunk_at(d, i, isx), L) for d in range(2)]
                for d, sc in enumerate(scans):
                    done("z_mm", d)
                    if not (isinstance(i, int) and i == 0 and not isx):
                        dve.wait_ge(s[f"ds_mm{d}"], n)
                    V.tensor_tensor(sc.gate.rearrange("p a b c -> p (a b) c"),
                                    bank[d][0][:, :].rearrange("p (q t) -> p q t", q=8),
                                    spread(vcol("wa0", 2, 8)[:, d], 8, L), ALU.add).then_inc(s[f"z_biased{d}"], 1)
                for d, sc in enumerate(scans):
                    done("z_tanh", d)
                    steps.do(V.tensor_scalar(sc.gate[:, 0], sc.gate[:, 0], -DECAY / 2, -DECAY / 2, ALU.mult, ALU.add))
                    steps.do(V.tensor_scalar(sc.gate[:, 1], sc.gate[:, 1], 0.5, 0.5, ALU.mult, ALU.add))
                for d, sc in enumerate(scans):
                    steps.last()
                    to, g, r = flat(sc.cum), flat(sc.gate[:, 0]), reset[:, d, :]
                    if d == 1:
                        to, g, r = to[:, ::-1], g[:, ::-1], r[:, ::-1]
                    steps.do(V.tensor_tensor_scan(to, r, g, 0.0, ALU.mult, ALU.add))
                    steps.do(V.scalar_tensor_tensor(sc.kd, sc.gate[:, 1], -1.0, kaS, ALU.add, ALU.mult))
                for d, sc in enumerate(scans):
                    steps.last()
                    V.tensor_tensor(sc.gate[:, 0], sc.cum, sc.gate[:, 0], ALU.subtract).then_inc(s[f"decays{d}"], 1)
                    steps.do(V.scalar_tensor_tensor(sc.kd, sc.kd, 1.0, kT[:, :, at[d]], ALU.add, ALU.mult))
                    steps.do(V.tensor_tensor(sc.gate[:, 1], sc.gate[:, 1], kk[:, :, at[d]], ALU.mult))
                for d, sc in enumerate(scans):
                    steps.last()
                    done("exps", d, 3)
                    V.tensor_tensor(sc.kt, kk[:, :, at[d]], sc.gate[:, 0], ALU.mult).then_inc(s[f"keys{d}"], 1)
                    V.tensor_tensor(sc.bh, sc.gate[:, 1], sc.cum, ALU.mult).then_inc(s[f"keys{d}"], 1)
                    for q in range(2):
                        r = slice(64 * q, 64 * q + 64)
                        V.tensor_tensor(sc.kh_bd[r, :, r], sc.kd[r], sc.cum[r], ALU.mult).then_inc(s[f"keys{d}"], 1)
                    if isx:
                        ax = bass.ds(chunk_at(d, i, isx) - TC, L)
                        V.tensor_tensor(sc.rt, rT[:, :, ax], sc.pin, ALU.mult).then_inc(s[f"rt{d}"], 1)
                for d, sc in enumerate(scans):
                    done("m_mm", d, 3, 1)
                    steps.do(V.scalar_tensor_tensor(sc.w, half(bank[d][3], 0), -1.0, over(level[:, d, 0]), ALU.mult,
                                                    ALU.mult))
                for d, sc in enumerate(scans):
                    steps.last()
                    V.tensor_tensor(sc.X, sc.w, i2, ALU.add).then_inc(s[f"X{d}"], 1)
                for d, sc in enumerate(scans):
                    for q in range(2):
                        r = slice(64 * q, 64 * q + 64)
                        V.tensor_tensor(sc.ak_bd[r, :, r], half(bank[d][3], 1)[r],
                                        over(strict[:, d])[r], ALU.mult).then_inc(s[f"ak_bd{d}"], 1)
                    if isx:
                        dve.wait_ge(s[f"m2_mm{d}"], i + 1)
                        V.tensor_tensor(sc.rm.rearrange("p a b c -> p (a b) c"),
                                        bank[d][2][:, :].rearrange("p (q t) -> p q t", q=8),
                                        incl[:, d].unsqueeze(1).broadcast_to([P, 8, L]),
                                        ALU.mult).then_inc(s[f"rm{d}"], 1)
                for l in range(2, LEVELS + 1):
                    for d, sc in enumerate(scans):
                        done("level_mm", d, 2 * LEVELS - 2, 2 * l - 3)
                        V.tensor_tensor(sc.w, half(bank[d][3], 0), over(level[:, d, l - 1]),
                                        ALU.mult).then_inc(s[f"w{d}"], 1)
                    for d, sc in enumerate(scans):
                        done("level_mm", d, 2 * LEVELS - 2, 2 * l - 2)
                        done("X_bd", d, LEVELS, l - 1)
                        V.tensor_tensor(sc.X, half(bank[d][3], 1), sc.X, ALU.add).then_inc(s[f"X{d}"], 1)
                for d, sc in enumerate(scans):
                    done("ds_mm", d)
                    if isx:
                        ax = bass.ds(chunk_at(d, i, isx) - TC, L)
                        V.tensor_copy(y_dir[d][:, :, ax], half(bank[d][2], 0)).then_inc(s[f"y_out{d}"], 1)
                    last_step = sc.pin[:, :, L - 1 if d == 0 else 0]
                    steps.do(V.tensor_tensor(sc.S, half(bank[d][2], 1), sc.S, ALU.add))
                    steps.last()
                    V.tensor_tensor(sc.S, sc.S, spread(last_step, NJ, L), ALU.mult).then_inc(s[f"S{d}"], 1)
                if not isx:
                    dve.wait_ge(s["product"], DONE[SLOT["ADA2"] + 3] + 4 * i)
                    V.tensor_tensor(mod[:, bass.ds(16 + 8 * i, 8), :],
                                    banks[2][:, 0:16].rearrange("p (m c) -> p m c", c=2),
                                    spread(vcol("adab")[:, bass.ds(16 + 8 * i, 8)], 8, 2),
                                    ALU.add).then_inc(s["mod"], 1)

            def turns(first, count, isx):
                with dve.Fori(first, first + count) as i:
                    steps.loop(i - first if first else i, 16)
                    chunk(i, isx)
                    steps.end(count)

            dve.wait_ge(s["bd_clean"], 10)
            chunk(0, False)
            turns(1, NCC - 1, False)
            turns(0, NCX, True)

            for d in range(2):
                dve.wait_ge(s[f"S_bd{d}"], NC)
                dve.wait_ge(s[f"y_out{d}"], NCX)
            for j in range(NJ):
                V.tensor_tensor(ys[:, j, :], y_dir[0][:, j, :], y_dir[1][:, j, :], ALU.add).then_inc(s["y_rkr"], 1)
                V.scalar_tensor_tensor(rkr[:, j, :], rT[:, j, :], vcol("rk")[:, j:j + 1], kT[:, j, TC:TT], ALU.mult,
                                       ALU.mult).then_inc(s["y_rkr"], 1)
            for j in range(NJ):
                dve.wait_ge(s["y_rkr_mm"], 2 * j + 1)
                V.scalar_tensor_tensor(yc[:, j, :], banks[j][:, :], -1.0 / L, ys[:, j, :], ALU.mult,
                                       ALU.add).then_inc(s["centred_bonus"], 1)
                dve.wait_ge(s["y_rkr_mm"], 2 * j + 2)
                V.tensor_tensor(bonus[:, j, :], banks[4 + j][:, :], vT[:, j, TC:TT], ALU.mult).then_inc(s["centred_bonus"], 1)
            for j in range(NJ):
                dve.wait_ge(s["head_sum"], NJ + j + 1)
                steps.do(V.tensor_scalar(yr[:, j, :], banks[j][:, :], 1.0 / L, GN_EPS, ALU.mult, ALU.add))
                steps.last()
                V.reciprocal(yr[:, j, :], yr[:, j, :]).then_inc(s["head_rec"], 1)
            for j in range(NJ):
                dve.wait_ge(s["head_root"], NJ + j + 1)
                steps.do(V.scalar_tensor_tensor(yc[:, j, :], yc[:, j, :], vcol("lng")[:, j:j + 1], yr[:, j, :],
                                                ALU.mult, ALU.mult))
                steps.last()
                steps.do(V.scalar_tensor_tensor(yc[:, j, :], yc[:, j, :], vcol("lnb")[:, j:j + 1], bonus[:, j, :],
                                                ALU.add, ALU.add))
                steps.last()
                dve.wait_ge(s["gate_mm"], j + 1)
                V.tensor_tensor(y_rwkv[:, j, :], banks[4 + j][:, :], yc[:, j, :], ALU.mult).then_inc(s["mixed"], 1)

            def residual(p0, n, nbanks, gate=None, per=1):
                def one(m, bank, i=None):
                    dve.wait_ge(s["product"], p0 + per * m + per)
                    xm = x[:, bass.ds(m, 1), :].rearrange("p a t -> p (a t)")
                    if gate is None:
                        V.tensor_tensor(xm, banks[bank][:, :], xm, ALU.add).then_inc(s["taken"], 1)
                    else:
                        V.scalar_tensor_tensor(xm, banks[bank][:, :], mod[:, bass.ds(gate + m, 1), 0], xm, ALU.mult,
                                               ALU.add).then_inc(s["taken"], 1)

                with dve.Fori(0, n // nbanks) as i:
                    for b in range(nbanks):
                        one(nbanks * i + b, b)

            residual(DONE[SLOT["W_OUT"] - 1], KB, 4, gate=2 * KB)
            V.scalar_tensor_tensor(gain2[:, :], mod[:, 4 * KB:5 * KB, 0], 1.0, vcol("n2"), ALU.add,
                                   ALU.mult).then_inc(s["gain"], 1)
            dve.wait_ge(s["gain"], 3)
            mean_square(rstd[:, :], banks[6], TX)
            norm(h, x, rstd[:, :], gain2, mod[:, 3 * KB:4 * KB, 0])

            def ffn(first, p0, taps):
                def body(i, u, base):
                    dve.wait_ge(s["gate_in"], first + 2 * i + u + 1)
                    if not (isinstance(i, int) and i == 0 and first == 0):
                        dve.wait_ge(s["silu"], first + 2 * i + u - 1)
                    taps(i, u)
                    dve.wait_ge(s["silu"], first + 2 * i + u + 1)
                    dve.wait_ge(s["product"], p0 + 4 * i + 2 * u + 2)
                    V.tensor_tensor(act[:, bass.ds(2 * i + u, 1), :].rearrange("p a t -> p (a t)"), silu[u],
                                    banks[2 * u + 1][:, :], ALU.mult).then_inc(s["val_free"], 1)
                return body

            def run_ffn(first, p0, taps, per):
                body = ffn(first, p0, taps)
                body(0, 0, 0)
                body(0, 1, 0)
                with dve.Fori(1, FB // 2) as i:
                    steps.loop(i - 1, 2 * per)
                    body(i, 0, 0)
                    body(i, 1, 0)
                    steps.end(FB // 2 - 1)

            def taps_grid(i, u):
                f0 = VEC["fcw"][0] + 10 * (2 * i + u)
                to = conv[u].rearrange("p (y x) -> p y x", y=GRID_H)
                steps.do(V.tensor_scalar(to, pad[u][:, 0:GRID_H, 0:GRID_W], v[:, bass.ds(f0, 1)],
                                         v[:, bass.ds(f0 + 9, 1)], ALU.mult, ALU.add))
                for n in range(1, 9):
                    steps.last()
                    ins = V.scalar_tensor_tensor(to, pad[u][:, n // 3:n // 3 + GRID_H, n % 3:n % 3 + GRID_W],
                                                 v[:, bass.ds(f0 + n, 1)], to, ALU.mult, ALU.add)
                    if n < 8:
                        steps.do(ins)
                ins.then_inc(s["conv"], 1)

            def taps_causal(i, u):
                f0 = VEC["cw2"][0] + 4 * (2 * i + u)
                steps.do(V.tensor_scalar(conv[u], pad1[u][:, 0:TX], v[:, bass.ds(f0, 1)], v[:, bass.ds(f0 + 3, 1)],
                                         ALU.mult, ALU.add))
                for n in range(1, 3):
                    steps.last()
                    ins = V.scalar_tensor_tensor(conv[u], pad1[u][:, n:n + TX], v[:, bass.ds(f0 + n, 1)], conv[u],
                                                 ALU.mult, ALU.add)
                    if n < 2:
                        steps.do(ins)
                ins.then_inc(s["conv"], 1)

            run_ffn(0, DONE[SLOT["UP1"] - 1], taps_grid, 8)
            residual(DONE[SLOT["DOWN1"] - 1], KB, 2, gate=5 * KB, per=2)
            mean_square(rstd[:, :], banks[6], TX)
            norm(x, x, rstd[:, :], vcol("fin"))

            lb = vcol("lb", 2, 4)
            V.tensor_tensor(lbv, lb[:, 0], lb[:, 1], ALU.subtract).then_inc(s["lb"], 1)
            mean_square(rstd[:, :], banks[7], TX)
            norm(h, x, rstd[:, :], vcol("nmix"))
            dve.wait_ge(s["sig"], 1)
            steps.do(V.tensor_scalar(oml, lbv, -1.0, 1.0, ALU.mult, ALU.add))
            steps.last()
            dve.wait_ge(s["taken"], 73)
            for hd in range(NH):
                dve.wait_ge(s["forget"], hd + 1)
                src = pr[:, 4 + hd, :].rearrange("p (n t) -> p n t", n=NB)
                V.tensor_scalar(cumf[:, :, hd, :], src, oml[:, hd:hd + 1], lbv[:, hd:hd + 1], ALU.mult,
                                ALU.add).then_inc(s["f"], 1)
            for hd in range(NH):
                dve.wait_ge(s["f"], hd + 1)
                V.tensor_scalar(kh[:, :, hd, :], cumf[:, :, hd, :], -1.0, 1.0, ALU.mult,
                                ALU.add).then_inc(s["keys_hg"], 1)
                V.tensor_scalar(qh[:, :, hd, :], pr[:, hd, :].rearrange("p (n t) -> p n t", n=NB), HC ** -0.5, None,
                                ALU.mult).then_inc(s["q_hg"], 1)
            cf2 = cumf.rearrange("p n h t -> p (n h t)")
            dve.wait_ge(s["cum_f"], NH)
            dve.wait_ge(s["pads2"], 5)
            V.tensor_tensor_scan(cf2, hreset.rearrange("p n h t -> p (n h t)"), cf2, 0.0, ALU.mult,
                                 ALU.add).then_inc(s["cum_scan"], 1)
            dve.wait_ge(s["cum_scan"], 1)
            dve.wait_ge(s["masks_in"], 32)

            def mixer2(i):
                first = isinstance(i, int) and i == 0
                chunk = bass.ds(NH * HC * i, NH * HC)
                cf, kf, qf = (a.rearrange("p n h t -> p (n h t)")[:, chunk] for a in (cumf, kh, qh))
                dve.wait_ge(s["a_s_mm"], i + 1)
                if not first:
                    dve.wait_ge(s["a_t_mm"], 4 * i)
                mask = band_sb[:, bass.ds(i, 1), :].broadcast_to([P, 2, 2 * HC])
                for j in range(4):
                    steps.do(V.scalar_tensor_tensor(pp[:, 2 * j:2 * j + 2, :],
                                                    banks[4 + j][:, :].rearrange("p (g k) -> p g k", g=2), 0.125,
                                                    mask, ALU.mult, ALU.add))
                steps.last()
                steps.do(V.tensor_reduce(hi, pp, AX.X, ALU.max))
                steps.last()
                steps.do(V.tensor_tensor(hi, hi, sink_order, ALU.max))
                steps.last()
                V.tensor_scalar(nm, hi, -1.0, None, ALU.mult).then_inc(s["a_nm"], 1)
                V.tensor_tensor(dsk, sink_order, hi, ALU.subtract).then_inc(s["a_ds"], 1)

                def halves(a, l):
                    w = a.rearrange("p (b t) -> p b t", t=1 << l)
                    return w[:, :, 0:1 << l - 1], w[:, :, 1 << l - 1:1 << l]

                def decay(l):
                    nb = NH * HC >> l
                    early, late = halves(cf, l)
                    mid = early[:, :, (1 << l - 1) - 1:1 << l - 1].broadcast_to([P, nb, 1 << l - 1])
                    de_early, de_late = halves(de[l % 2], l)
                    V.tensor_tensor(de_early, mid, early, ALU.subtract).then_inc(s["h_d"], 1)
                    V.tensor_tensor(de_late, late, mid, ALU.subtract).then_inc(s["h_d"], 1)

                def scale(l):
                    dve.wait_ge(s["h_e"], HLEV * i + l)
                    if not first or l > 2:
                        dve.wait_ge(s["h_mm"], 8 * i + l - 2)
                    z, e = halves(zz[l % 2], l), halves(de[l % 2], l)
                    V.tensor_tensor(z[0], e[0], halves(kf, l)[0], ALU.mult).then_inc(s["h_z"], 1)
                    if l > 1:
                        dve.wait_ge(s["h_mm"], 8 * i + l - 1)
                    V.tensor_tensor(z[1], e[1], halves(qf, l)[1], ALU.mult).then_inc(s["h_z"], 1)

                def pick(l):
                    mask = hmask_sb[:, l - 1, :].unsqueeze(1).broadcast_to([P, NH, HC])
                    bank = banks[l % 2][:, :].rearrange("p (h t) -> p h t", h=NH)
                    if l == 1:
                        if not first:
                            dve.wait_ge(s["h_o_mm"], i)
                        V.tensor_tensor(sT, bank, mask, ALU.mult).then_inc(s["h_s"], 1)
                    else:
                        V.copy_predicated(sT, mask, bank).then_inc(s["h_s"], 1)

                decay(1)
                decay(2)
                dve.wait_ge(s["h_ec"], i + 1)
                V.tensor_tensor(qe.rearrange("p h t -> p (h t)"), ec.rearrange("p h t -> p (h t)"), qf,
                                ALU.mult).then_inc(s["h_qe"], 1)
                cw_ = cf.rearrange("p (h t) -> p h t", h=NH)
                V.tensor_tensor(ke, cw_[:, :, HC - 1:HC].broadcast_to([P, NH, HC]), cw_,
                                ALU.subtract).then_inc(s["h_ke"], 1)
                for l in range(1, HLEV + 1):
                    if l > 2:
                        dve.wait_ge(s["h_s"], 8 * i + l - 2)
                    scale(l)
                    if l > 1:
                        pick(l - 1)
                    if l + 2 <= HLEV:
                        dve.wait_ge(s["h_z"], 2 * HLEV * i + 2 * l)
                        decay(l + 2)
                dve.wait_ge(s["h_ke_e"], i + 1)
                dve.wait_ge(s["h_mm"], 8 * i + HLEV)
                dve.wait_ge(s["h_s"], 8 * i + HLEV - 1)
                V.tensor_tensor(ke.rearrange("p h t -> p (h t)"), ke.rearrange("p h t -> p (h t)"), kf,
                                ALU.mult).then_inc(s["h_kend"], 1)
                pick(HLEV)
                dve.wait_ge(s["a_es"], i + 1)
                dve.wait_ge(s["a_p"], NQ * i + NQ)
                dve.wait_ge(s["h_mm"], 8 * i + HLEV + 1)
                dve.wait_ge(s["h_s"], 8 * i + HLEV)
                steps.do(V.tensor_tensor(den, den, esk, ALU.add))
                pick(HLEV + 1)
                steps.last()
                steps.do(V.reciprocal(den, den))
                steps.last()
                V.tensor_tensor(pp, pp, spread(den, NQ, 2 * HC), ALU.mult).then_inc(s["a_pn"], 1)
                dve.wait_ge(s["h_o_mm"], i + 1)
                steps.do(V.tensor_tensor(S2, S2, ec[:, :, HC - 1:HC].broadcast_to([P, NH, HC]), ALU.mult))
                steps.last()
                dve.wait_ge(s["h_ds"], i + 1)
                V.tensor_tensor(S2, banks[3][:, :].rearrange("p (h t) -> p h t", h=NH), S2,
                                ALU.add).then_inc(s["h_S"], 1)

            sink_order = vcol("sinks")
            dve.wait_ge(s["S_clean"], 1)
            mixer2(0)
            with dve.Fori(1, NB) as i:
                steps.loop(i - 1, 9)
                mixer2(i)
                steps.end(NB - 1)
            for hd in range(NH):
                dve.wait_ge(s["head_sum"], 2 * NJ + hd + 1)
                steps.do(V.tensor_scalar(yr2[:, hd, :], banks[hd][:, :], 1.0 / HC, EPS, ALU.mult, ALU.add))
                steps.last()
                V.reciprocal(yr2[:, hd, :], yr2[:, hd, :]).then_inc(s["head_rec"], 1)
            for hd in range(NH):
                dve.wait_ge(s["head_root"], 2 * NJ + hd + 1)
                steps.do(V.scalar_tensor_tensor(mix[:, hd, :], mix[:, hd, :], vcol("hgn"), yr2[:, hd, :], ALU.mult,
                                                ALU.mult))
            steps.last()
            for hd in range(NH):
                V.tensor_tensor(mix[:, hd, :], mix[:, hd, :], pr[:, 12 + hd, :], ALU.mult).then_inc(s["mix2"], 1)
            residual(DONE[SLOT["W_OUT2"] - 1], KB, 4)
            mean_square(rstd[:, :], banks[6], TX)
            norm(h, x, rstd[:, :], vcol("nffn"))
            run_ffn(FB, DONE[SLOT["UP2"] - 1], taps_causal, 2)
            residual(DONE[SLOT["DOWN2"] - 1], KB, 2, per=2)
            mean_square(rstd[:, :], banks[6], TX)
            norm(x, x, rstd[:, :], vcol("fin2"))


def _tiles(w, blocks=KB):
    k, m = w.shape
    t = w.reshape(k // P, P, m // P, P).transpose(2, 1, 0, 3)
    return t.reshape(m // P, P, k)


def _halves(w):
    t = _tiles(w).reshape(D // P, P, 2, HALF * P)
    return t.transpose(0, 2, 1, 3).reshape(2 * D // P, P, HALF * P)


def _columns(v):
    return v.reshape(-1, P).T


def _arrange(a):
    g = {n: np.asarray(v) for n, v in a.items()}
    dc = D // 2
    w_in = g["w_in"][0]
    w_in = np.concatenate([w_in[:, :4 * dc], w_in[:, 6 * dc + 128:], w_in[:, 4 * dc:6 * dc + 128]], axis=1)
    up1 = g["ffn_w_up"][0].reshape(D, 2, FB, P).transpose(0, 2, 1, 3).reshape(D, 2 * DFF)
    up2 = np.stack([g["w_gate_2"][0].reshape(D, FB, P), g["w_up_2"][0].reshape(D, FB, P)], axis=2).reshape(D, 2 * DFF)
    head = np.concatenate([np.arange(64) + 64 * h for j in range(4) for h in (j, j + 4)])
    w_in2 = g["w_in_2"][0]
    w_in2 = np.concatenate([w_in2[:, :2048], w_in2[:, 2048 + head], w_in2[:, 2560:]], axis=1)
    w_out2 = g["w_out_2"][0]
    w_out2 = np.concatenate([w_out2[:512], w_out2[512 + head]], axis=0)
    batt = g["b_attn_2"][0]
    batt = np.concatenate([batt[head], batt[512:]])
    ada = _tiles(g["ada_w"][0])
    w8 = np.concatenate([ada[:16], _tiles(w_in), ada[16:], _tiles(g["w_out"][0]), _tiles(up1),
                         _tiles(w_in2), _tiles(w_out2), _tiles(up2)])
    w11 = np.concatenate([_halves(g["ffn_w_down"][0]), _halves(g["w_down_2"][0])])
    lora = np.zeros((P, 2, 2, 4, P), np.float32)
    for d in range(2):
        lora[:64, d, 0] = g["rw_w_up"][0, d].reshape(64, 4, P)
        lora[64:, d, 1] = g["rw_a_up"][0, d].reshape(64, 4, P)
    vec = np.zeros((P, NVEC), np.float32)

    def put(name, v):
        o, w = VEC[name]
        vec[:, o:o + w] = v.reshape(P, w)

    put("n1", _columns(g["norm1_g"]))
    put("n2", _columns(g["norm2_g"]))
    put("fin", _columns(g["final_g"]))
    put("cs", np.stack([_columns(g["c"]), _columns(g["c_ctx"])], axis=2))
    put("adab", _columns(g["ada_b"]))
    put("conva", _columns(g["conv_a_w"]))
    put("wa0", np.concatenate([_columns(g[n][0, d]) for d in range(2) for n in ("rw_w0", "rw_a0")], axis=1))
    put("kk", _columns(g["rw_k_k"]))
    put("ka", _columns(g["rw_k_a"]))
    put("rk", _columns(g["rw_r_k"]))
    put("lng", _columns(g["rw_ln_g"]))
    put("lnb", _columns(g["rw_ln_b"]))
    fcw = np.concatenate([g["ffn_conv_w"].reshape(9, FB, P), g["ffn_conv_b"].reshape(1, FB, P)])
    put("fcw", fcw.transpose(2, 1, 0))
    put("nmix", _columns(g["norm_mix_w_2"]))
    put("nffn", _columns(g["norm_ffn_w_2"]))
    put("batt", _columns(batt))
    put("lb", _columns(g["lb_logits_2"]))
    put("hgn", _columns(g["hg_norm_w_2"]))
    sinks = g["sinks_2"][0][[h for j in range(4) for h in (j, j + 4)]]
    put("sinks", np.broadcast_to(sinks, (P, NQ)))
    cw2 = np.concatenate([g["conv_w_2"].reshape(3, FB, P), g["conv_b_2"].reshape(1, FB, P)])
    put("cw2", cw2.transpose(2, 1, 0))
    put("fin2", _columns(g["final_norm_w_2"]))

    def features(x):
        return np.ascontiguousarray(x.T.reshape(KB, P, -1).transpose(1, 0, 2))

    return {
        "xT": features(g["x"][0]), "ctxT": features(g["ctx"][0]), "vec": vec, "con": constants(),
        "hmask": level_masks(), "band": band_masks(), "w8": w8, "w11": w11,
        "lora": lora.reshape(P, 16 * P), "gup": np.ascontiguousarray(g["rw_g_up"][0]),
    }


def kernel(**inputs):
    import concourse.bacc as _bacc
    from concourse.bass_utils import run_bass_kernel_spmd as _run

    nc = _bacc.Bacc("TRN2", target_bir_lowering=False, num_devices=1)
    arrays = {n: np.ascontiguousarray(a) for n, a in _arrange(inputs).items()}
    args = {n: nc.dram_tensor(n, a.shape, mybir.dt.from_np(a.dtype), kind="ExternalInput").ap()
            for n, a in arrays.items()}
    out = nc.dram_tensor("outT", (P, KB, TX), F32, kind="ExternalOutput").ap()
    two_blocks(nc, outT=out, **args)
    r = _run(nc, [arrays], core_ids=[0])
    got = r.results[0]["outT"]
    return got.transpose(2, 1, 0).reshape(1, TX, D)
```

```python
from contextlib import ExitStack

import numpy as np
import concourse.bass as bass
from concourse import mybir

F32 = mybir.dt.float32
U32 = mybir.dt.uint32
ALU = mybir.AluOpType
ACT = mybir.ActivationFunctionType
AX = mybir.AxisListType

P = 128
D = 1024
KB = D // P
TX = 512
TC = 256
TT = TC + TX
DFF = 2816
FB = DFF // P
HALF = FB // 2
GRID_W = 64
GRID_H = TX // GRID_W
DECAY = float(np.exp(-0.5))
EPS = 1e-6
GN_EPS = 64e-5
HD = 64
L = 128
NJ = 4
GP = 2
GH = 2 * GP
NG = NJ // GP
NCC, NCX = NG * TC // L, NG * TX // L
NC = NCC + NCX
LEVELS = 7
HC = 128
NH = 4
NB = TX // HC
NQ = 8
HLEV = 7

VEC = {}
_n = 0
for _name, _w in (("n1", KB), ("n2", KB), ("fin", KB), ("cs", 2 * KB), ("adab", 6 * KB), ("conva", 3 * 4),
                  ("wa0", 2 * 8), ("kk", 4), ("ka", 4), ("rk", 4), ("lng", 4), ("lnb", 4), ("fcw", FB * 10),
                  ("nmix", KB), ("nffn", KB), ("batt", 6), ("lb", 8), ("hgn", 1), ("sinks", NQ),
                  ("cw2", FB * 4), ("fin2", KB)):
    VEC[_name] = (_n, _w)
    _n += _w
NVEC = _n

CON = {}
_n = 0
for _name, _w in (("ident", P), ("ones", P), ("headones", P), ("level", 2 * LEVELS * L),
                  ("strict", 2 * L), ("incl", 2 * L), ("reset", 2 * GP * L)):
    CON[_name] = (_n, _w)
    _n += _w
NCON = _n


def constants():
    c = np.zeros((P, NCON), np.float32)

    def put(name, a):
        o, w = CON[name]
        c[:, o:o + w] = a.reshape(P, w)

    put("ident", np.eye(P))
    put("ones", np.ones((P, P)))
    put("headones", np.kron(np.eye(2), np.ones((HD, HD))))
    t, s = np.arange(L)[:, None], np.arange(L)[None, :]
    level = np.stack([(t >> l == s >> l) & (t >> (l - 1) & 1 == 1) & (s >> (l - 1) & 1 == 0)
                      for l in range(1, LEVELS + 1)])
    level = np.stack([level, level.transpose(0, 2, 1)])
    put("level", level.transpose(2, 0, 1, 3))
    put("strict", np.stack([t < s, t > s]).transpose(1, 0, 2))
    put("incl", np.stack([t <= s, t >= s]).transpose(1, 0, 2))
    reset = np.ones((2, GP, L))
    reset[0, :, 0] = 0
    reset[1, :, -1] = 0
    put("reset", np.broadcast_to(reset, (P, 2, GP, L)))
    return c


def band_masks():
    q, k = np.arange(HC)[:, None], np.arange(2 * HC)[None, :]
    band = (q + HC - k >= 0) & (q + HC - k < HC)
    m = np.stack([band & (k >= HC), band, band, band])
    return np.ascontiguousarray(np.where(m, 0.0, -3e38).transpose(1, 0, 2).astype(np.float32))


RING = 2
STAGES = (("ADA1", 8, 1), ("W_IN", 8, 2), ("W_INB", 1, 3), ("W_INC", 4, 4), ("ADA2", 16, 1), ("W_OUT", 4, 2),
          ("UP1", FB, 2), ("DOWN1", 16, 1), ("W_IN2", 11, 2), ("W_OUT2", 4, 2), ("UP2", FB, 2), ("DOWN2", 16, 1))
SLOT, DONE = {}, []
_n = _g = 0
for _name, _slots, _per in STAGES:
    SLOT[_name] = _g
    for _ in range(_slots):
        _n += _per
        DONE.append(_n)
    _g += _slots


def in_pairs(eng, n, body, peel=False):
    first = 0
    if peel:
        body(0, 0)
        body(0, 1)
        first = 1
    with eng.Fori(first, n // 2) as i:
        body(i, 0)
        body(i, 1)
    if n % 2:
        body(n // 2, 0)


def two_blocks(nc, xT, ctxT, vec, con, band, w8, w11, lora, gup, outT):
    with ExitStack() as ctx:
        def sb(name, shape, dt=F32):
            return ctx.enter_context(nc.sbuf_tensor(name, shape, dt))

        s = {}

        def sem(*names):
            for name in names:
                s[name] = ctx.enter_context(nc.semaphore(name))

        banks = [ctx.enter_context(nc.psum_tensor(f"bank{b}", [P, 512], F32)) for b in range(8)]

        x = sb("x", [P, KB, TX])
        v = sb("v", [P, NVEC])
        k_ = sb("k_", [P, NCON])
        ring = sb("ring", [P, RING, 2 * KB * P])
        mod = sb("mod", [P, 6 * KB, 2])
        gains = sb("gains", [P, 3, KB])
        siluc = sb("siluc", [P, 2 * KB])
        rstd = sb("rstd", [P, TX])
        gain2 = sb("gain2", [P, KB])
        rstd_c = sb("rstd_c", [P, TC])
        NARENA = 40084
        arena = sb("arena", [P, NARENA])

        class Area:

            def __init__(self, at=0):
                self.at = at

            def take(self, *shape):
                n = int(np.prod(shape))
                a = arena[:, self.at:self.at + n]
                self.at += n
                assert self.at <= NARENA, self.at
                names = " ".join(f"d{i}" for i in range(len(shape)))
                return a.rearrange(f"p ({names}) -> p {names}",
                                   **{f"d{i}": n for i, n in enumerate(shape)}) if len(shape) > 1 else a

        def vcol(name, *shape):
            o, w = VEC[name]
            a = v[:, o:o + w]
            if not shape:
                return a
            names = " ".join(f"d{i}" for i in range(len(shape)))
            return a.rearrange(f"p ({names}) -> p {names}", **{f"d{i}": n for i, n in enumerate(shape)})

        def kcol(name, *shape):
            o, w = CON[name]
            a = k_[:, o:o + w]
            if not shape:
                return a
            names = " ".join(f"d{i}" for i in range(len(shape)))
            return a.rearrange(f"p ({names}) -> p {names}", **{f"d{i}": n for i, n in enumerate(shape)})

        def spread(a, *shape):
            return a.unsqueeze(len(a.shape)).broadcast_to([P, *shape])

        ident, ones, headones = kcol("ident"), kcol("ones"), kcol("headones")
        level = kcol("level", 2, LEVELS, L)
        strict, incl = kcol("strict", 2, L), kcol("incl", 2, L)
        reset = kcol("reset", 2, GP * L)

        A1 = Area()
        kv = A1.take(9, TT)
        px = A1.take(17, TX)
        kk = A1.take(4, TT)
        y_conv, rT, g_lo = px[:, 0:4], px[:, 12:16], px[:, 16]
        y_dir = [px[:, 4:8], px[:, 8:12]]
        kT, vT, lowT = kv[:, 0:4], kv[:, 4:8], kv[:, 8]
        staged = A1.at
        h = A1.take(KB, TX)
        hc = A1.take(KB, TC)
        ctx_sb = px[:, 0:4].rearrange("p a (b t) -> p (a b) t", b=2)
        kk_sq = Area(staged + 2048 + 512).take(NJ, TT)
        A2 = Area(staged)
        up = A2.take(2, 2, 4, P)
        gup_sb = A2.take(4 * P)

        class Scan:

            def __init__(self):
                self.gate = A2.take(2, GP, L)
                self.cum = A2.take(GP, L)
                self.pin = A2.take(GP, L)
                self.half = A2.take(GP)
                self.decay = A2.take(GP)
                self.kh = A2.take(GP, L)
                self.kt, self.bh, self.rt, self.v_in = (A2.take(GP, L) for _ in range(4))
                self.kt_z, self.bh_z, self.kh_z = (A2.take(GP, 2, L) for _ in range(3))
                self.n, self.ak = A2.take(GH, L), A2.take(GH, L)
                self.rb, self.rk = A2.take(GH, L), A2.take(GH, L)
                self.w, self.X, self.Y = (A2.take(GH, L) for _ in range(3))
                self.bk_tok = A2.take(2, GP, P)
                self.v_tok = A2.take(GP, P)
                self.u = A2.take(GH, HD)
                self.S = A2.take(NG, GP, HD)
                self.S_in = A2.take(GP, HD)
                self.S_bd = A2.take(GP, P)
                self.g = self.u

        scans = [Scan(), Scan()]

        A3 = Area(staged + 6144)
        ys, yc, ysq, yr, rkr, bonus, y_rwkv = (A3.take(4, TX) for _ in range(7))

        act = Area(0).take(FB, TX)
        A4 = Area(staged + KB * TX)
        pad = [A4.take(GRID_H + 2, GRID_W + 2) for _ in range(2)]
        pad1 = [A4.take(TX + 2) for _ in range(2)]
        conv = [A4.take(TX) for _ in range(2)]
        silu = [A4.take(TX) for _ in range(2)]

        A5 = Area(0)
        pr = A5.take(16, TX)
        aq = A5.take(4, TX)
        kz = [A5.take(HC + TX) for _ in range(2)]
        vp = A5.take(HC + TX)
        hreset, cumf = A5.take(NB, NH, HC), A5.take(NB, NH, HC)
        assert A5.at <= staged
        kh, qh = A5.take(NB, NH, HC), A5.take(NB, NH, HC)
        assert A5.at <= staged + KB * TX
        A6 = Area(staged + KB * TX)
        band_sb = A6.take(NB, 2 * HC)
        v_ch, k_ch, sT, S2, qe, ec, ke, k_tok2, v_tok2 = (A6.take(NH, HC) for _ in range(9))
        de = [A6.take(NH * HC) for _ in range(2)]
        zz = [A6.take(NH * HC) for _ in range(2)]
        q_ch = A6.take(NH, HC)
        v_st = A6.take(2, HC)
        vz = A6.take(2, 2, HC)
        pp = A6.take(NQ, 2 * HC)
        pT = A6.take(2 * NQ, HC)
        mix = A6.take(KB, TX)
        lbv, oml = A6.take(4), A6.take(4)
        hi, nm, dsk, den, esk = (A6.take(NQ) for _ in range(5))
        sq2 = Area(0).take(4, TX)
        yr2 = pr[:, 4:8]

        sem("x_in", "ctx_in", "vec_in", "con_in", "lora_in", "slot_in0", "slot_in1")
        sem("product", "taken")
        sem("silu_c", "mod", "squares", "square_sum", "mean_sq", "root", "gain", "normed")
        sem("head_sq", "head_sum", "head_rec", "head_root", "kk_ready", "low_tanh", "conv_ready", "bd_clean")
        sem("y_rkr", "y_rkr_mm", "centred_bonus", "g_sig", "gate_mm", "mixed")
        per_scan = ("z_mm", "z_biased", "z_tanh", "decays", "exps", "keys", "z", "rt", "v_in", "a_mm", "m_mm", "n",
                    "ak", "r_mm", "r_out", "tok_mm", "tok", "X", "Y", "y_mm", "nx_mm", "dx_mm", "w",
                    "gu_mm", "gu", "early_mm", "early", "y_out", "ds_mm", "S", "S_in", "S_bd")
        for d in range(2):
            sem(*(f"{n}{d}" for n in per_scan))
        sem("pads_clean", "gate_in", "conv", "silu", "val_free")
        sem("masks_in", "lb", "forget", "sig", "q_hg", "cum_f", "cum_scan", "f", "keys_hg", "g_silu", "pads2", "S_clean")
        sem("h_in", "h_d", "h_e", "h_z", "h_mm", "h_s", "h_ec", "h_qe", "h_ke", "h_ke_e", "h_kend", "h_v_mm",
            "h_v", "h_k_mm", "h_k", "h_o_mm", "h_o", "h_ds", "h_S")
        sem("a_in", "a_s_mm", "a_nm", "a_ds", "a_p", "a_es", "a_pn", "a_v_mm", "a_v", "a_t_mm", "a_t",
            "a_o_mm", "a_o")
        sem("mix2", "out")
        sem("dve_step", "act_step", "pool_step")

        class Steps:

            def __init__(self, eng, name):
                self.eng, self.sem, self.n, self.per, self.i = eng, s[name], 0, 0, 0

            def do(self, ins):
                ins.then_inc(self.sem, 1)
                self.n += 1

            def last(self):
                self.eng.wait_ge(self.sem, self.n + self.per * self.i)

            def loop(self, i, per):
                self.i, self.per, self.at = i, per, self.n

            def end(self, turns):
                assert self.n - self.at == self.per, (self.n - self.at, self.per)
                self.n = self.at + self.per * turns
                self.per = self.i = 0

        def slot_view(g, blocks=2 * KB):
            return ring[:, g % 2, 0:blocks * P].rearrange("p (k m) -> p k m", m=P)

        def slot_ready(pe, g, i):
            pe.wait_ge(s[f"slot_in{g % 2}"], 16 * (g // 2) + 16 + 16 * i)

        def chunk_at(d, c, isx):
            if d == 0:
                return c * L
            return c * -L + (TT - L + TC if isx else TC - L)

        def places(eng, c, isx):
            at = [chunk_at(d, c, isx) for d in range(2)]
            return at if isinstance(c, int) else [eng.snap(a) for a in at]

        def all_turns(eng, prepare, turn, steps=None, count=0):
            prepare()
            for n in range(NCC + 1):
                turn(n, n // NG, n % NG, n >= NCC, n + 1 >= NCC)
            pairs = (NCX - 2) // 2
            with eng.Fori(0, pairs) as i:
                if steps:
                    steps.loop(i, count)
                turn(2 * i + (NCC + 1), i + NCC // NG, 1, True, True)
                turn(2 * i + (NCC + 2), i + (NCC // NG + 1), 0, True, True)
                if steps:
                    steps.end(pairs)
            turn(NC - 1, NC // NG - 1, 1, True, None)

        def pair_of(h):
            return h // 2, slice(HD * (h % 2), HD * (h % 2) + HD)

        TAKEN_IN = 35
        block = ctx.enter_context(nc.Block())

        @block.sync
        def _(sp):
            def load(g, i, src, at, used):
                if used is not None:
                    sp.wait_ge(s["product"], used)
                if src is w8:
                    to = ring[:, g % 2, :].rearrange("p (c n) -> p c n", c=2)
                    ap = w8[bass.ds(2 * at + 4 * i, 2)].rearrange("c p n -> p c n")
                else:
                    to = ring[:, g % 2, 0:HALF * P]
                    ap = w11[bass.ds(at + 2 * i, 1)].rearrange("c p n -> p (c n)")
                sp.dma_start(to, ap).then_inc(s[f"slot_in{g % 2}"], 16)

            def load_stage(name, src, at, skip=0):
                g = SLOT[name]
                _, n, per = next(st for st in STAGES if st[0] == name)
                for u in range(skip, min(2, n)):
                    load(g + u, 0, src, at + u, DONE[g + u - 2] if g + u >= 2 else None)
                if n > 3:
                    with sp.Fori(1, n // 2) as i:
                        for u in range(2):
                            load(g + u, i, src, at + u, DONE[g + u] - 2 * per + 2 * per * i)
                if n > 2 and n % 2:
                    load(g, n // 2, src, at, DONE[g + n - 3])

            sp.dma_start(v[:, :], vec).then_inc(s["vec_in"], 16)
            load(0, 0, w8, 0, None)
            load(1, 0, w8, 1, None)
            sp.dma_start(k_[:, :], con).then_inc(s["con_in"], 16)
            sp.dma_start(x[:, :, :], xT).then_inc(s["x_in"], 16)
            sp.dma_start(ctx_sb, ctxT).then_inc(s["ctx_in"], 16)
            load_stage("ADA1", w8, 0, skip=2)
            load_stage("W_IN", w8, 8)
            load_stage("W_INB", w8, 16)
            load_stage("W_INC", w8, 17)
            sp.wait_ge(s["product"], DONE[SLOT["ADA2"] - 1])
            sp.dma_start(up.rearrange("p a b c d -> p (a b c d)"), lora).then_inc(s["lora_in"], 16)
            sp.dma_start(gup_sb, gup).then_inc(s["lora_in"], 16)
            load_stage("ADA2", w8, 21)
            load_stage("W_OUT", w8, 37)
            load_stage("UP1", w8, 41)
            load_stage("DOWN1", w11, 0)
            sp.wait_ge(s["normed"], 5 * KB)
            sp.dma_start(band_sb, band).then_inc(s["masks_in"], 16)
            load_stage("W_IN2", w8, 63)
            load_stage("W_OUT2", w8, 74)
            load_stage("UP2", w8, 78)
            load_stage("DOWN2", w11, 16)
            for k in range(0, KB, 2):
                sp.wait_ge(s["normed"], 6 * KB + k + 2)
                sp.dma_start(outT[:, k:k + 2], x[:, k:k + 2, :]).then_inc(s["out"], 16)
            sp.wait_ge(s["out"], 16 * KB // 2)

        @block.tensor
        def _(pe):
            mm = nc.tensor.matmul

            def ada(name, bank, col):
                g = SLOT[name]

                def body(i, u):
                    slot_ready(pe, g + u, i)
                    w = slot_view(g + u)
                    for c in range(2):
                        o = bank[:, bass.ds(col + 2 * (2 * u + c) + 8 * i, 2)]
                        for k in range(KB):
                            last = mm(o, w[:, c * KB + k, :], siluc[:, 2 * k:2 * k + 2], start=k == 0,
                                      stop=k == KB - 1)
                    last.then_inc(s["product"], 1)
                return body

            pe.wait_ge(s["silu_c"], 1)
            in_pairs(pe, 8, ada("ADA1", banks[7], 0))

            norms = [0]

            def sum_squares(sq, bank, t):
                for k in range(KB):
                    pe.wait_ge(s["squares"], norms[0] * KB + k + 1)
                    last = mm(bank[:, 0:t], ones, sq[:, k, :], start=k == 0, stop=k == KB - 1)
                last.then_inc(s["square_sum"], 1)
                norms[0] += 1

            def stage(name, prods, taken, free=None):
                g = SLOT[name]
                n = next(st[1] for st in STAGES if st[0] == name)
                q = len(prods)

                def body(i, u):
                    slot_ready(pe, g + u, i)
                    w = slot_view(g + u)
                    for c, (blk, src, t) in enumerate(prods):
                        if not (isinstance(i, int) and i == 0):
                            if free:
                                pe.wait_ge(s[free[c]], 2 * i + taken + u - 1)
                            else:
                                pe.wait_ge(s["taken"], 2 * q * i + taken + q * u + c + 1 - 2 * q)
                        bank = banks[q * u + c]
                        for k in range(KB):
                            last = mm(bank[:, 0:t], w[:, blk * KB + k, :], src(k), start=k == 0, stop=k == KB - 1)
                        last.then_inc(s["product"], 1)

                if n == 1:
                    body(0, 0)
                else:
                    in_pairs(pe, n, body, peel=True)

            def blocks(a):
                return lambda k: a[:, k, :]

            def down(name, taken):
                g = SLOT[name]
                with pe.Fori(0, KB // 2) as i:
                    for m in range(2):
                        pe.wait_ge(s["taken"], taken + 2 * i + m - 1)
                        for half in range(2):
                            slot_ready(pe, g + 2 * m + half, 2 * i)
                            w = slot_view(g + half, HALF)
                            for k in range(HALF):
                                last = mm(banks[m][:, :], w[:, k, :], act[:, HALF * half + k, :],
                                          start=half == 0 and k == 0, stop=half == 1 and k == HALF - 1)
                            last.then_inc(s["product"], 1)

            pe.wait_ge(s["con_in"], 16)
            sum_squares(hc, banks[0], TC)
            sum_squares(h, banks[1], TX)
            pe.wait_ge(s["normed"], 2 * KB)
            hb, hcb = blocks(h), blocks(hc)
            stage("W_IN", [(0, hb, TX), (1, hb, TX)], 0)
            pe.wait_ge(s["taken"], 16)
            stage("W_INB", [(0, hb, TX), (1, hb, TX), (1, hcb, TC)], 16)
            pe.wait_ge(s["taken"], 19)
            stage("W_INC", [(0, hb, TX), (0, hcb, TC), (1, hb, TX), (1, hcb, TC)], 19)

            pe.wait_ge(s["taken"], TAKEN_IN)
            for j in range(NJ):
                pe.wait_ge(s["head_sq"], j + 1)
                mm(banks[2 * j][:, 0:TX], headones, kk_sq[:, j, TC:TT], start=True, stop=True)
                mm(banks[2 * j + 1][:, 0:TC], headones, kk_sq[:, j, 0:TC], start=True,
                   stop=True).then_inc(s["head_sum"], 1)

            bank = [banks[0:4], banks[4:8]]

            def heads(b):
                return b[:, :].rearrange("p (h t) -> p h t", h=GH)

            def each(d, out, lhs, rhs, name=None):
                for h in range(GH):
                    last = mm(out[:, h, :], lhs(h), rhs(h), start=True, stop=True)
                if name:
                    last.then_inc(s[f"{name}{d}"], 1)

            def of_head(a):
                return (lambda h: a[:, h // 2, h % 2, :]) if len(a.shape) == 4 else (lambda h: a[:, h, :])

            def of_pair(a):
                return lambda h: a[:, h // 2, :]

            def done(name, d, n, per=1, at=0):
                pe.wait_ge(s[f"{name}{d}"], per * n + (at or per))

            def in_x(name, d, n, per=1, at=0):
                pe.wait_ge(s[f"{name}{d}"], per * (n - NCC) + (at or per))

            def gates_in(n, g, ats):
                for d in range(2):
                    if not (isinstance(n, int) and n == 0):
                        done("ak", d, n - 1)
                    z = heads(bank[d][0])
                    for q in range(2 * GP):
                        last = mm(z[:, q, :], up[:, d, q // GP, GP * g + q % GP, :], lowT[:, bass.ds(ats[d], L)],
                                  start=True, stop=True)
                    last.then_inc(s[f"z_mm{d}"], 1)

            def score(n, d):
                sc = scans[d]
                done("z", d, n, 3, 1)
                done("keys", d, n, 3, 2)
                each(d, heads(bank[d][3]), of_head(sc.kt_z), of_pair(sc.bh), "a_mm")

            def score_t(n, d):
                sc = scans[d]
                done("z", d, n, 3, 2)
                each(d, heads(bank[d][1]), of_head(sc.bh_z), of_pair(sc.kt), "m_mm")

            def score_k(n, d):
                done("z", d, n, 3)
                done("z_biased", d, n)
                each(d, heads(bank[d][0]), of_head(scans[d].kh_z), of_pair(scans[d].kt), "m_mm")

            def score_r(n, d, k):
                sc = scans[d]
                if k == 0:
                    in_x("rt", d, n)
                else:
                    in_x("r_out", d, n, 2, 1)
                each(d, heads(bank[d][2]), of_head((sc.bh_z, sc.kh_z)[k]), of_pair(sc.rt), "r_mm")

            def turned(n, d, isx):
                sc = scans[d]
                if isx:
                    in_x("r_out", d, n, 2)
                elif not (isinstance(n, int) and n == 0):
                    done("S", d, n - 1)
                    pe.wait_ge(s["mod"], 1 + n)
                for k, src in enumerate((sc.bh, sc.kh)):
                    for j in range(GP):
                        last = nc.tensor.transpose(heads(bank[d][2])[:, GP * k + j, :], src[:, j, :], ident)
                last.then_inc(s[f"tok_mm{d}"], 1)

            def turned_v(n, d):
                done("tok", d, n, 2, 1)
                done("v_in", d, n)
                for j in range(GP):
                    last = nc.tensor.transpose(heads(bank[d][2])[:, j, :], scans[d].v_in[:, j, :], ident)
                last.then_inc(s[f"tok_mm{d}"], 1)

            def state_in(n, d, nxt):
                sc = scans[d]
                done("tok", d, n, 2)
                done("ak", d, n)
                done("S_in", d, n)
                if nxt is not None:
                    done("z_biased", d, n + 1)
                out = bank[d][0][:, 0:GH * HD].rearrange("p (h f) -> p h f", h=GH)
                for h in range(GH):
                    j, r = pair_of(h)
                    mm(out[:, h, :], sc.kt_z[:, j, h % 2, :], sc.S_in[:, j, :], start=True, stop=False)
                    last = mm(out[:, h, :], sc.ak[:, h, :], sc.v_tok[:, j, r], start=False, stop=True)
                last.then_inc(s[f"gu_mm{d}"], 1)

            def early_out(n, d):
                sc = scans[d]
                done("tok", d, n, 2)
                in_x("S_bd", d, n)
                for j in range(GP):
                    y = heads(bank[d][2])[:, j, :]
                    mm(y, sc.S_bd[:, j, :], sc.rt[:, j, :], start=True, stop=False)
                    for q in range(2):
                        r = slice(HD * q, HD * q + HD)
                        last = mm(y[r], sc.v_tok[:, j, r], sc.rk[:, 2 * j + q, :], start=False, stop=True)
                last.then_inc(s[f"early_mm{d}"], 1)

            def nx(n, d, l):
                done("X", d, n, LEVELS, l - 1)
                if l == 2:
                    done("n", d, n)
                each(d, heads(bank[d][3]), of_head(scans[d].n), of_head(scans[d].X), "nx_mm")

            def dx(n, d, l):
                done("w", d, n, LEVELS - 1, l - 1)
                done("Y", d, n, LEVELS, l - 1)
                each(d, heads(bank[d][3]), of_head(scans[d].Y), of_head(scans[d].w), "dx_mm")

            def turn_x(n, d, l):
                done("X", d, n, LEVELS, l)
                if l == 1:
                    done("n", d, n)
                for h in range(GH):
                    last = nc.tensor.transpose(heads(bank[d][1])[:, h, :], scans[d].X[:, h, :], ident)
                last.then_inc(s[f"y_mm{d}"], 1)

            def updates(n, d):
                sc = scans[d]
                done("Y", d, n, LEVELS)
                done("gu", d, n, 2, 1)
                each(d, bank[d][0][:, 0:GH * HD].rearrange("p (h f) -> p h f", h=GH), of_head(sc.Y),
                     of_head(sc.g), "gu_mm")

            def results(n, d, cur, nxt):
                sc = scans[d]
                done("gu", d, n, 2)
                if cur:
                    in_x("early", d, n)
                    for h in range(GH):
                        j, r = pair_of(h)
                        last = mm(heads(bank[d][2])[r, j, :], sc.u[:, h, :], sc.rb[:, h, :], start=True, stop=True)
                else:
                    done("tok", d, n, 2)
                if nxt is not None:
                    ds = bank[d][2][:, 256:256 + GP * HD].rearrange("p (j f) -> p j f", j=GP)
                    for h in range(GH):
                        j, r = pair_of(h)
                        mm(ds[r, j, :], sc.bk_tok[:, 0, j, r], sc.u[:, h, :], start=True, stop=False)
                        last = mm(ds[r, j, :], sc.bk_tok[:, 1, j, r], sc.v_tok[:, j, r], start=False, stop=True)
                last.then_inc(s[f"ds_mm{d}"], 1)

            def ada_terms(n):
                done("S", 0, n)
                g = SLOT["ADA2"]
                for u in range(4):
                    slot_ready(pe, g + u, 2 * n)
                    w = slot_view(g + u)
                    for c in range(2):
                        o = bank[0][2][:, 2 * (2 * u + c):2 * (2 * u + c) + 2]
                        for k in range(KB):
                            last = mm(o, w[:, c * KB + k, :], siluc[:, 2 * k:2 * k + 2], start=k == 0,
                                      stop=k == KB - 1)
                    last.then_inc(s["product"], 1)

            def prepare():
                gates_in(0, 0, places(pe, 0, False))
                for d in range(2):
                    score(0, d)
                    score_t(0, d)
                for d in range(2):
                    score_k(0, d)

            def turn(n, c, g, cur, nxt):
                ats = places(pe, c + g, nxt)
                turn_x(n, 0, 1)
                for l in range(2, LEVELS + 1):
                    nx(n, 0, l)
                    turn_x(n, 1, l - 1)
                    if l == 2 and nxt is not None:
                        gates_in(n + 1, 1 - g, ats)
                    for d in range(2):
                        if l == 2:
                            turned(n, d, cur)
                        elif l == 3:
                            turned_v(n, d)
                        elif l == 4:
                            state_in(n, d, nxt)
                        elif l == 5 and cur:
                            early_out(n, d)
                    dx(n, 0, l)
                    nx(n, 1, l)
                    turn_x(n, 0, l)
                    dx(n, 1, l)
                if nxt is not None:
                    score(n + 1, 0)
                turn_x(n, 1, LEVELS)
                updates(n, 0)
                if nxt is not None:
                    score_t(n + 1, 0)
                    score(n + 1, 1)
                updates(n, 1)
                if nxt is not None:
                    score_t(n + 1, 1)
                for d in range(2):
                    results(n, d, cur, nxt)
                    if nxt is not None:
                        score_k(n + 1, d)
                if not cur:
                    ada_terms(n)
                if nxt:
                    for k in range(2):
                        for d in range(2):
                            if k == 0:
                                done("S", d, n)
                                if not cur:
                                    pe.wait_ge(s["mod"], 1 + NCC)
                            score_r(n + 1, d, k)

            pe.wait_ge(s["kk_ready"], NJ)
            pe.wait_ge(s["lora_in"], 32)
            pe.wait_ge(s["low_tanh"], 1)
            pe.wait_ge(s["bd_clean"], 2)
            all_turns(pe, prepare, turn)

            for j in range(NJ):
                pe.wait_ge(s["y_rkr"], 2 * j + 1)
                mm(banks[j][:, :], headones, ys[:, j, :], start=True, stop=True).then_inc(s["y_rkr_mm"], 1)
                pe.wait_ge(s["y_rkr"], 2 * j + 2)
                mm(banks[4 + j][:, :], headones, rkr[:, j, :], start=True, stop=True).then_inc(s["y_rkr_mm"], 1)
            for j in range(NJ):
                pe.wait_ge(s["head_sq"], NJ + j + 1)
                mm(banks[j][:, :], headones, ysq[:, j, :], start=True, stop=True).then_inc(s["head_sum"], 1)
            pe.wait_ge(s["g_sig"], 1)
            for j in range(NJ):
                pe.wait_ge(s["centred_bonus"], 2 * j + 2)
                mm(banks[4 + j][:, :], gup_sb[:, j * P:(j + 1) * P], g_lo, start=True,
                   stop=True).then_inc(s["gate_mm"], 1)
            pe.wait_ge(s["mixed"], NJ)
            stage("W_OUT", [(c, lambda k: y_conv[:, k, :] if k < 4 else y_rwkv[:, k - 4, :], TX) for c in range(2)],
                  35)
            sum_squares(h, banks[6], TX)
            pe.wait_ge(s["normed"], 3 * KB)
            stage("UP1", [(0, hb, TX), (1, hb, TX)], 0, free=("gate_in", "val_free"))
            pe.wait_ge(s["val_free"], FB)
            down("DOWN1", 43)
            sum_squares(h, banks[6], TX)

            sum_squares(h, banks[7], TX)
            pe.wait_ge(s["normed"], 5 * KB)
            stage("W_IN2", [(0, hb, TX), (1, hb, TX)], 51)
            pe.wait_ge(s["taken"], 51 + 22)

            def mixer2(i):
                first = isinstance(i, int) and i == 0

                def heads(b):
                    return b[:, :].rearrange("p (h t) -> p h t", h=NH)

                pe.wait_ge(s["a_in"], 2 * i + 1)
                if not first:
                    pe.wait_ge(s["a_o"], i)
                for j in range(4):
                    for g in range(2):
                        last = mm(banks[4 + j][:, 256 * g:256 * g + 256], q_ch[:, j, :],
                                  kz[g][:, bass.ds(HC * i, 2 * HC)], start=True, stop=True)
                last.then_inc(s["a_s_mm"], 1)
                pe.wait_ge(s["h_in"], 2 * i + 2)
                if not first:
                    pe.wait_ge(s["h_k"], i)
                for hd in range(NH):
                    last = nc.tensor.transpose(heads(banks[2])[:, hd, :], v_ch[:, hd, :], ident)
                last.then_inc(s["h_v_mm"], 1)
                for l in range(1, HLEV + 2):
                    b = banks[l % 2]
                    if not first or l > 2:
                        pe.wait_ge(s["h_s"], 8 * i + l - 2)
                    if l <= HLEV:
                        pe.wait_ge(s["h_z"], 2 * HLEV * i + 2 * l)
                    for hd in range(NH):
                        zl = zz[l % 2].rearrange("p (h t) -> p h t", h=NH)
                        if l <= HLEV:
                            last = mm(heads(b)[:, hd, :], zl[:, hd, :], zl[:, hd, :], start=True, stop=True)
                        else:
                            last = mm(heads(b)[:, hd, :], k_ch[:, hd, :], q2d(i, hd), start=True, stop=True)
                    last.then_inc(s["h_mm"], 1)
                pe.wait_ge(s["h_kend"], i + 1)
                pe.wait_ge(s["h_v"], i + 1)
                for hd in range(NH):
                    last = nc.tensor.transpose(heads(banks[2])[:, hd, :], ke[:, hd, :], ident)
                last.then_inc(s["h_k_mm"], 1)
                pe.wait_ge(s["h_s"], 8 * i + 8)
                pe.wait_ge(s["h_qe"], i + 1)
                if not first:
                    pe.wait_ge(s["h_S"], i)
                for hd in range(NH):
                    mm(heads(banks[3])[:, hd, :], v_tok2[:, hd, :], sT[:, hd, :], start=True, stop=False)
                    last = mm(heads(banks[3])[:, hd, :], S2[:, hd, :], qe[:, hd, :], start=False, stop=True)
                last.then_inc(s["h_o_mm"], 1)
                pe.wait_ge(s["a_pn"], i + 1)
                for b in range(4):
                    for c in range(4):
                        last = nc.tensor.transpose(heads(banks[4 + b])[:, c, :],
                                                   pp[:, 2 * b + c // 2, HC * (c % 2):HC * (c % 2) + HC], ident)
                    last.then_inc(s["a_t_mm"], 1)
                pe.wait_ge(s["h_k"], i + 1)
                pe.wait_ge(s["h_o"], i + 1)
                for hd in range(NH):
                    last = mm(heads(banks[3])[:, hd, :], k_tok2[:, hd, :], v_tok2[:, hd, :], start=True, stop=True)
                last.then_inc(s["h_ds"], 1)
                pe.wait_ge(s["a_in"], 2 * i + 2)
                pe.wait_ge(s["a_t"], 4 * i + 4)
                for c in range(2):
                    last = nc.tensor.transpose(banks[4][:, HC * c:HC * c + HC], v_st[:, c, :], ident)
                last.then_inc(s["a_v_mm"], 1)
                pe.wait_ge(s["a_v"], 2 * i + 2)
                for j in range(4):
                    for n, (g, c) in enumerate(((0, 0), (0, 1), (1, 0), (1, 1))):
                        last = mm(heads(banks[5])[:, j, :], vz[:, g, c, :], pT[:, 4 * j + 2 * g + c, :],
                                  start=n == 0, stop=n == 3)
                last.then_inc(s["a_o_mm"], 1)

            def q2d(i, hd):
                return qh.rearrange("p n h t -> p (n h t)")[:, bass.ds(NH * HC * i + HC * hd, HC)]

            pe.wait_ge(s["q_hg"], NH)
            pe.wait_ge(s["S_clean"], 1)
            pe.wait_ge(s["pads2"], 4)
            mixer2(0)
            with pe.Fori(1, NB) as i:
                mixer2(i)
            pe.wait_ge(s["h_S"], NB)
            for hd in range(NH):
                pe.wait_ge(s["head_sq"], 2 * NJ + hd + 1)
                mm(banks[hd][:, :], ones, sq2[:, hd, :], start=True, stop=True).then_inc(s["head_sum"], 1)
            pe.wait_ge(s["mix2"], NH)
            pe.wait_ge(s["a_o"], NB)
            stage("W_OUT2", [(c, blocks(mix), TX) for c in range(2)], 73)
            sum_squares(h, banks[6], TX)

            pe.wait_ge(s["normed"], 6 * KB)
            stage("UP2", [(0, hb, TX), (1, hb, TX)], FB, free=("gate_in", "val_free"))
            pe.wait_ge(s["val_free"], 2 * FB)
            down("DOWN2", 81)
            sum_squares(h, banks[6], TX)

        @block.scalar
        def _(se):
            act_f = nc.scalar.activation
            steps = Steps(se, "act_step")
            se.wait_ge(s["vec_in"], 16)
            act_f(siluc[:, :], vcol("cs"), ACT.Silu).then_inc(s["silu_c"], 1)

            def squares(src, to, after=None):
                for k in range(KB):
                    if after:
                        se.wait_ge(s[after[0]], after[1] + k + 1)
                    act_f(to[:, k, :], src[:, k, :], ACT.Square).then_inc(s["squares"], 1)

            roots = [0]

            def root(r):
                roots[0] += 1
                se.wait_ge(s["mean_sq"], roots[0])
                act_f(r, r, ACT.Sqrt).then_inc(s["root"], 1)

            se.wait_ge(s["ctx_in"], 16)
            squares(ctx_sb, hc)
            se.wait_ge(s["x_in"], 16)
            squares(x, h)
            root(rstd_c[:, :])
            root(rstd[:, :])

            def take(to, bank, product, **kw):
                se.wait_ge(s["product"], product)
                act_f(to, bank, ACT.Copy, **kw).then_inc(s["taken"], 1)

            p_in = DONE[SLOT["W_IN"] - 1]

            def take_x(i, u):
                for c in range(2):
                    m = 4 * i + 2 * u + c
                    take(px[:, m, :] if isinstance(i, int) else px[:, bass.ds(m, 1), :], banks[2 * u + c][:, :],
                         p_in + 4 * i + 2 * u + c + 1)

            in_pairs(se, 8, take_x)
            take(px[:, 16, :], banks[0][:, :], p_in + 17)
            take(kv[:, 0, TC:TT], banks[1][:, :], p_in + 18)
            take(kv[:, 0, 0:TC], banks[2][:, 0:TC], p_in + 19)

            def take_xc(i, u):
                for c in range(4):
                    m = 1 + 4 * i + 2 * u + c // 2
                    to = kv[:, bass.ds(m, 1), TC:TT] if c % 2 == 0 else kv[:, bass.ds(m, 1), 0:TC]
                    take(to, banks[4 * u + c][:, 0:TX if c % 2 == 0 else TC], p_in + 20 + 8 * i + 4 * u + c)

            in_pairs(se, 4, take_xc)

            se.wait_ge(s["taken"], TAKEN_IN)
            for j in range(NJ):
                act_f(kk_sq[:, j, :], kT[:, j, :], ACT.Square, scale=vcol("kk")[:, j:j + 1]).then_inc(s["head_sq"], 1)
            act_f(lowT[0:64, :], lowT[0:64, :], ACT.Tanh).then_inc(s["low_tanh"], 1)
            for j in range(NJ):
                se.wait_ge(s["head_rec"], j + 1)
                act_f(kk[:, j, :], kk[:, j, :], ACT.Sqrt).then_inc(s["head_root"], 1)

            bank = [banks[0:4], banks[4:8]]

            def heads(b):
                return b[:, :].rearrange("p (h t) -> p h t", h=GH)

            def done(name, d, n, per=1, at=0):
                se.wait_ge(s[f"{name}{d}"], per * n + (at or per))

            def copy(to, src, name, d, scale=1.0):
                act_f(to, src, ACT.Copy, scale=scale).then_inc(s[f"{name}{d}"], 1)

            def gate_tanh(n):
                for d, sc in enumerate(scans):
                    done("z_biased", d, n)
                    act_f(sc.gate, sc.gate, ACT.Tanh, scale=0.5).then_inc(s[f"z_tanh{d}"], 1)

            def decay_exps(n):
                for d, sc in enumerate(scans):
                    done("decays", d, n)
                    act_f(sc.gate[:, 0], sc.gate[:, 0], ACT.Exp).then_inc(s[f"exps{d}"], 1)
                    act_f(sc.pin, sc.cum, ACT.Exp).then_inc(s[f"exps{d}"], 1)
                    done("exps", d, n, 3, 2)
                    act_f(sc.cum, sc.cum, ACT.Exp, scale=-1.0).then_inc(s[f"exps{d}"], 1)

            def scores_out(n, d):
                done("m_mm", d, n, 2, 1)
                copy(scans[d].n, heads(bank[d][1]), "n", d, -1.0)

            def x_turned(n, d, l):
                done("y_mm", d, n, LEVELS, l)
                copy(scans[d].Y, heads(bank[d][1]), "Y", d)

            def values_in(n, g, at):
                for d, sc in enumerate(scans):
                    if not (isinstance(n, int) and n == 0):
                        done("tok_mm", d, n - 1, 2)
                    copy(sc.v_in, vT[:, GP * g:GP * g + GP, bass.ds(at[d], L)], "v_in", d)

            def tok_out(n, d, k):
                sc = scans[d]
                done("tok_mm", d, n, 2, k + 1)
                if k == 0:
                    copy(sc.bk_tok.rearrange("p a j f -> p (a j) f"), heads(bank[d][2]), "tok", d)
                else:
                    copy(sc.v_tok, heads(bank[d][2])[:, 0:GP, :], "tok", d)

            def u_view(d):
                return bank[d][0][:, 0:GH * HD].rearrange("p (h f) -> p h f", h=GH)

            def prepare():
                values_in(0, 0, places(se, 0, False))
                gate_tanh(0)
                decay_exps(0)
                for d in range(2):
                    scores_out(0, d)

            def turn(n, c, g, cur, nxt):
                at = places(se, c, cur)
                at_next = places(se, c + g, nxt)
                x_turned(n, 0, 1)
                for l in range(2, LEVELS + 1):
                    x_turned(n, 1, l - 1)
                    for d, sc in enumerate(scans):
                        if l == 2:
                            tok_out(n, d, 0)
                        elif l == 3:
                            tok_out(n, d, 1)
                        elif l == 4:
                            done("gu_mm", d, n, 2, 1)
                            copy(sc.g, u_view(d), "gu", d, -1.0)
                        elif l == 5 and cur:
                            se.wait_ge(s[f"early_mm{d}"], n - NCC + 1)
                            copy(y_dir[d][:, GP * g:GP * g + GP, bass.ds(at[d] - TC, L)],
                                 heads(bank[d][2])[:, 0:GP, :], "early", d)
                    if nxt is not None:
                        if l == 2:
                            gate_tanh(n + 1)
                        elif l == 5:
                            decay_exps(n + 1)
                        elif l == 6:
                            values_in(n + 1, 1 - g, at_next)
                    x_turned(n, 0, l)
                x_turned(n, 1, LEVELS)
                for d, sc in enumerate(scans):
                    done("gu_mm", d, n, 2)
                    copy(sc.u, u_view(d), "gu", d)
                    if nxt is not None:
                        scores_out(n + 1, d)

            se.wait_ge(s["bd_clean"], 2)
            all_turns(se, prepare, turn)

            for d in range(2):
                se.wait_ge(s[f"y_out{d}"], NCX)
            act_f(g_lo, g_lo, ACT.Sigmoid).then_inc(s["g_sig"], 1)
            for j in range(NJ):
                se.wait_ge(s["centred_bonus"], 2 * j + 1)
                act_f(ysq[:, j, :], yc[:, j, :], ACT.Square).then_inc(s["head_sq"], 1)
            for j in range(NJ):
                se.wait_ge(s["head_rec"], NJ + j + 1)
                act_f(yr[:, j, :], yr[:, j, :], ACT.Sqrt).then_inc(s["head_root"], 1)
            squares(x, h, ("taken", 35))
            root(rstd[:, :])

            def ffn(first, p0, name):
                def body(i, u):
                    if not (isinstance(i, int) and i == 0 and first == 0):
                        se.wait_ge(s["conv"], first + 2 * i + u - 1)
                    se.wait_ge(s["product"], p0 + 4 * i + 2 * u + 1)
                    if name == 1:
                        act_f(pad[u][:, 1:1 + GRID_H, 1:1 + GRID_W],
                              banks[2 * u][:, :].rearrange("p (y x) -> p y x", y=GRID_H),
                              ACT.Copy).then_inc(s["gate_in"], 1)
                    else:
                        act_f(pad1[u][:, 2:2 + TX], banks[2 * u][:, :], ACT.Copy).then_inc(s["gate_in"], 1)
                    se.wait_ge(s["conv"], first + 2 * i + u + 1)
                    if not (isinstance(i, int) and i == 0):
                        se.wait_ge(s["val_free"], first + 2 * i + u - 1)
                    act_f(silu[u], conv[u], ACT.Silu).then_inc(s["silu"], 1)

                se.wait_ge(s["pads_clean"], 2 * name)
                in_pairs(se, FB, body, peel=True)

            ffn(0, DONE[SLOT["UP1"] - 1], 1)
            squares(x, h, ("taken", 43))
            root(rstd[:, :])

            squares(x, h, ("normed", 3 * KB))
            root(rstd[:, :])
            se.wait_ge(s["lb"], 1)
            act_f(lbv, lbv, ACT.Sigmoid).then_inc(s["sig"], 1)
            p_in2 = DONE[SLOT["W_IN2"] - 1]

            def take2(i, u):
                for c in range(2):
                    m = 4 * i + 2 * u + c
                    take(pr[:, m, :] if isinstance(i, int) else pr[:, bass.ds(m, 1), :], banks[2 * u + c][:, :],
                         p_in2 + 4 * i + 2 * u + c + 1)

            in_pairs(se, 8, take2)
            bias = vcol("batt")
            for j in range(4):
                se.wait_ge(s["product"], p_in2 + 17 + j)
                act_f(aq[:, j, :], banks[j][:, :], ACT.Identity, bias=bias[:, j:j + 1]).then_inc(s["taken"], 1)
            se.wait_ge(s["pads2"], 4)
            se.wait_ge(s["product"], p_in2 + 21)
            act_f(kz[0][0:64, HC:], banks[0][0:64, :], ACT.Identity, bias=bias[0:64, 4:5]).then_inc(s["act_step"], 1)
            act_f(kz[1][64:128, HC:], banks[0][64:128, :], ACT.Identity,
                  bias=bias[64:128, 4:5]).then_inc(s["taken"], 1)
            se.wait_ge(s["product"], p_in2 + 22)
            act_f(vp[:, HC:], banks[1][:, :], ACT.Identity, bias=bias[:, 5:6]).then_inc(s["taken"], 1)
            for hd in range(NH):
                act_f(pr[:, 4 + hd, :], pr[:, 4 + hd, :], ACT.Sigmoid).then_inc(s["forget"], 1)
            for hd in range(NH):
                act_f(pr[:, 12 + hd, :], pr[:, 12 + hd, :], ACT.Silu).then_inc(s["g_silu"], 1)
            for hd in range(NH):
                se.wait_ge(s["keys_hg"], hd + 1)
                act_f(cumf[:, :, hd, :], cumf[:, :, hd, :], ACT.Ln).then_inc(s["cum_f"], 1)

            def mixer2(i):
                first = isinstance(i, int) and i == 0
                chunk = bass.ds(NH * HC * i, NH * HC)
                cf = cumf.rearrange("p n h t -> p (n h t)")[:, chunk]

                def heads(b):
                    return b[:, :].rearrange("p (h t) -> p h t", h=NH)

                if not first:
                    se.wait_ge(s["h_S"], i)
                act_f(ec.rearrange("p h t -> p (h t)"), cf, ACT.Exp).then_inc(s["h_ec"], 1)
                se.wait_ge(s["h_v_mm"], i + 1)
                act_f(v_tok2, heads(banks[2]), ACT.Copy).then_inc(s["h_v"], 1)

                def level(l):
                    se.wait_ge(s["h_d"], 2 * HLEV * i + 2 * l)
                    act_f(de[l % 2], de[l % 2], ACT.Exp).then_inc(s["h_e"], 1)

                level(1)
                level(2)
                se.wait_ge(s["a_ds"], i + 1)
                for q in range(NQ):
                    act_f(pp[:, q, :], pp[:, q, :], ACT.Exp, bias=nm[:, q:q + 1],
                          accum_out=den[:, q:q + 1]).then_inc(s["a_p"], 1)
                act_f(esk, dsk, ACT.Exp).then_inc(s["a_es"], 1)
                for l in range(3, HLEV + 1):
                    level(l)
                se.wait_ge(s["h_ke"], i + 1)
                act_f(ke, ke, ACT.Exp).then_inc(s["h_ke_e"], 1)
                se.wait_ge(s["h_k_mm"], i + 1)
                act_f(k_tok2, heads(banks[2]), ACT.Copy).then_inc(s["h_k"], 1)
                se.wait_ge(s["h_o_mm"], i + 1)
                act_f(mix[:, 0:4, bass.ds(HC * i, HC)], heads(banks[3]), ACT.Copy).then_inc(s["h_o"], 1)
                for b in range(4):
                    se.wait_ge(s["a_t_mm"], 4 * i + b + 1)
                    act_f(pT[:, 4 * b:4 * b + 4, :], heads(banks[4 + b]), ACT.Copy).then_inc(s["a_t"], 1)
                se.wait_ge(s["a_v_mm"], i + 1)
                for g in range(2):
                    act_f(vz[:, g, :, 64 * g:64 * g + 64],
                          banks[4][:, 0:2 * HC].rearrange("p (c f) -> p c f", c=2)[:, :, 64 * g:64 * g + 64],
                          ACT.Copy).then_inc(s["a_v"], 1)
                se.wait_ge(s["a_o_mm"], i + 1)
                act_f(mix[:, 4:8, bass.ds(HC * i, HC)], heads(banks[5]), ACT.Copy).then_inc(s["a_o"], 1)

            se.wait_ge(s["cum_scan"], 1)
            mixer2(0)
            with se.Fori(1, NB) as i:
                mixer2(i)
            se.wait_ge(s["h_o"], NB)
            for hd in range(NH):
                act_f(sq2[:, hd, :], mix[:, hd, :], ACT.Square).then_inc(s["head_sq"], 1)
            for hd in range(NH):
                se.wait_ge(s["head_rec"], 2 * NJ + hd + 1)
                act_f(yr2[:, hd, :], yr2[:, hd, :], ACT.Sqrt).then_inc(s["head_root"], 1)
            squares(x, h, ("taken", 73))
            root(rstd[:, :])
            ffn(FB, DONE[SLOT["UP2"] - 1], 2)
            squares(x, h, ("taken", 81))
            root(rstd[:, :])

        @block.gpsimd
        def _(pool):
            pool.wait_ge(s["head_sum"], NJ)
            for sc in scans:
                nc.gpsimd.memset(sc.S, 0.0).then_inc(s["bd_clean"], 1)

            def done(name, d, n, per=1, at=0):
                pool.wait_ge(s[f"{name}{d}"], per * n + (at or per))

            def apart(to, src, name, w):
                nc.gpsimd.tensor_tensor(to, src.unsqueeze(2).broadcast_to([P, GP, 2, w]),
                                        headones[:, ::HD].unsqueeze(1).unsqueeze(3).broadcast_to([P, GP, 2, w]),
                                        ALU.mult).then_inc(s[name], 1)

            def heads_apart(n):
                for k in range(3):
                    for d, sc in enumerate(scans):
                        done("keys", d, n, 3, k + 1)
                        if k == 0 and not (isinstance(n, int) and n == 0):
                            done("gu_mm", d, n - 1, 2, 1)
                        a, b = ((sc.kt_z, sc.kt), (sc.bh_z, sc.bh), (sc.kh_z, sc.kh))[k]
                        apart(a, b, f"z{d}", L)

            def prepare():
                heads_apart(0)

            def turn(n, c, g, cur, nxt):
                if nxt is not None:
                    heads_apart(n + 1)
                if nxt:
                    for d, sc in enumerate(scans):
                        done("S_in", d, n + 1)
                        if cur:
                            pool.wait_ge(s[f"early_mm{d}"], n - NCC + 1)
                        apart(sc.S_bd.rearrange("p j (q f) -> p j q f", q=2), sc.S_in, f"S_bd{d}", HD)

            all_turns(pool, prepare, turn)
            pool.wait_ge(s["mixed"], NJ)
            for a in pad:
                nc.gpsimd.memset(a, 0.0).then_inc(s["pads_clean"], 1)
            pool.wait_ge(s["taken"], 51)
            nc.gpsimd.memset(hreset, 1.0).then_inc(s["pool_step"], 1)
            pool.wait_ge(s["pool_step"], 1)
            nc.gpsimd.memset(hreset[:, :, :, 0:1], 0.0).then_inc(s["pads2"], 1)
            for a in (kz[0], kz[1], vp[:, 0:HC]):
                nc.gpsimd.memset(a, 0.0).then_inc(s["pads2"], 1)
            nc.gpsimd.memset(vz, 0.0).then_inc(s["pads2"], 1)
            nc.gpsimd.memset(S2, 0.0).then_inc(s["S_clean"], 1)

            def mixer2(i):
                first = isinstance(i, int) and i == 0
                if not first:
                    pool.wait_ge(s["a_s_mm"], i)
                nc.gpsimd.tensor_copy(q_ch, aq[:, :, bass.ds(HC * i, HC)]).then_inc(s["a_in"], 1)
                if not first:
                    pool.wait_ge(s["h_mm"], 8 * i)
                    pool.wait_ge(s["h_v_mm"], i)
                nc.gpsimd.tensor_copy(v_ch, pr[:, 8:12, bass.ds(HC * i, HC)]).then_inc(s["h_in"], 1)
                nc.gpsimd.tensor_copy(k_ch.rearrange("p h t -> p (h t)"),
                                      kh.rearrange("p n h t -> p (n h t)")[:, bass.ds(NH * HC * i, NH * HC)]
                                      ).then_inc(s["h_in"], 1)
                if not first:
                    pool.wait_ge(s["a_v_mm"], i)
                nc.gpsimd.tensor_copy(v_st.rearrange("p c t -> p (c t)"),
                                      vp[:, bass.ds(HC * i, 2 * HC)]).then_inc(s["a_in"], 1)

            pool.wait_ge(s["taken"], 73)
            pool.wait_ge(s["keys_hg"], NH)
            mixer2(0)
            with pool.Fori(1, NB) as i:
                mixer2(i)
            pool.wait_ge(s["mix2"], NH)
            pool.wait_ge(s["a_o"], NB)
            for a in pad1:
                nc.gpsimd.memset(a[:, 0:2], 0.0).then_inc(s["pads_clean"], 1)

        @block.vector
        def _(dve):
            V = nc.vector
            steps = Steps(dve, "dve_step")
            norms = [0]

            def mean_square(r, bank, t):
                norms[0] += 1
                dve.wait_ge(s["square_sum"], norms[0])
                steps.do(V.tensor_scalar(r, bank[:, 0:t], 1.0 / D, EPS, ALU.mult, ALU.add))
                steps.last()
                V.reciprocal(r, r).then_inc(s["mean_sq"], 1)

            def norm(to, src, r, gain, shift=None):
                dve.wait_ge(s["root"], norms_done[0] + 1)
                norms_done[0] += 1
                for k in range(KB):
                    ins = V.scalar_tensor_tensor(to[:, k, :], src[:, k, :], gain[:, k:k + 1], r, ALU.mult, ALU.mult)
                    if shift is None:
                        ins.then_inc(s["normed"], 1)
                    else:
                        steps.do(ins)
                if shift is not None:
                    steps.last()
                    for k in range(KB):
                        V.tensor_scalar(to[:, k, :], to[:, k, :], shift[:, k:k + 1], None,
                                        ALU.add).then_inc(s["normed"], 1)

            norms_done = [0]
            dve.wait_ge(s["vec_in"], 16)
            mean_square(rstd_c[:, :], banks[0], TC)
            mean_square(rstd[:, :], banks[1], TX)
            dve.wait_ge(s["product"], DONE[SLOT["W_IN"] - 1])
            V.tensor_tensor(mod[:, 0:16, :], banks[7][:, 0:32].rearrange("p (m c) -> p m c", c=2),
                            spread(vcol("adab")[:, 0:16], 16, 2), ALU.add).then_inc(s["mod"], 1)
            dve.wait_ge(s["mod"], 1)
            for c in range(2):
                V.scalar_tensor_tensor(gains[:, c, :], mod[:, 8:16, c], 1.0, vcol("n1"), ALU.add,
                                       ALU.mult).then_inc(s["gain"], 1)
            dve.wait_ge(s["gain"], 2)
            norm(hc, ctx_sb, rstd_c[:, :], gains[:, 1], mod[:, 0:8, 1])
            norm(h, x, rstd[:, :], gains[:, 0], mod[:, 0:8, 0])

            for j in range(NJ):
                dve.wait_ge(s["head_sum"], j + 1)
                steps.do(V.tensor_scalar(kk[:, j, TC:TT], banks[2 * j][:, 0:TX], 1e-24, None, ALU.max))
                steps.do(V.tensor_scalar(kk[:, j, 0:TC], banks[2 * j + 1][:, 0:TC], 1e-24, None, ALU.max))
                steps.last()
                V.reciprocal(kk[:, j, :], kk[:, j, :]).then_inc(s["head_rec"], 1)
            for j in range(NJ):
                dve.wait_ge(s["head_root"], j + 1)
                V.scalar_tensor_tensor(kk[:, j, :], kT[:, j, :], vcol("kk")[:, j:j + 1], kk[:, j, :], ALU.mult,
                                       ALU.mult).then_inc(s["kk_ready"], 1)
            cw = vcol("conva", 3, 4)
            cb, u_, t_ = px[:, 0:4], px[:, 4:8], px[:, 8:12]
            steps.do(V.tensor_tensor(u_, u_, t_, ALU.mult))
            steps.last()
            for j in range(4):
                steps.do(V.tensor_scalar(t_[:, j, :], u_[:, j, :], cw[:, 1, j:j + 1], None, ALU.mult))
            steps.last()
            for j in range(4):
                steps.do(V.scalar_tensor_tensor(t_[:, j, 1:TX], u_[:, j, 0:TX - 1], cw[:, 0, j:j + 1],
                                                t_[:, j, 1:TX], ALU.mult, ALU.add))
            steps.last()
            for j in range(4):
                steps.do(V.scalar_tensor_tensor(t_[:, j, 0:TX - 1], u_[:, j, 1:TX], cw[:, 2, j:j + 1],
                                                t_[:, j, 0:TX - 1], ALU.mult, ALU.add))
            steps.last()
            V.tensor_tensor(cb, cb, t_, ALU.mult).then_inc(s["conv_ready"], 1)
            dve.wait_ge(s["conv_ready"], 1)

            bank = [banks[0:4], banks[4:8]]

            def heads(b):
                return b[:, :].rearrange("p (h t) -> p h t", h=GH)

            def flat(a):
                return a.rearrange("p a b -> p (a b)")

            def over(mask):
                return mask.unsqueeze(1).broadcast_to([P, GH, L])

            def done(name, d, n, per=1, at=0):
                dve.wait_ge(s[f"{name}{d}"], per * n + (at or per))

            def group(a, g):
                return a[:, GP * g:GP * g + GP]

            def last_of(a, d):
                return a[:, :, L - 1 if d == 0 else 0]

            def gate_bias(n, g):
                for d, sc in enumerate(scans):
                    done("z_mm", d, n)
                    for k in range(2):
                        bias = spread(vcol("wa0", 2, 2, NJ)[:, d, k, GP * g:GP * g + GP], GP, L)
                        ins = V.tensor_tensor(sc.gate[:, k], heads(bank[d][0])[:, GP * k:GP * k + GP, :], bias,
                                              ALU.add)
                    ins.then_inc(s[f"z_biased{d}"], 1)

            def gates(n, g):
                for d, sc in enumerate(scans):
                    done("z_tanh", d, n)
                    steps.do(V.tensor_scalar(sc.gate[:, 0], sc.gate[:, 0], -DECAY / 2, -DECAY / 2, ALU.mult, ALU.add))
                    steps.do(V.tensor_scalar(sc.gate[:, 1], sc.gate[:, 1], 0.5, 0.5, ALU.mult, ALU.add))

            def running_sums(n, g):
                steps.last()
                for d, sc in enumerate(scans):
                    if not (isinstance(n, int) and n == 0):
                        done("tok_mm", d, n - 1, 2, 1)
                    to, gate, r = flat(sc.cum), flat(sc.gate[:, 0]), reset[:, d, :]
                    if d == 1:
                        to, gate, r = to[:, ::-1], gate[:, ::-1], r[:, ::-1]
                    steps.do(V.tensor_tensor_scan(to, r, gate, 0.0, ALU.mult, ALU.add))
                    steps.do(V.scalar_tensor_tensor(sc.kh, sc.gate[:, 1], -1.0,
                                                    spread(group(vcol("ka"), g), GP, L), ALU.add, ALU.mult))

            def centre(n, g):
                steps.last()
                for d, sc in enumerate(scans):
                    at = bass.ds(chunk_at(d, n_place[0], n_place[1]), L)
                    steps.do(V.tensor_scalar(sc.half, last_of(sc.cum, d), -0.5, None, ALU.mult))
                    steps.do(V.scalar_tensor_tensor(sc.kh, sc.kh, 1.0, group(kT, g)[:, :, at], ALU.add, ALU.mult))
                    steps.do(V.tensor_tensor(sc.gate[:, 1], sc.gate[:, 1], group(kk, g)[:, :, at], ALU.mult))
                steps.last()
                for d, sc in enumerate(scans):
                    steps.do(V.tensor_tensor(sc.cum, sc.cum, spread(sc.half, GP, L), ALU.add))
                steps.last()
                for d, sc in enumerate(scans):
                    V.tensor_tensor(sc.gate[:, 0], sc.cum, sc.gate[:, 0], ALU.subtract).then_inc(s[f"decays{d}"], 1)

            def keys(n, g):
                for d, sc in enumerate(scans):
                    at = bass.ds(chunk_at(d, n_place[0], n_place[1]), L)
                    done("exps", d, n, 3)
                    V.tensor_tensor(sc.kt, group(kk, g)[:, :, at], sc.gate[:, 0], ALU.mult).then_inc(s[f"keys{d}"], 1)
                    V.tensor_tensor(sc.bh, sc.gate[:, 1], sc.cum, ALU.mult).then_inc(s[f"keys{d}"], 1)
                    V.tensor_tensor(sc.kh, sc.kh, sc.cum, ALU.mult).then_inc(s[f"keys{d}"], 1)

            def keys_r(n, g, cur):
                for d, sc in enumerate(scans):
                    ax = bass.ds(chunk_at(d, n_place[0], True) - TC, L)
                    if cur:
                        dve.wait_ge(s[f"early_mm{d}"], n - NCC)
                    V.tensor_tensor(sc.rt, group(rT, g)[:, :, ax], sc.pin, ALU.mult).then_inc(s[f"rt{d}"], 1)

            def first_level(n, d):
                sc = scans[d]
                done("a_mm", d, n)
                steps.do(V.scalar_tensor_tensor(sc.X, heads(bank[d][3]), -1.0, over(level[:, d, 0]), ALU.mult,
                                                ALU.mult))
                steps.last()
                V.tensor_tensor(sc.X, sc.X, over(ident), ALU.add).then_inc(s[f"X{d}"], 1)

            def k_scores(n, d):
                done("m_mm", d, n, 2)
                V.tensor_tensor(scans[d].ak, heads(bank[d][0]), over(strict[:, d]), ALU.mult).then_inc(s[f"ak{d}"], 1)

            def r_scores(n, d, k):
                sc = scans[d]
                dve.wait_ge(s[f"r_mm{d}"], 2 * (n - NCC) + k + 1)
                V.tensor_tensor((sc.rb, sc.rk)[k], heads(bank[d][2]), over(incl[:, d]),
                                ALU.mult).then_inc(s[f"r_out{d}"], 1)

            def state_decayed(g):
                for d, sc in enumerate(scans):
                    steps.do(V.tensor_copy(sc.decay, last_of(sc.pin, d)))
                    V.tensor_tensor(sc.S_in, sc.S[:, g], spread(last_of(sc.pin, d), GP, HD),
                                    ALU.mult).then_inc(s[f"S_in{d}"], 1)

            def w_out(n, d, l):
                done("nx_mm", d, n, LEVELS - 1, l - 1)
                V.tensor_tensor(scans[d].w, heads(bank[d][3]), over(level[:, d, l - 1]),
                                ALU.mult).then_inc(s[f"w{d}"], 1)

            def x_out(n, d, l):
                done("dx_mm", d, n, LEVELS - 1, l - 1)
                V.tensor_tensor(scans[d].X, heads(bank[d][3]), scans[d].X, ALU.add).then_inc(s[f"X{d}"], 1)

            n_place = [0, False]

            def prepare():
                for step in (gate_bias, gates, running_sums, centre, keys):
                    step(0, 0)
                state_decayed(0)
                for d in range(2):
                    first_level(0, d)
                for d in range(2):
                    k_scores(0, d)

            def turn(n, c, g, cur, nxt):
                n_place[:] = c + g, nxt
                for l in range(2, LEVELS + 1):
                    w_out(n, 0, l)
                    if nxt is not None:
                        if l == 2:
                            gate_bias(n + 1, 1 - g)
                        elif l == 4:
                            running_sums(n + 1, 1 - g)
                        elif l == 6:
                            keys(n + 1, 1 - g)
                    x_out(n, 0, l)
                    w_out(n, 1, l)
                    if nxt is not None:
                        if l == 3:
                            gates(n + 1, 1 - g)
                        elif l == 4:
                            centre(n + 1, 1 - g)
                        elif l == 6 and nxt:
                            keys_r(n + 1, 1 - g, cur)
                    x_out(n, 1, l)
                if nxt is not None:
                    for d in range(2):
                        first_level(n + 1, d)
                for d, sc in enumerate(scans):
                    done("ds_mm", d, n)
                    if cur:
                        y = group(y_dir[d], g)[:, :, bass.ds(chunk_at(d, c, True) - TC, L)]
                        V.tensor_tensor(y, heads(bank[d][2])[:, 0:GP, :], y, ALU.add).then_inc(s[f"y_out{d}"], 1)
                    if nxt is not None:
                        steps.do(V.tensor_tensor(sc.S[:, g], bank[d][2][:, 256:256 + GP * HD].rearrange(
                            "p (j f) -> p j f", j=GP), sc.S_in, ALU.add))
                        steps.last()
                        V.tensor_tensor(sc.S[:, g], sc.S[:, g], spread(sc.decay, GP, HD),
                                        ALU.mult).then_inc(s[f"S{d}"], 1)
                        k_scores(n + 1, d)
                if nxt is not None:
                    for d in range(2):
                        done("S", d, n)
                    state_decayed(1 - g)
                if not cur:
                    dve.wait_ge(s["product"], DONE[SLOT["ADA2"] + 3] + 4 * n)
                    V.tensor_tensor(mod[:, 16 + 8 * n:24 + 8 * n, :],
                                    banks[2][:, 0:16].rearrange("p (m c) -> p m c", c=2),
                                    spread(vcol("adab")[:, 16 + 8 * n:24 + 8 * n], 8, 2),
                                    ALU.add).then_inc(s["mod"], 1)
                if nxt:
                    for k in range(2):
                        for d in range(2):
                            r_scores(n + 1, d, k)

            dve.wait_ge(s["bd_clean"], 2)
            all_turns(dve, prepare, turn, steps, 44)

            for d in range(2):
                dve.wait_ge(s[f"y_out{d}"], NCX)
            for j in range(NJ):
                V.tensor_tensor(ys[:, j, :], y_dir[0][:, j, :], y_dir[1][:, j, :], ALU.add).then_inc(s["y_rkr"], 1)
                V.scalar_tensor_tensor(rkr[:, j, :], rT[:, j, :], vcol("rk")[:, j:j + 1], kT[:, j, TC:TT], ALU.mult,
                                       ALU.mult).then_inc(s["y_rkr"], 1)
            for j in range(NJ):
                dve.wait_ge(s["y_rkr_mm"], 2 * j + 1)
                V.scalar_tensor_tensor(yc[:, j, :], banks[j][:, :], -1.0 / HD, ys[:, j, :], ALU.mult,
                                       ALU.add).then_inc(s["centred_bonus"], 1)
                dve.wait_ge(s["y_rkr_mm"], 2 * j + 2)
                V.tensor_tensor(bonus[:, j, :], banks[4 + j][:, :], vT[:, j, TC:TT], ALU.mult).then_inc(s["centred_bonus"], 1)
            for j in range(NJ):
                dve.wait_ge(s["head_sum"], NJ + j + 1)
                steps.do(V.tensor_scalar(yr[:, j, :], banks[j][:, :], 1.0 / HD, GN_EPS, ALU.mult, ALU.add))
                steps.last()
                V.reciprocal(yr[:, j, :], yr[:, j, :]).then_inc(s["head_rec"], 1)
            for j in range(NJ):
                dve.wait_ge(s["head_root"], NJ + j + 1)
                steps.do(V.scalar_tensor_tensor(yc[:, j, :], yc[:, j, :], vcol("lng")[:, j:j + 1], yr[:, j, :],
                                                ALU.mult, ALU.mult))
                steps.last()
                steps.do(V.scalar_tensor_tensor(yc[:, j, :], yc[:, j, :], vcol("lnb")[:, j:j + 1], bonus[:, j, :],
                                                ALU.add, ALU.add))
                steps.last()
                dve.wait_ge(s["gate_mm"], j + 1)
                V.tensor_tensor(y_rwkv[:, j, :], banks[4 + j][:, :], yc[:, j, :], ALU.mult).then_inc(s["mixed"], 1)

            def residual(p0, n, nbanks, gate=None, per=1):
                def one(m, bank, i=None):
                    dve.wait_ge(s["product"], p0 + per * m + per)
                    xm = x[:, bass.ds(m, 1), :].rearrange("p a t -> p (a t)")
                    if gate is None:
                        V.tensor_tensor(xm, banks[bank][:, :], xm, ALU.add).then_inc(s["taken"], 1)
                    else:
                        V.scalar_tensor_tensor(xm, banks[bank][:, :], mod[:, bass.ds(gate + m, 1), 0], xm, ALU.mult,
                                               ALU.add).then_inc(s["taken"], 1)

                with dve.Fori(0, n // nbanks) as i:
                    for b in range(nbanks):
                        one(nbanks * i + b, b)

            residual(DONE[SLOT["W_OUT"] - 1], KB, 4, gate=2 * KB)
            V.scalar_tensor_tensor(gain2[:, :], mod[:, 4 * KB:5 * KB, 0], 1.0, vcol("n2"), ALU.add,
                                   ALU.mult).then_inc(s["gain"], 1)
            dve.wait_ge(s["gain"], 3)
            mean_square(rstd[:, :], banks[6], TX)
            norm(h, x, rstd[:, :], gain2, mod[:, 3 * KB:4 * KB, 0])

            def ffn(first, p0, taps):
                def body(i, u, base):
                    dve.wait_ge(s["gate_in"], first + 2 * i + u + 1)
                    if not (isinstance(i, int) and i == 0 and first == 0):
                        dve.wait_ge(s["silu"], first + 2 * i + u - 1)
                    taps(i, u)
                    dve.wait_ge(s["silu"], first + 2 * i + u + 1)
                    dve.wait_ge(s["product"], p0 + 4 * i + 2 * u + 2)
                    V.tensor_tensor(act[:, bass.ds(2 * i + u, 1), :].rearrange("p a t -> p (a t)"), silu[u],
                                    banks[2 * u + 1][:, :], ALU.mult).then_inc(s["val_free"], 1)
                return body

            def run_ffn(first, p0, taps, per):
                body = ffn(first, p0, taps)
                body(0, 0, 0)
                body(0, 1, 0)
                with dve.Fori(1, FB // 2) as i:
                    steps.loop(i - 1, 2 * per)
                    body(i, 0, 0)
                    body(i, 1, 0)
                    steps.end(FB // 2 - 1)

            def taps_grid(i, u):
                f0 = VEC["fcw"][0] + 10 * (2 * i + u)
                to = conv[u].rearrange("p (y x) -> p y x", y=GRID_H)
                steps.do(V.tensor_scalar(to, pad[u][:, 0:GRID_H, 0:GRID_W], v[:, bass.ds(f0, 1)],
                                         v[:, bass.ds(f0 + 9, 1)], ALU.mult, ALU.add))
                for n in range(1, 9):
                    steps.last()
                    ins = V.scalar_tensor_tensor(to, pad[u][:, n // 3:n // 3 + GRID_H, n % 3:n % 3 + GRID_W],
                                                 v[:, bass.ds(f0 + n, 1)], to, ALU.mult, ALU.add)
                    if n < 8:
                        steps.do(ins)
                ins.then_inc(s["conv"], 1)

            def taps_causal(i, u):
                f0 = VEC["cw2"][0] + 4 * (2 * i + u)
                steps.do(V.tensor_scalar(conv[u], pad1[u][:, 0:TX], v[:, bass.ds(f0, 1)], v[:, bass.ds(f0 + 3, 1)],
                                         ALU.mult, ALU.add))
                for n in range(1, 3):
                    steps.last()
                    ins = V.scalar_tensor_tensor(conv[u], pad1[u][:, n:n + TX], v[:, bass.ds(f0 + n, 1)], conv[u],
                                                 ALU.mult, ALU.add)
                    if n < 2:
                        steps.do(ins)
                ins.then_inc(s["conv"], 1)

            run_ffn(0, DONE[SLOT["UP1"] - 1], taps_grid, 8)
            residual(DONE[SLOT["DOWN1"] - 1], KB, 2, gate=5 * KB, per=2)
            mean_square(rstd[:, :], banks[6], TX)
            norm(x, x, rstd[:, :], vcol("fin"))

            lb = vcol("lb", 2, 4)
            V.tensor_tensor(lbv, lb[:, 0], lb[:, 1], ALU.subtract).then_inc(s["lb"], 1)
            mean_square(rstd[:, :], banks[7], TX)
            norm(h, x, rstd[:, :], vcol("nmix"))
            dve.wait_ge(s["sig"], 1)
            steps.do(V.tensor_scalar(oml, lbv, -1.0, 1.0, ALU.mult, ALU.add))
            steps.last()
            dve.wait_ge(s["taken"], 73)
            for hd in range(NH):
                dve.wait_ge(s["forget"], hd + 1)
                src = pr[:, 4 + hd, :].rearrange("p (n t) -> p n t", n=NB)
                V.tensor_scalar(cumf[:, :, hd, :], src, oml[:, hd:hd + 1], lbv[:, hd:hd + 1], ALU.mult,
                                ALU.add).then_inc(s["f"], 1)
            for hd in range(NH):
                dve.wait_ge(s["f"], hd + 1)
                V.tensor_scalar(kh[:, :, hd, :], cumf[:, :, hd, :], -1.0, 1.0, ALU.mult,
                                ALU.add).then_inc(s["keys_hg"], 1)
                V.tensor_scalar(qh[:, :, hd, :], pr[:, hd, :].rearrange("p (n t) -> p n t", n=NB), HC ** -0.5, None,
                                ALU.mult).then_inc(s["q_hg"], 1)
            cf2 = cumf.rearrange("p n h t -> p (n h t)")
            dve.wait_ge(s["cum_f"], NH)
            dve.wait_ge(s["pads2"], 5)
            V.tensor_tensor_scan(cf2, hreset.rearrange("p n h t -> p (n h t)"), cf2, 0.0, ALU.mult,
                                 ALU.add).then_inc(s["cum_scan"], 1)
            dve.wait_ge(s["cum_scan"], 1)
            dve.wait_ge(s["masks_in"], 16)

            def mixer2(i):
                first = isinstance(i, int) and i == 0
                chunk = bass.ds(NH * HC * i, NH * HC)
                cf, kf, qf = (a.rearrange("p n h t -> p (n h t)")[:, chunk] for a in (cumf, kh, qh))
                dve.wait_ge(s["a_s_mm"], i + 1)
                if not first:
                    dve.wait_ge(s["a_t_mm"], 4 * i)
                mask = band_sb[:, bass.ds(i, 1), :].broadcast_to([P, 2, 2 * HC])
                for j in range(4):
                    steps.do(V.scalar_tensor_tensor(pp[:, 2 * j:2 * j + 2, :],
                                                    banks[4 + j][:, :].rearrange("p (g k) -> p g k", g=2), 0.125,
                                                    mask, ALU.mult, ALU.add))
                steps.last()
                steps.do(V.tensor_reduce(hi, pp, AX.X, ALU.max))
                steps.last()
                steps.do(V.tensor_tensor(hi, hi, sink_order, ALU.max))
                steps.last()
                V.tensor_scalar(nm, hi, -1.0, None, ALU.mult).then_inc(s["a_nm"], 1)
                V.tensor_tensor(dsk, sink_order, hi, ALU.subtract).then_inc(s["a_ds"], 1)

                def halves(a, l):
                    w = a.rearrange("p (b t) -> p b t", t=1 << l)
                    return w[:, :, 0:1 << l - 1], w[:, :, 1 << l - 1:1 << l]

                def decay(l):
                    nb = NH * HC >> l
                    early, late = halves(cf, l)
                    mid = early[:, :, (1 << l - 1) - 1:1 << l - 1].broadcast_to([P, nb, 1 << l - 1])
                    de_early, de_late = halves(de[l % 2], l)
                    V.tensor_tensor(de_early, mid, early, ALU.subtract).then_inc(s["h_d"], 1)
                    V.tensor_tensor(de_late, late, mid, ALU.subtract).then_inc(s["h_d"], 1)

                def scale(l):
                    dve.wait_ge(s["h_e"], HLEV * i + l)
                    if not first or l > 2:
                        dve.wait_ge(s["h_mm"], 8 * i + l - 2)
                    z, e = halves(zz[l % 2], l), halves(de[l % 2], l)
                    V.tensor_tensor(z[0], e[0], halves(kf, l)[0], ALU.mult).then_inc(s["h_z"], 1)
                    if l > 1:
                        dve.wait_ge(s["h_mm"], 8 * i + l - 1)
                    V.tensor_tensor(z[1], e[1], halves(qf, l)[1], ALU.mult).then_inc(s["h_z"], 1)

                def pick(l):
                    mask = (level[:, 1, l - 1] if l <= HLEV else ident).unsqueeze(1).broadcast_to([P, NH, HC])
                    bank = banks[l % 2][:, :].rearrange("p (h t) -> p h t", h=NH)
                    if l == 1:
                        if not first:
                            dve.wait_ge(s["h_o_mm"], i)
                        V.tensor_tensor(sT, bank, mask, ALU.mult).then_inc(s["h_s"], 1)
                    else:
                        V.copy_predicated(sT, mask.bitcast(U32), bank).then_inc(s["h_s"], 1)

                decay(1)
                decay(2)
                dve.wait_ge(s["h_ec"], i + 1)
                V.tensor_tensor(qe.rearrange("p h t -> p (h t)"), ec.rearrange("p h t -> p (h t)"), qf,
                                ALU.mult).then_inc(s["h_qe"], 1)
                cw_ = cf.rearrange("p (h t) -> p h t", h=NH)
                V.tensor_tensor(ke, cw_[:, :, HC - 1:HC].broadcast_to([P, NH, HC]), cw_,
                                ALU.subtract).then_inc(s["h_ke"], 1)
                for l in range(1, HLEV + 1):
                    if l > 2:
                        dve.wait_ge(s["h_s"], 8 * i + l - 2)
                    scale(l)
                    if l > 1:
                        pick(l - 1)
                    if l + 2 <= HLEV:
                        dve.wait_ge(s["h_z"], 2 * HLEV * i + 2 * l)
                        decay(l + 2)
                dve.wait_ge(s["h_ke_e"], i + 1)
                dve.wait_ge(s["h_mm"], 8 * i + HLEV)
                dve.wait_ge(s["h_s"], 8 * i + HLEV - 1)
                V.tensor_tensor(ke.rearrange("p h t -> p (h t)"), ke.rearrange("p h t -> p (h t)"), kf,
                                ALU.mult).then_inc(s["h_kend"], 1)
                pick(HLEV)
                dve.wait_ge(s["a_es"], i + 1)
                dve.wait_ge(s["a_p"], NQ * i + NQ)
                dve.wait_ge(s["h_mm"], 8 * i + HLEV + 1)
                dve.wait_ge(s["h_s"], 8 * i + HLEV)
                steps.do(V.tensor_tensor(den, den, esk, ALU.add))
                pick(HLEV + 1)
                steps.last()
                steps.do(V.reciprocal(den, den))
                steps.last()
                V.tensor_tensor(pp, pp, spread(den, NQ, 2 * HC), ALU.mult).then_inc(s["a_pn"], 1)
                dve.wait_ge(s["h_o_mm"], i + 1)
                steps.do(V.tensor_tensor(S2, S2, ec[:, :, HC - 1:HC].broadcast_to([P, NH, HC]), ALU.mult))
                steps.last()
                dve.wait_ge(s["h_ds"], i + 1)
                V.tensor_tensor(S2, banks[3][:, :].rearrange("p (h t) -> p h t", h=NH), S2,
                                ALU.add).then_inc(s["h_S"], 1)

            sink_order = vcol("sinks")
            dve.wait_ge(s["S_clean"], 1)
            mixer2(0)
            with dve.Fori(1, NB) as i:
                steps.loop(i - 1, 9)
                mixer2(i)
                steps.end(NB - 1)
            for hd in range(NH):
                dve.wait_ge(s["head_sum"], 2 * NJ + hd + 1)
                steps.do(V.tensor_scalar(yr2[:, hd, :], banks[hd][:, :], 1.0 / HC, EPS, ALU.mult, ALU.add))
                steps.last()
                V.reciprocal(yr2[:, hd, :], yr2[:, hd, :]).then_inc(s["head_rec"], 1)
            for hd in range(NH):
                dve.wait_ge(s["head_root"], 2 * NJ + hd + 1)
                steps.do(V.scalar_tensor_tensor(mix[:, hd, :], mix[:, hd, :], vcol("hgn"), yr2[:, hd, :], ALU.mult,
                                                ALU.mult))
            steps.last()
            for hd in range(NH):
                V.tensor_tensor(mix[:, hd, :], mix[:, hd, :], pr[:, 12 + hd, :], ALU.mult).then_inc(s["mix2"], 1)
            residual(DONE[SLOT["W_OUT2"] - 1], KB, 4)
            mean_square(rstd[:, :], banks[6], TX)
            norm(h, x, rstd[:, :], vcol("nffn"))
            run_ffn(FB, DONE[SLOT["UP2"] - 1], taps_causal, 2)
            residual(DONE[SLOT["DOWN2"] - 1], KB, 2, per=2)
            mean_square(rstd[:, :], banks[6], TX)
            norm(x, x, rstd[:, :], vcol("fin2"))


def _tiles(w, blocks=KB):
    k, m = w.shape
    t = w.reshape(k // P, P, m // P, P).transpose(2, 1, 0, 3)
    return t.reshape(m // P, P, k)


def _halves(w):
    t = _tiles(w).reshape(D // P, P, 2, HALF * P)
    return t.transpose(0, 2, 1, 3).reshape(2 * D // P, P, HALF * P)


def _columns(v):
    return v.reshape(-1, P).T


def _arrange(a):
    g = {n: np.asarray(v) for n, v in a.items()}
    dc = D // 2
    w_in = g["w_in"][0]
    w_in = np.concatenate([w_in[:, :4 * dc], w_in[:, 6 * dc + 128:], w_in[:, 4 * dc:6 * dc + 128]], axis=1)
    up1 = g["ffn_w_up"][0].reshape(D, 2, FB, P).transpose(0, 2, 1, 3).reshape(D, 2 * DFF)
    up2 = np.stack([g["w_gate_2"][0].reshape(D, FB, P), g["w_up_2"][0].reshape(D, FB, P)], axis=2).reshape(D, 2 * DFF)
    head = np.concatenate([np.arange(64) + 64 * h for j in range(4) for h in (j, j + 4)])
    w_in2 = g["w_in_2"][0]
    w_in2 = np.concatenate([w_in2[:, :2048], w_in2[:, 2048 + head], w_in2[:, 2560:]], axis=1)
    w_out2 = g["w_out_2"][0]
    w_out2 = np.concatenate([w_out2[:512], w_out2[512 + head]], axis=0)
    batt = g["b_attn_2"][0]
    batt = np.concatenate([batt[head], batt[512:]])
    ada = _tiles(g["ada_w"][0])
    w8 = np.concatenate([ada[:16], _tiles(w_in), ada[16:], _tiles(g["w_out"][0]), _tiles(up1),
                         _tiles(w_in2), _tiles(w_out2), _tiles(up2)])
    w11 = np.concatenate([_halves(g["ffn_w_down"][0]), _halves(g["w_down_2"][0])])
    lora = np.zeros((P, 2, 2, 4, P), np.float32)
    for d in range(2):
        lora[:64, d, 0] = g["rw_w_up"][0, d].reshape(64, 4, P)
        lora[64:, d, 1] = g["rw_a_up"][0, d].reshape(64, 4, P)
    vec = np.zeros((P, NVEC), np.float32)

    def put(name, v):
        o, w = VEC[name]
        vec[:, o:o + w] = v.reshape(P, w)

    put("n1", _columns(g["norm1_g"]))
    put("n2", _columns(g["norm2_g"]))
    put("fin", _columns(g["final_g"]))
    put("cs", np.stack([_columns(g["c"]), _columns(g["c_ctx"])], axis=2))
    put("adab", _columns(g["ada_b"]))
    put("conva", _columns(g["conv_a_w"]))
    put("wa0", np.concatenate([_columns(g[n][0, d]) for d in range(2) for n in ("rw_w0", "rw_a0")], axis=1))
    put("kk", _columns(g["rw_k_k"]))
    put("ka", _columns(g["rw_k_a"]))
    put("rk", _columns(g["rw_r_k"]))
    put("lng", _columns(g["rw_ln_g"]))
    put("lnb", _columns(g["rw_ln_b"]))
    fcw = np.concatenate([g["ffn_conv_w"].reshape(9, FB, P), g["ffn_conv_b"].reshape(1, FB, P)])
    put("fcw", fcw.transpose(2, 1, 0))
    put("nmix", _columns(g["norm_mix_w_2"]))
    put("nffn", _columns(g["norm_ffn_w_2"]))
    put("batt", _columns(batt))
    put("lb", _columns(g["lb_logits_2"]))
    put("hgn", _columns(g["hg_norm_w_2"]))
    sinks = g["sinks_2"][0][[h for j in range(4) for h in (j, j + 4)]]
    put("sinks", np.broadcast_to(sinks, (P, NQ)))
    cw2 = np.concatenate([g["conv_w_2"].reshape(3, FB, P), g["conv_b_2"].reshape(1, FB, P)])
    put("cw2", cw2.transpose(2, 1, 0))
    put("fin2", _columns(g["final_norm_w_2"]))

    def features(x):
        return np.ascontiguousarray(x.T.reshape(KB, P, -1).transpose(1, 0, 2))

    return {
        "xT": features(g["x"][0]), "ctxT": features(g["ctx"][0]), "vec": vec, "con": constants(),
        "band": band_masks(), "w8": w8, "w11": w11,
        "lora": lora.reshape(P, 16 * P), "gup": np.ascontiguousarray(g["rw_g_up"][0]),
    }


def kernel(**inputs):
    import concourse.bacc as _bacc
    from concourse.bass_utils import run_bass_kernel_spmd as _run

    nc = _bacc.Bacc("TRN2", target_bir_lowering=False, num_devices=1)
    arrays = {n: np.ascontiguousarray(a) for n, a in _arrange(inputs).items()}
    args = {n: nc.dram_tensor(n, a.shape, mybir.dt.from_np(a.dtype), kind="ExternalInput").ap()
            for n, a in arrays.items()}
    out = nc.dram_tensor("outT", (P, KB, TX), F32, kind="ExternalOutput").ap()
    two_blocks(nc, outT=out, **args)
    r = _run(nc, [arrays], core_ids=[0])
    got = r.results[0]["outT"]
    return got.transpose(2, 1, 0).reshape(1, TX, D)
```

```python
from contextlib import ExitStack

import numpy as np
import concourse.bass as bass
from concourse import mybir

F32 = mybir.dt.float32
F32R = mybir.dt.float32r
U32 = mybir.dt.uint32
ALU = mybir.AluOpType
ACT = mybir.ActivationFunctionType
AX = mybir.AxisListType

P = 128
D = 1024
KB = D // P
TX = 512
TC = 256
TT = TC + TX
DFF = 2816
FB = DFF // P
HALF = FB // 2
GRID_W = 64
GRID_H = TX // GRID_W
DECAY = float(np.exp(-0.5))
EPS = 1e-6
GN_EPS = 64e-5
HD = 64
L = 128
NJ = 4
GP = 2
GH = 2 * GP
NG = NJ // GP
NCC, NCX = NG * TC // L, NG * TX // L
NC = NCC + NCX
LEVELS = 7
HC = 128
NH = 4
NB = TX // HC
NQ = 8
HLEV = 7

VEC = {}
_n = 0
for _name, _w in (("n1", KB), ("n2", KB), ("fin", KB), ("cs", 2 * KB), ("adab", 6 * KB), ("conva", 3 * 4),
                  ("wa0", 2 * 8), ("kk", 4), ("ka", 4), ("rk", 4), ("lng", 4), ("lnb", 4), ("fcw", FB * 10),
                  ("nmix", KB), ("nffn", KB), ("batt", 6), ("lb", 8), ("hgn", 1), ("sinks", NQ),
                  ("cw2", FB * 4), ("fin2", KB)):
    VEC[_name] = (_n, _w)
    _n += _w
NVEC = _n

CON = {}
_n = 0
for _name, _w in (("ident", P), ("ones", P), ("headones", P), ("level", 2 * LEVELS * L),
                  ("strict", 2 * L), ("incl", 2 * L), ("reset", 2 * GP * L)):
    CON[_name] = (_n, _w)
    _n += _w
NCON = _n


def constants():
    c = np.zeros((P, NCON), np.float32)

    def put(name, a):
        o, w = CON[name]
        c[:, o:o + w] = a.reshape(P, w)

    put("ident", np.eye(P))
    put("ones", np.ones((P, P)))
    put("headones", np.kron(np.eye(2), np.ones((HD, HD))))
    t, s = np.arange(L)[:, None], np.arange(L)[None, :]
    level = np.stack([(t >> l == s >> l) & (t >> (l - 1) & 1 == 1) & (s >> (l - 1) & 1 == 0)
                      for l in range(1, LEVELS + 1)])
    level = np.stack([level, level.transpose(0, 2, 1)])
    put("level", level.transpose(2, 0, 1, 3))
    put("strict", np.stack([t < s, t > s]).transpose(1, 0, 2))
    put("incl", np.stack([t <= s, t >= s]).transpose(1, 0, 2))
    reset = np.ones((2, GP, L))
    reset[0, :, 0] = 0
    reset[1, :, -1] = 0
    put("reset", np.broadcast_to(reset, (P, 2, GP, L)))
    return c


def band_masks():
    q, k = np.arange(HC)[:, None], np.arange(2 * HC)[None, :]
    band = (q + HC - k >= 0) & (q + HC - k < HC)
    m = np.stack([band & (k >= HC), band, band, band])
    return np.ascontiguousarray(np.where(m, 0.0, -3e38).transpose(1, 0, 2).astype(np.float32))


RING = 2
STAGES = (("ADA1", 8, 1), ("W_IN", 8, 2), ("W_INB", 1, 3), ("W_INC", 4, 4), ("ADA2", 16, 1), ("W_OUT", 4, 2),
          ("UP1", FB, 2), ("DOWN1", 16, 1), ("W_IN2", 11, 2), ("W_OUT2", 4, 2), ("UP2", FB, 2), ("DOWN2", 16, 1))
SLOT, DONE = {}, []
_n = _g = 0
for _name, _slots, _per in STAGES:
    SLOT[_name] = _g
    for _ in range(_slots):
        _n += _per
        DONE.append(_n)
    _g += _slots


WHOLE = ("ADA1", "ADA2")
PIECE, FREED = {}, []
_n = 0
for _name, _slots, _per in STAGES:
    PIECE[_name] = _n
    for _ in range(_slots):
        if _name not in WHOLE:
            _n += 1 if _name.startswith("DOWN") else 2
            FREED.append(("w_lo", _n))
        else:
            FREED.append(("product", DONE[len(FREED)]))


def in_pairs(eng, n, body, peel=False):
    first = 0
    if peel:
        body(0, 0)
        body(0, 1)
        first = 1
    with eng.Fori(first, n // 2) as i:
        body(i, 0)
        body(i, 1)
    if n % 2:
        body(n // 2, 0)


def two_blocks(nc, xT, ctxT, vec, con, band, w8, w11, lora, gup, outT):
    with ExitStack() as ctx:
        def sb(name, shape, dt=F32):
            return ctx.enter_context(nc.sbuf_tensor(name, shape, dt))

        s = {}

        def sem(*names):
            for name in names:
                s[name] = ctx.enter_context(nc.semaphore(name))

        banks = [ctx.enter_context(nc.psum_tensor(f"bank{b}", [P, 512], F32)) for b in range(8)]

        x = sb("x", [P, KB, TX])
        v = sb("v", [P, NVEC])
        k_ = sb("k_", [P, NCON])
        ring = sb("ring", [P, RING, 2 * KB * P])
        mod = sb("mod", [P, 6 * KB, 2])
        gains = sb("gains", [P, 3, KB])
        siluc = sb("siluc", [P, 2 * KB])
        rstd = sb("rstd", [P, TX])
        gain2 = sb("gain2", [P, KB])
        rstd_c = sb("rstd_c", [P, TC])
        NARENA = 40084

        def overlay(name, at, dt, *shape):
            assert at + int(np.prod(shape)) <= NARENA
            with nc.sbuf_tensor(f"{name}_from", [P, at], F32) if at else ExitStack():
                with nc.sbuf_tensor(name, [P, *shape], dt) as a:
                    return a

        act_hi = overlay("act_hi", 0, F32R, FB, TX)
        act_lo = overlay("act_lo", FB * TX, F32R, FB, TX)
        at_h = 2 * FB * TX
        hf = overlay("hf", at_h, F32, KB, TX)
        hf_lo = overlay("hf_lo", at_h, F32R, KB, TX)
        hf_hi = overlay("hf_hi", at_h + KB * TX, F32R, KB, TX)
        at_w = at_h + 2 * KB * TX
        w_up = [overlay(f"w_up{c}", at_w + c * 2 * KB * P, F32R, 2, KB, P) for c in range(2)]
        w_down = [overlay(f"w_down{c}", at_w + c * 2 * HALF * P, F32R, 2, HALF, P) for c in range(2)]
        at_ffn = at_w + 4 * KB * P
        ffn_sb = overlay("ffn_sb", at_ffn, F32, 4420)

        def low_high(name, at, at_high, n, t):
            lo = overlay(f"{name}_lo", at, F32R, n, t)
            return overlay(f"{name}_hi", at_high, F32R, n, t), lo

        def pieces(name, *at):
            return [overlay(f"{name}{c}", a, F32R, 2, KB, P) for c, a in enumerate(at)]

        at_px, at_kk = 9 * TT, 9 * TT + 17 * TX
        at_n = at_kk + 4 * TT
        at_s = at_n + 3 * KB * TC
        hx = low_high("hx", at_n, at_s, KB, TX)
        hc_ = low_high("hc", at_n + KB * TX, at_s + KB * TX, KB, TC)
        w_in = pieces("w_in", *(at_s + KB * (TX + TC) + 2 * KB * P * c for c in range(2)))
        ycv = low_high("ycv", at_px, at_n, 4, TX)
        yrw = low_high("yrw", at_s + 6 * 4 * TX, at_px + 4 * TX, 4, TX)
        w_out = pieces("w_out", 0, at_kk)
        at_mix = at_n + KB * TX + 2 * NB * HC + 9 * NH * HC + 4 * NH * HC + NH * HC + 2 * HC + 4 * HC + 4 * NQ * HC
        h2 = low_high("h2", at_n, at_mix, KB, TX)
        w_in2 = pieces("w_in2", at_mix - 2 * NQ * HC, at_n + KB * TX + 2 * NB * HC + 9 * NH * HC)
        mx = low_high("mx", at_mix, 20 * TX, KB, TX)
        w_out2 = pieces("w_out2", 8 * TX, 16 * TX)
        w_of = {"W_IN": w_in, "W_INB": w_in, "W_INC": w_in, "W_OUT": w_out, "UP1": w_up, "W_IN2": w_in2,
                "W_OUT2": w_out2, "UP2": w_up}
        arena = sb("arena", [P, NARENA])

        class Area:

            def __init__(self, at=0, of=None):
                self.at, self.of = at, arena if of is None else of

            def take(self, *shape):
                n = int(np.prod(shape))
                a = self.of[:, self.at:self.at + n]
                self.at += n
                assert self.at <= NARENA, self.at
                names = " ".join(f"d{i}" for i in range(len(shape)))
                return a.rearrange(f"p ({names}) -> p {names}",
                                   **{f"d{i}": n for i, n in enumerate(shape)}) if len(shape) > 1 else a

        def vcol(name, *shape):
            o, w = VEC[name]
            a = v[:, o:o + w]
            if not shape:
                return a
            names = " ".join(f"d{i}" for i in range(len(shape)))
            return a.rearrange(f"p ({names}) -> p {names}", **{f"d{i}": n for i, n in enumerate(shape)})

        def kcol(name, *shape):
            o, w = CON[name]
            a = k_[:, o:o + w]
            if not shape:
                return a
            names = " ".join(f"d{i}" for i in range(len(shape)))
            return a.rearrange(f"p ({names}) -> p {names}", **{f"d{i}": n for i, n in enumerate(shape)})

        def spread(a, *shape):
            return a.unsqueeze(len(a.shape)).broadcast_to([P, *shape])

        ident, ones, headones = kcol("ident"), kcol("ones"), kcol("headones")
        level = kcol("level", 2, LEVELS, L)
        strict, incl = kcol("strict", 2, L), kcol("incl", 2, L)
        reset = kcol("reset", 2, GP * L)

        A1 = Area()
        kv = A1.take(9, TT)
        px = A1.take(17, TX)
        kk = A1.take(4, TT)
        y_conv, rT, g_lo = px[:, 0:4], px[:, 12:16], px[:, 16]
        y_dir = [px[:, 4:8], px[:, 8:12]]
        kT, vT, lowT = kv[:, 0:4], kv[:, 4:8], kv[:, 8]
        staged = A1.at
        h = A1.take(KB, TX)
        hc = A1.take(KB, TC)
        ctx_sb = px[:, 0:4].rearrange("p a (b t) -> p (a b) t", b=2)
        ada_w = [Area(staged + 6144 + 2 * KB * P * g) for g in range(7)] + [Area(0)]
        ada_w = [a.take(2, KB, P) for a in ada_w]
        ada_row = Area(2 * KB * P).take(4, 4 * P)
        kk_sq = Area(staged + 2048 + 512).take(NJ, TT)
        A2 = Area(staged)
        up = A2.take(2, 2, 4, P)
        gup_sb = A2.take(4 * P)

        class Scan:

            def __init__(self):
                self.gate = A2.take(2, GP, L)
                self.cum = A2.take(GP, L)
                self.pin = A2.take(GP, L)
                self.half = A2.take(GP)
                self.decay = A2.take(GP)
                self.kh = A2.take(GP, L)
                self.kt, self.bh, self.rt, self.v_in = (A2.take(GP, L) for _ in range(4))
                self.kt_z, self.bh_z, self.kh_z = (A2.take(GP, 2, L) for _ in range(3))
                self.n, self.ak = A2.take(GH, L), A2.take(GH, L)
                self.rb, self.rk = A2.take(GH, L), A2.take(GH, L)
                self.w, self.X, self.Y = (A2.take(GH, L) for _ in range(3))
                self.bk_tok = A2.take(2, GP, P)
                self.v_tok = A2.take(GP, P)
                self.u = A2.take(GH, HD)
                self.S = A2.take(NG, GP, HD)
                self.S_in = A2.take(GP, HD)
                self.S_bd = A2.take(GP, P)
                self.g = self.u

        scans = [Scan(), Scan()]
        ada_row2 = [sc.rb.rearrange("p h t -> p (h t)") for sc in scans]

        A3 = Area(staged + 6144)
        ys, yc, ysq, yr, rkr, bonus, y_rwkv = (A3.take(4, TX) for _ in range(7))
        assert (staged, A3.at) == (at_n, at_s + 7 * 4 * TX)

        A4 = Area(0, ffn_sb)
        pad = [A4.take(GRID_H + 2, GRID_W + 2) for _ in range(2)]
        pad1 = [A4.take(TX + 2) for _ in range(2)]
        conv = [A4.take(TX) for _ in range(2)]
        silu = [A4.take(TX) for _ in range(2)]

        A5 = Area(0)
        pr = A5.take(16, TX)
        aq = A5.take(4, TX)
        kz = [A5.take(HC + TX) for _ in range(2)]
        vp = A5.take(HC + TX)
        hreset, cumf = A5.take(NB, NH, HC), A5.take(NB, NH, HC)
        assert A5.at <= staged
        kh, qh = A5.take(NB, NH, HC), A5.take(NB, NH, HC)
        assert A5.at <= staged + KB * TX
        A6 = Area(staged + KB * TX)
        band_sb = A6.take(NB, 2 * HC)
        v_ch, k_ch, sT, S2, qe, ec, ke, k_tok2, v_tok2 = (A6.take(NH, HC) for _ in range(9))
        de = [A6.take(NH * HC) for _ in range(2)]
        zz = [A6.take(NH * HC) for _ in range(2)]
        q_ch = A6.take(NH, HC)
        v_st = A6.take(2, HC)
        vz = A6.take(2, 2, HC)
        pp = A6.take(NQ, 2 * HC)
        pT = A6.take(2 * NQ, HC)
        assert A6.at == at_mix
        mix = A6.take(KB, TX)
        lbv, oml = A6.take(4), A6.take(4)
        hi, nm, dsk, den, esk = (A6.take(NQ) for _ in range(5))
        sq2 = Area(0).take(4, TX)
        yr2 = pr[:, 4:8]

        sem("x_in", "ctx_in", "vec_in", "con_in", "lora_in", "ada_in0", "ada_in1", "ada_in2", "slot_in0", "slot_in1")
        sem("product", "taken")
        sem("silu_c", "ada_row", "ada_turned", "mod", "squares", "square_sum", "mean_sq", "root", "normed")
        sem("w_hi", "w_lo", "h_f", "h_hi", "act_hi", "act_lo")
        sem("head_sq", "head_sum", "head_rec", "head_root", "kk_ready", "low_tanh", "conv_ready", "bd_clean")
        sem("y_rkr", "y_rkr_mm", "centred_bonus", "g_sig", "gate_mm", "mixed")
        per_scan = ("z_mm", "z_biased", "z_tanh", "decays", "exps", "keys", "z", "rt", "v_in", "a_mm", "m_mm", "n",
                    "ak", "r_mm", "r_out", "tok_mm", "tok", "X", "Y", "y_mm", "nx_mm", "dx_mm", "w",
                    "gu_mm", "gu", "early_mm", "early", "y_out", "ds_mm", "S", "S_in", "S_bd")
        for d in range(2):
            sem(*(f"{n}{d}" for n in per_scan))
        sem("pads_clean", "gate_in", "conv", "silu", "val_free")
        sem("masks_in", "lb", "forget", "q_hg", "cum_f", "cum_scan", "f", "keys_hg", "g_silu", "pads2")
        sem("h_in", "h_d", "h_e", "h_z", "h_mm", "h_s", "h_ec", "h_qe", "h_ke", "h_ke_e", "h_kend", "h_v_mm",
            "h_v", "h_k_mm", "h_k", "h_o_mm", "h_o", "h_ds", "h_S")
        sem("a_in", "a_s_mm", "a_nm", "a_ds", "a_p", "a_es", "a_pn", "a_v_mm", "a_v", "a_t_mm", "a_t",
            "a_o_mm", "a_o")
        sem("mix2", "out")
        sem("dve_step", "act_step", "pool_step")

        class Steps:

            def __init__(self, eng, name):
                self.eng, self.sem, self.n, self.per, self.i = eng, s[name], 0, 0, 0

            def do(self, ins):
                ins.then_inc(self.sem, 1)
                self.n += 1

            def last(self):
                self.eng.wait_ge(self.sem, self.n + self.per * self.i)

            def loop(self, i, per):
                self.i, self.per, self.at = i, per, self.n

            def end(self, turns):
                assert self.n - self.at == self.per, (self.n - self.at, self.per)
                self.n = self.at + self.per * turns
                self.per = self.i = 0

        def slot_view(g, blocks=2 * KB):
            return ring[:, g % 2, 0:blocks * P].rearrange("p (k m) -> p k m", m=P)

        def slot_ready(eng, g, i):
            eng.wait_ge(s[f"slot_in{g % 2}"], 16 * ((g - FIRST) // 2) + 16 + 16 * i)

        def chunk_at(d, c, isx):
            if d == 0:
                return c * L
            return c * -L + (TT - L + TC if isx else TC - L)

        def places(eng, c, isx):
            at = [chunk_at(d, c, isx) for d in range(2)]
            return at if isinstance(c, int) else [eng.snap(a) for a in at]

        def all_turns(eng, prepare, turn, steps=None, count=0):
            prepare()
            for n in range(NCC + 1):
                turn(n, n // NG, n % NG, n >= NCC, n + 1 >= NCC)
            pairs = (NCX - 2) // 2
            with eng.Fori(0, pairs) as i:
                if steps:
                    steps.loop(i, count)
                turn(2 * i + (NCC + 1), i + NCC // NG, 1, True, True)
                turn(2 * i + (NCC + 2), i + (NCC // NG + 1), 0, True, True)
                if steps:
                    steps.end(pairs)
            turn(NC - 1, NC // NG - 1, 1, True, None)

        def pair_of(h):
            return h // 2, slice(HD * (h % 2), HD * (h % 2) + HD)

        FIRST = SLOT["W_IN"]
        TAKEN_IN = 35
        block = ctx.enter_context(nc.Block())

        @block.sync
        def _(sp):
            def load(g, i, src, at, used):
                if used is not None:
                    sp.wait_ge(s[used[0]], used[1])
                if src is w8:
                    to = ring[:, g % 2, :].rearrange("p (c n) -> p c n", c=2)
                    ap = w8[bass.ds(2 * at + 4 * i, 2)].rearrange("c p n -> p c n")
                else:
                    to = ring[:, g % 2, 0:HALF * P]
                    ap = w11[bass.ds(at + 2 * i, 1)].rearrange("c p n -> p (c n)")
                sp.dma_start(to, ap).then_inc(s[f"slot_in{g % 2}"], 16)

            def load_stage(name, src, at):
                g = SLOT[name]
                _, n, per = next(st for st in STAGES if st[0] == name)
                for u in range(min(2, n)):
                    load(g + u, 0, src, at + u, FREED[g + u - 2] if g > FIRST else None)
                if n > 3:
                    with sp.Fori(1, n // 2) as i:
                        for u in range(2):
                            by, n0 = FREED[g + u]
                            step = FREED[g + u + 2][1] - n0
                            load(g + u, i, src, at + u, (by, n0 - step + step * i))
                if n > 2 and n % 2:
                    load(g, n // 2, src, at, FREED[g + n - 3])

            sp.dma_start(v[:, :], vec).then_inc(s["vec_in"], 16)

            def load_ada(first, n, name):
                at = staged + 6144 + 2 * KB * P * first if first < 7 else 0
                sp.dma_start(arena[:, at:at + 2 * KB * P * n].rearrange("p (c n) -> p c n", c=2 * n),
                             w8[2 * first:2 * (first + n)].rearrange("c p n -> p c n")).then_inc(s[name], 16)

            load_ada(0, 2, "ada_in0")
            sp.dma_start(ctx_sb, ctxT).then_inc(s["ctx_in"], 16)
            load_ada(2, 3, "ada_in1")
            sp.dma_start(x[:, :, :], xT).then_inc(s["x_in"], 16)
            load_ada(5, 2, "ada_in2")
            load_ada(7, 1, "ada_in2")
            sp.dma_start(k_[:, :], con).then_inc(s["con_in"], 16)
            load_stage("W_IN", w8, 8)
            load_stage("W_INB", w8, 16)
            load_stage("W_INC", w8, 17)
            sp.wait_ge(s["product"], DONE[SLOT["ADA2"] - 1])
            sp.dma_start(up.rearrange("p a b c d -> p (a b c d)"), lora).then_inc(s["lora_in"], 16)
            sp.dma_start(gup_sb, gup).then_inc(s["lora_in"], 16)
            load_stage("ADA2", w8, 21)
            load_stage("W_OUT", w8, 37)
            load_stage("UP1", w8, 41)
            load_stage("DOWN1", w11, 0)
            load_stage("W_IN2", w8, 63)
            sp.wait_ge(s["normed"], 6 * KB)
            sp.dma_start(band_sb, band).then_inc(s["masks_in"], 16)
            load_stage("W_OUT2", w8, 74)
            load_stage("UP2", w8, 78)
            load_stage("DOWN2", w11, 16)
            for k in range(0, KB, 2):
                sp.wait_ge(s["normed"], 8 * KB + k + 2)
                sp.dma_start(outT[:, k:k + 2], x[:, k:k + 2, :]).then_inc(s["out"], 16)
            sp.wait_ge(s["out"], 16 * KB // 2)

        @block.tensor
        def _(pe):
            mm = nc.tensor.matmul

            def ada_rows(w, out):
                for k in range(KB):
                    last = mm(out.rearrange("r (c m) -> r c m", c=2), siluc[:, 2 * k:2 * k + 2], w[:, :, k, :],
                              start=k == 0, stop=k == KB - 1)
                last.then_inc(s["product"], 1)
                return last

            def ada_turned(row, n, out, count):
                pe.wait_ge(s["ada_row"], count)
                for m in range(n):
                    last = nc.tensor.transpose(out[:, 2 * m:2 * m + 2], row(m), ident[0:2, 0:2])
                last.then_inc(s["ada_turned"], 1)

            pe.wait_ge(s["silu_c"], 1)
            for g in range(8):
                if g in (0, 2, 5):
                    pe.wait_ge(s[f"ada_in{(0, 2, 5).index(g)}"], 16 if g < 5 else 32)
                ada_rows(ada_w[g], banks[4 + g // 2][0:2, 2 * P * (g % 2):2 * P * (g % 2) + 2 * P])

            norms = [0]

            def sum_squares(sq, bank, t):
                for k in range(KB):
                    pe.wait_ge(s["squares"], norms[0] * KB + k + 1)
                    last = mm(bank[:, 0:t], ones, sq[:, k, :], start=k == 0, stop=k == KB - 1)
                last.then_inc(s["square_sum"], 1)
                norms[0] += 1

            def of_block(a, k):
                return a[k // 4][:, k % 4, :] if isinstance(a, list) else a[:, k, :]

            def split_product(out, w, n, hi, lo, k0, first, last, when=None):
                for k in range(n):
                    if when is not None:
                        pe.wait_ge(s["normed"], when + k + 1)
                    for m, (a, b) in enumerate(((0, lo), (1, hi), (0, hi))):
                        ins = mm(out, w[:, a, k, :], of_block(b, k0 + k),
                                 start=first and k == 0 and m == 0, stop=last and k == n - 1 and m == 2)
                ins.then_inc(s["product"], 1)

            def stage(name, prods, taken, normed=None):
                n0 = PIECE[name]
                n = next(st[1] for st in STAGES if st[0] == name)
                q = len(prods)

                def body(i, u):
                    start = isinstance(i, int) and i == 0
                    for c, (blk, (hi, lo), t) in enumerate(prods):
                        pe.wait_ge(s["w_lo"], 4 * i + n0 + 2 * u + blk + 1)
                        if not start:
                            pe.wait_ge(s["taken"], 2 * q * i + taken + q * u + c + 1 - 2 * q)
                        split_product(banks[q * u + c][:, 0:t], w_of[name][blk], KB, hi, lo, 0, True, True,
                                      normed if start and u == 0 and c == 0 else None)

                if n == 1:
                    body(0, 0)
                else:
                    in_pairs(pe, n, body, peel=True)

            def ffn_up(name, used, normed):
                n0 = PIECE[name]

                def body(i, u):
                    for c in range(2):
                        pe.wait_ge(s["w_lo"], 4 * i + n0 + 2 * u + c + 1)
                        if not (isinstance(i, int) and i == 0):
                            pe.wait_ge(s[("gate_in", "val_free")[c]], 2 * i + used + u - 1)
                        first = isinstance(i, int) and i == 0 and u == 0 and c == 0
                        split_product(banks[2 * u + c][:, :], w_up[c], KB, hf_hi, hf_lo, 0, True, True,
                                      normed if first else None)

                in_pairs(pe, FB, body, peel=True)

            def ffn_down(name, taken):
                n0 = PIECE[name]
                with pe.Fori(0, KB // 2) as i:
                    for m in range(2):
                        pe.wait_ge(s["taken"], taken + 2 * i + m - 1)
                        for half in range(2):
                            pe.wait_ge(s["w_lo"], 4 * i + n0 + 2 * m + half + 1)
                            split_product(banks[m][:, :], w_down[half], HALF, act_hi, act_lo, HALF * half,
                                          half == 0, half == 1)

            pe.wait_ge(s["con_in"], 16)
            sum_squares(hc, banks[0], TC)
            sum_squares(h, banks[1], TX)
            ada_turned(lambda m: ada_row[0:2, m // 4, P * (m % 4):P * (m % 4) + P], 16, banks[3], 4)
            stage("W_IN", [(0, hx, TX), (1, hx, TX)], 0, normed=0)
            pe.wait_ge(s["taken"], 16)
            pe.wait_ge(s["normed"], 2 * KB)
            stage("W_INB", [(0, hx, TX), (1, hx, TX), (1, hc_, TC)], 16)
            pe.wait_ge(s["taken"], 19)
            stage("W_INC", [(0, hx, TX), (0, hc_, TC), (1, hx, TX), (1, hc_, TC)], 19)

            pe.wait_ge(s["taken"], TAKEN_IN)
            for j in range(NJ):
                pe.wait_ge(s["head_sq"], j + 1)
                mm(banks[2 * j][:, 0:TX], headones, kk_sq[:, j, TC:TT], start=True, stop=True)
                mm(banks[2 * j + 1][:, 0:TC], headones, kk_sq[:, j, 0:TC], start=True,
                   stop=True).then_inc(s["head_sum"], 1)

            bank = [banks[0:4], banks[4:8]]

            def heads(b):
                return b[:, :].rearrange("p (h t) -> p h t", h=GH)

            def each(d, out, lhs, rhs, name=None):
                for h in range(GH):
                    last = mm(out[:, h, :], lhs(h), rhs(h), start=True, stop=True)
                if name:
                    last.then_inc(s[f"{name}{d}"], 1)

            def of_head(a):
                return (lambda h: a[:, h // 2, h % 2, :]) if len(a.shape) == 4 else (lambda h: a[:, h, :])

            def of_pair(a):
                return lambda h: a[:, h // 2, :]

            def done(name, d, n, per=1, at=0):
                pe.wait_ge(s[f"{name}{d}"], per * n + (at or per))

            def in_x(name, d, n, per=1, at=0):
                pe.wait_ge(s[f"{name}{d}"], per * (n - NCC) + (at or per))

            def gates_in(n, g, ats):
                for d in range(2):
                    if not (isinstance(n, int) and n == 0):
                        done("ak", d, n - 1)
                    z = heads(bank[d][0])
                    for q in range(2 * GP):
                        last = mm(z[:, q, :], up[:, d, q // GP, GP * g + q % GP, :], lowT[:, bass.ds(ats[d], L)],
                                  start=True, stop=True)
                    last.then_inc(s[f"z_mm{d}"], 1)

            def score(n, d):
                sc = scans[d]
                done("z", d, n, 3, 1)
                done("keys", d, n, 3, 2)
                each(d, heads(bank[d][3]), of_head(sc.kt_z), of_pair(sc.bh), "a_mm")

            def score_t(n, d):
                sc = scans[d]
                done("z", d, n, 3, 2)
                each(d, heads(bank[d][1]), of_head(sc.bh_z), of_pair(sc.kt), "m_mm")

            def score_k(n, d):
                done("z", d, n, 3)
                done("z_biased", d, n)
                each(d, heads(bank[d][0]), of_head(scans[d].kh_z), of_pair(scans[d].kt), "m_mm")

            def score_r(n, d, k):
                sc = scans[d]
                if k == 0:
                    in_x("rt", d, n)
                else:
                    in_x("r_out", d, n, 2, 1)
                each(d, heads(bank[d][2]), of_head((sc.bh_z, sc.kh_z)[k]), of_pair(sc.rt), "r_mm")

            def turned(n, d, isx):
                sc = scans[d]
                if isx:
                    in_x("r_out", d, n, 2)
                elif not (isinstance(n, int) and n == 0):
                    done("S", d, n - 1)
                for k, src in enumerate((sc.bh, sc.kh)):
                    for j in range(GP):
                        last = nc.tensor.transpose(heads(bank[d][2])[:, GP * k + j, :], src[:, j, :], ident)
                last.then_inc(s[f"tok_mm{d}"], 1)

            def turned_v(n, d):
                done("tok", d, n, 2, 1)
                done("v_in", d, n)
                for j in range(GP):
                    last = nc.tensor.transpose(heads(bank[d][2])[:, j, :], scans[d].v_in[:, j, :], ident)
                last.then_inc(s[f"tok_mm{d}"], 1)

            def state_in(n, d, nxt):
                sc = scans[d]
                done("tok", d, n, 2)
                done("ak", d, n)
                done("S_in", d, n)
                if nxt is not None:
                    done("z_biased", d, n + 1)
                out = bank[d][0][:, 0:GH * HD].rearrange("p (h f) -> p h f", h=GH)
                for h in range(GH):
                    j, r = pair_of(h)
                    mm(out[:, h, :], sc.kt_z[:, j, h % 2, :], sc.S_in[:, j, :], start=True, stop=False)
                    last = mm(out[:, h, :], sc.ak[:, h, :], sc.v_tok[:, j, r], start=False, stop=True)
                last.then_inc(s[f"gu_mm{d}"], 1)

            def early_out(n, d):
                sc = scans[d]
                done("tok", d, n, 2)
                in_x("S_bd", d, n)
                for j in range(GP):
                    y = heads(bank[d][2])[:, j, :]
                    mm(y, sc.S_bd[:, j, :], sc.rt[:, j, :], start=True, stop=False)
                    for q in range(2):
                        r = slice(HD * q, HD * q + HD)
                        last = mm(y[r], sc.v_tok[:, j, r], sc.rk[:, 2 * j + q, :], start=False, stop=True)
                last.then_inc(s[f"early_mm{d}"], 1)

            def nx(n, d, l):
                done("X", d, n, LEVELS, l - 1)
                if l == 2:
                    done("n", d, n)
                each(d, heads(bank[d][3]), of_head(scans[d].n), of_head(scans[d].X), "nx_mm")

            def dx(n, d, l):
                done("w", d, n, LEVELS - 1, l - 1)
                done("Y", d, n, LEVELS, l - 1)
                each(d, heads(bank[d][3]), of_head(scans[d].Y), of_head(scans[d].w), "dx_mm")

            def turn_x(n, d, l):
                done("X", d, n, LEVELS, l)
                if l == 1:
                    done("n", d, n)
                for h in range(GH):
                    last = nc.tensor.transpose(heads(bank[d][1])[:, h, :], scans[d].X[:, h, :], ident)
                last.then_inc(s[f"y_mm{d}"], 1)

            def updates(n, d):
                sc = scans[d]
                done("Y", d, n, LEVELS)
                done("gu", d, n, 2, 1)
                each(d, bank[d][0][:, 0:GH * HD].rearrange("p (h f) -> p h f", h=GH), of_head(sc.Y),
                     of_head(sc.g), "gu_mm")

            def results(n, d, cur, nxt):
                sc = scans[d]
                done("gu", d, n, 2)
                if cur:
                    in_x("early", d, n)
                    for h in range(GH):
                        j, r = pair_of(h)
                        last = mm(heads(bank[d][2])[r, j, :], sc.u[:, h, :], sc.rb[:, h, :], start=True, stop=True)
                elif d == 0:
                    pe.wait_ge(s["mod"], 2 + n)
                if nxt is not None:
                    ds = bank[d][2][:, 256:256 + GP * HD].rearrange("p (j f) -> p j f", j=GP)
                    for h in range(GH):
                        j, r = pair_of(h)
                        mm(ds[r, j, :], sc.bk_tok[:, 0, j, r], sc.u[:, h, :], start=True, stop=False)
                        last = mm(ds[r, j, :], sc.bk_tok[:, 1, j, r], sc.v_tok[:, j, r], start=False, stop=True)
                last.then_inc(s[f"ds_mm{d}"], 1)

            def ada_terms(n, u):
                done("tok", u // 2, n, 2)
                g = SLOT["ADA2"] + 4 * n + u
                slot_ready(pe, g, 0)
                ada_rows(slot_view(g).rearrange("p (c k) m -> p c k m", c=2),
                         bank[u // 2][2][0:2, 2 * P * (u % 2):2 * P * (u % 2) + 2 * P])

            def prepare():
                gates_in(0, 0, places(pe, 0, False))
                for d in range(2):
                    score(0, d)
                    score_t(0, d)
                for d in range(2):
                    score_k(0, d)

            def turn(n, c, g, cur, nxt):
                ats = places(pe, c + g, nxt)
                turn_x(n, 0, 1)
                for l in range(2, LEVELS + 1):
                    nx(n, 0, l)
                    turn_x(n, 1, l - 1)
                    if l == 2 and nxt is not None:
                        gates_in(n + 1, 1 - g, ats)
                    for d in range(2):
                        if l == 2:
                            turned(n, d, cur)
                        elif l == 3:
                            turned_v(n, d)
                        elif l == 4:
                            state_in(n, d, nxt)
                        elif l == 5 and cur:
                            early_out(n, d)
                    dx(n, 0, l)
                    if not cur and l >= 4:
                        ada_terms(n, l - 4)
                    nx(n, 1, l)
                    turn_x(n, 0, l)
                    dx(n, 1, l)
                if nxt is not None:
                    score(n + 1, 0)
                turn_x(n, 1, LEVELS)
                updates(n, 0)
                if not cur:
                    ada_turned(lambda m: ada_row2[m // 4][0:2, P * (m % 4):P * (m % 4) + P], 8, bank[0][2],
                               6 + 2 * n)
                if nxt is not None:
                    score_t(n + 1, 0)
                    score(n + 1, 1)
                updates(n, 1)
                if nxt is not None:
                    score_t(n + 1, 1)
                for d in range(2):
                    results(n, d, cur, nxt)
                    if nxt is not None:
                        score_k(n + 1, d)
                if nxt:
                    for k in range(2):
                        for d in range(2):
                            if k == 0:
                                done("S", d, n)
                            score_r(n + 1, d, k)

            pe.wait_ge(s["kk_ready"], NJ)
            pe.wait_ge(s["lora_in"], 32)
            pe.wait_ge(s["low_tanh"], 1)
            pe.wait_ge(s["bd_clean"], 2)
            all_turns(pe, prepare, turn)

            for j in range(NJ):
                pe.wait_ge(s["y_rkr"], 2 * j + 1)
                mm(banks[j][:, :], headones, ys[:, j, :], start=True, stop=True).then_inc(s["y_rkr_mm"], 1)
                pe.wait_ge(s["y_rkr"], 2 * j + 2)
                mm(banks[4 + j][:, :], headones, rkr[:, j, :], start=True, stop=True).then_inc(s["y_rkr_mm"], 1)
            for j in range(NJ):
                pe.wait_ge(s["head_sq"], NJ + j + 1)
                mm(banks[j][:, :], headones, ysq[:, j, :], start=True, stop=True).then_inc(s["head_sum"], 1)
            pe.wait_ge(s["g_sig"], 1)
            for j in range(NJ):
                pe.wait_ge(s["centred_bonus"], 2 * j + 2)
                mm(banks[4 + j][:, :], gup_sb[:, j * P:(j + 1) * P], g_lo, start=True,
                   stop=True).then_inc(s["gate_mm"], 1)
            pe.wait_ge(s["normed"], 3 * KB)
            stage("W_OUT", [(c, ([ycv[0], yrw[0]], [ycv[1], yrw[1]]), TX) for c in range(2)], 35)
            sum_squares(hf, banks[6], TX)
            ffn_up("UP1", 0, 3 * KB)
            pe.wait_ge(s["act_lo"], FB)
            ffn_down("DOWN1", 43)
            sum_squares(hf, banks[6], TX)

            sum_squares(h, banks[7], TX)
            stage("W_IN2", [(0, h2, TX), (1, h2, TX)], 51, normed=5 * KB)
            pe.wait_ge(s["taken"], 51 + 22)

            def mixer2(i):
                first = isinstance(i, int) and i == 0

                def heads(b):
                    return b[:, :].rearrange("p (h t) -> p h t", h=NH)

                pe.wait_ge(s["a_in"], 2 * i + 1)
                if not first:
                    pe.wait_ge(s["a_o"], i)
                for j in range(4):
                    for g in range(2):
                        last = mm(banks[4 + j][:, 256 * g:256 * g + 256], q_ch[:, j, :],
                                  kz[g][:, bass.ds(HC * i, 2 * HC)], start=True, stop=True)
                last.then_inc(s["a_s_mm"], 1)
                pe.wait_ge(s["h_in"], 2 * i + 2)
                if not first:
                    pe.wait_ge(s["h_k"], i)
                for hd in range(NH):
                    last = nc.tensor.transpose(heads(banks[2])[:, hd, :], v_ch[:, hd, :], ident)
                last.then_inc(s["h_v_mm"], 1)
                for l in range(1, HLEV + 2):
                    b = banks[l % 2]
                    if not first or l > 2:
                        pe.wait_ge(s["h_s"], 8 * i + l - 2)
                    if l <= HLEV:
                        pe.wait_ge(s["h_z"], 2 * HLEV * i + 2 * l)
                    for hd in range(NH):
                        zl = zz[l % 2].rearrange("p (h t) -> p h t", h=NH)
                        if l <= HLEV:
                            last = mm(heads(b)[:, hd, :], zl[:, hd, :], zl[:, hd, :], start=True, stop=True)
                        else:
                            last = mm(heads(b)[:, hd, :], k_ch[:, hd, :], q2d(i, hd), start=True, stop=True)
                    last.then_inc(s["h_mm"], 1)
                pe.wait_ge(s["h_kend"], i + 1)
                pe.wait_ge(s["h_v"], i + 1)
                for hd in range(NH):
                    last = nc.tensor.transpose(heads(banks[2])[:, hd, :], ke[:, hd, :], ident)
                last.then_inc(s["h_k_mm"], 1)
                pe.wait_ge(s["h_s"], 8 * i + 8)
                pe.wait_ge(s["h_qe"], i + 1)
                if not first:
                    pe.wait_ge(s["h_S"], i)
                for hd in range(NH):
                    mm(heads(banks[3])[:, hd, :], v_tok2[:, hd, :], sT[:, hd, :], start=True, stop=False)
                    last = mm(heads(banks[3])[:, hd, :], S2[:, hd, :], qe[:, hd, :], start=False, stop=True)
                last.then_inc(s["h_o_mm"], 1)
                pe.wait_ge(s["a_pn"], i + 1)
                for b in range(4):
                    for c in range(4):
                        last = nc.tensor.transpose(heads(banks[4 + b])[:, c, :],
                                                   pp[:, 2 * b + c // 2, HC * (c % 2):HC * (c % 2) + HC], ident)
                    last.then_inc(s["a_t_mm"], 1)
                pe.wait_ge(s["h_k"], i + 1)
                pe.wait_ge(s["h_o"], i + 1)
                for hd in range(NH):
                    last = mm(heads(banks[3])[:, hd, :], k_tok2[:, hd, :], v_tok2[:, hd, :], start=True, stop=True)
                last.then_inc(s["h_ds"], 1)
                pe.wait_ge(s["a_in"], 2 * i + 2)
                pe.wait_ge(s["a_t"], 4 * i + 4)
                for c in range(2):
                    last = nc.tensor.transpose(banks[4][:, HC * c:HC * c + HC], v_st[:, c, :], ident)
                last.then_inc(s["a_v_mm"], 1)
                pe.wait_ge(s["a_v"], 2 * i + 2)
                for j in range(4):
                    for n, (g, c) in enumerate(((0, 0), (0, 1), (1, 0), (1, 1))):
                        last = mm(heads(banks[5])[:, j, :], vz[:, g, c, :], pT[:, 4 * j + 2 * g + c, :],
                                  start=n == 0, stop=n == 3)
                last.then_inc(s["a_o_mm"], 1)

            def q2d(i, hd):
                return qh.rearrange("p n h t -> p (n h t)")[:, bass.ds(NH * HC * i + HC * hd, HC)]

            pe.wait_ge(s["q_hg"], NH)
            pe.wait_ge(s["pads2"], 6)
            mixer2(0)
            with pe.Fori(1, NB) as i:
                mixer2(i)
            pe.wait_ge(s["h_S"], NB)
            for hd in range(NH):
                pe.wait_ge(s["head_sq"], 2 * NJ + hd + 1)
                mm(banks[hd][:, :], ones, sq2[:, hd, :], start=True, stop=True).then_inc(s["head_sum"], 1)
            pe.wait_ge(s["normed"], 7 * KB)
            stage("W_OUT2", [(c, mx, TX) for c in range(2)], 73)
            sum_squares(hf, banks[6], TX)

            ffn_up("UP2", FB, 7 * KB)
            pe.wait_ge(s["act_lo"], 2 * FB)
            ffn_down("DOWN2", 81)
            sum_squares(hf, banks[6], TX)

        @block.scalar
        def _(se):
            act_f = nc.scalar.activation
            steps = Steps(se, "act_step")
            se.wait_ge(s["vec_in"], 16)
            act_f(siluc[:, :], vcol("cs"), ACT.Silu).then_inc(s["silu_c"], 1)

            def squares(src, to, after=None):
                for k in range(KB):
                    if after:
                        se.wait_ge(s[after[0]], after[1] + k + 1)
                    act_f(to[:, k, :], src[:, k, :], ACT.Square).then_inc(s["squares"], 1)

            roots = [0]

            def root(r):
                roots[0] += 1
                se.wait_ge(s["mean_sq"], roots[0])
                act_f(r, r, ACT.Sqrt).then_inc(s["root"], 1)

            def high(w, g, blocks, at, used, i, step):
                slot_ready(se, g, i)
                se.wait_ge(s["product"], used + step * i)
                act_f(w[:, 0], slot_view(g)[:, at:at + blocks, :], ACT.Copy).then_inc(s["w_hi"], 1)

            def split_up(name, i, u, c):
                p0 = DONE[SLOT[name] - 1]
                used = p0 if isinstance(i, int) and i == 0 and u == 0 else p0 + 2 * u - 2 + c + 1
                high(w_of[name][c], SLOT[name] + u, KB, c * KB, used, i, 4)

            def split_down(name, i, m, half):
                p0 = DONE[SLOT[name] - 1]
                used = p0 if isinstance(i, int) and i == 0 and m == 0 else p0 + 2 * m + half - 1
                g = SLOT[name] + 2 * m + half
                slot_ready(se, g, 2 * i)
                se.wait_ge(s["product"], used + 4 * i)
                act_f(w_down[half][:, 0], slot_view(g, HALF), ACT.Copy).then_inc(s["w_hi"], 1)

            def split_first(name):
                for c in range(2):
                    split_up(name, 0, 0, c)

            split_n = [0]

            def squares_split(name, taken):
                for j in range(4):
                    for c in range(2):
                        if j < 3:
                            split_up(name, (j + 1) // 2, (j + 1) % 2, c)
                        se.wait_ge(s["taken"], taken + 2 * j + c + 1)
                        act_f(hf[:, 2 * j + c, :], x[:, 2 * j + c, :], ACT.Square).then_inc(s["squares"], 1)

            split_n = [0]

            def split_input(to, src, ready, count):
                for k, (a, b) in enumerate(zip(to, src)):
                    se.wait_ge(s[ready], count + k + 1)
                    act_f(a, b, ACT.Copy).then_inc(s["h_hi"], 1)

            def split_normed(shift, to=hf_hi, src=hf):
                for k in range(KB):
                    se.wait_ge(s["h_f"], split_n[0] + k + 1)
                    bias = 0.0 if shift is None else shift[:, k:k + 1]
                    act_f(to[:, k, :], src[:, k, :], ACT.Copy if shift is None else ACT.Identity,
                          bias=bias).then_inc(s["h_hi"], 1)
                split_n[0] += KB

            se.wait_ge(s["ctx_in"], 16)
            squares(ctx_sb, hc)
            se.wait_ge(s["x_in"], 16)
            squares(x, h)
            for b in range(4):
                se.wait_ge(s["product"], 2 * b + 2)
                act_f(ada_row[0:2, b, :], banks[4 + b][0:2, :], ACT.Copy).then_inc(s["ada_row"], 1)
            split_first("W_IN")
            root(rstd_c[:, :])
            root(rstd[:, :])
            split_normed(mod[:, 0:8, 0], hx[0], h)
            split_normed(mod[:, 0:8, 1], hc_[0], hc)

            def take(to, bank, product, **kw):
                se.wait_ge(s["product"], product)
                act_f(to, bank, ACT.Copy, **kw).then_inc(s["taken"], 1)

            p_in = DONE[SLOT["W_IN"] - 1]

            def next_high(name, i, u, c, used, step):
                g = SLOT[name] + u + 1
                high(w_of[name][c], g, KB, c * KB, used, i, step)

            def take_x(i, u):
                for c in range(2):
                    m = 4 * i + 2 * u + c
                    next_high("W_IN", i, u, c, p_in + 2 * u + c + 1, 4)
                    take(px[:, m, :] if isinstance(i, int) else px[:, bass.ds(m, 1), :], banks[2 * u + c][:, :],
                         p_in + 4 * i + 2 * u + c + 1)

            in_pairs(se, 8, take_x)
            next_high("W_INB", 0, 0, 0, p_in + 17, 0)
            take(px[:, 16, :], banks[0][:, :], p_in + 17)
            next_high("W_INB", 0, 0, 1, p_in + 19, 0)
            take(kv[:, 0, TC:TT], banks[1][:, :], p_in + 18)
            take(kv[:, 0, 0:TC], banks[2][:, 0:TC], p_in + 19)

            def take_xc(i, u):
                for c in range(4):
                    m = 1 + 4 * i + 2 * u + c // 2
                    to = kv[:, bass.ds(m, 1), TC:TT] if c % 2 == 0 else kv[:, bass.ds(m, 1), 0:TC]
                    if c % 2 == 0 and not (isinstance(i, int) and i == 1 and u == 1):
                        next_high("W_INC", i, u, c // 2, p_in + 19 + 4 * u + c + 2, 8)
                    take(to, banks[4 * u + c][:, 0:TX if c % 2 == 0 else TC], p_in + 20 + 8 * i + 4 * u + c)

            for i in range(2):
                for u in range(2):
                    take_xc(i, u)

            se.wait_ge(s["taken"], TAKEN_IN)
            for j in range(NJ):
                act_f(kk_sq[:, j, :], kT[:, j, :], ACT.Square, scale=vcol("kk")[:, j:j + 1]).then_inc(s["head_sq"], 1)
            act_f(lowT[0:64, :], lowT[0:64, :], ACT.Tanh).then_inc(s["low_tanh"], 1)
            for j in range(NJ):
                se.wait_ge(s["head_rec"], j + 1)
                act_f(kk[:, j, :], kk[:, j, :], ACT.Sqrt).then_inc(s["head_root"], 1)

            bank = [banks[0:4], banks[4:8]]

            def heads(b):
                return b[:, :].rearrange("p (h t) -> p h t", h=GH)

            def done(name, d, n, per=1, at=0):
                se.wait_ge(s[f"{name}{d}"], per * n + (at or per))

            def copy(to, src, name, d, scale=1.0):
                act_f(to, src, ACT.Copy, scale=scale).then_inc(s[f"{name}{d}"], 1)

            def gate_tanh(n):
                for d, sc in enumerate(scans):
                    done("z_biased", d, n)
                    act_f(sc.gate, sc.gate, ACT.Tanh, scale=0.5).then_inc(s[f"z_tanh{d}"], 1)

            def decay_exps(n):
                for d, sc in enumerate(scans):
                    done("decays", d, n)
                    act_f(sc.gate[:, 0], sc.gate[:, 0], ACT.Exp).then_inc(s[f"exps{d}"], 1)
                    act_f(sc.pin, sc.cum, ACT.Exp).then_inc(s[f"exps{d}"], 1)
                    done("exps", d, n, 3, 2)
                    act_f(sc.cum, sc.cum, ACT.Exp, scale=-1.0).then_inc(s[f"exps{d}"], 1)

            def scores_out(n, d):
                done("m_mm", d, n, 2, 1)
                copy(scans[d].n, heads(bank[d][1]), "n", d, -1.0)

            def x_turned(n, d, l):
                done("y_mm", d, n, LEVELS, l)
                copy(scans[d].Y, heads(bank[d][1]), "Y", d)

            def values_in(n, g, at):
                for d, sc in enumerate(scans):
                    if not (isinstance(n, int) and n == 0):
                        done("tok_mm", d, n - 1, 2)
                    copy(sc.v_in, vT[:, GP * g:GP * g + GP, bass.ds(at[d], L)], "v_in", d)

            def tok_out(n, d, k):
                sc = scans[d]
                done("tok_mm", d, n, 2, k + 1)
                if k == 0:
                    copy(sc.bk_tok.rearrange("p a j f -> p (a j) f"), heads(bank[d][2]), "tok", d)
                else:
                    copy(sc.v_tok, heads(bank[d][2])[:, 0:GP, :], "tok", d)

            def u_view(d):
                return bank[d][0][:, 0:GH * HD].rearrange("p (h f) -> p h f", h=GH)

            def prepare():
                values_in(0, 0, places(se, 0, False))
                gate_tanh(0)
                decay_exps(0)
                for d in range(2):
                    scores_out(0, d)

            def turn(n, c, g, cur, nxt):
                at = places(se, c, cur)
                at_next = places(se, c + g, nxt)
                x_turned(n, 0, 1)
                for l in range(2, LEVELS + 1):
                    x_turned(n, 1, l - 1)
                    for d, sc in enumerate(scans):
                        if l == 2:
                            tok_out(n, d, 0)
                        elif l == 3:
                            tok_out(n, d, 1)
                        elif l == 4:
                            done("gu_mm", d, n, 2, 1)
                            copy(sc.g, u_view(d), "gu", d, -1.0)
                        elif l == 5 and cur:
                            se.wait_ge(s[f"early_mm{d}"], n - NCC + 1)
                            copy(y_dir[d][:, GP * g:GP * g + GP, bass.ds(at[d] - TC, L)],
                                 heads(bank[d][2])[:, 0:GP, :], "early", d)
                    if not cur and l in (6, 7):
                        se.wait_ge(s["product"], DONE[SLOT["ADA2"] + 4 * n + 2 * (l - 6) + 1])
                        act_f(ada_row2[l - 6][0:2, :], bank[l - 6][2][0:2, :], ACT.Copy).then_inc(s["ada_row"], 1)
                    if nxt is not None:
                        if l == 2:
                            gate_tanh(n + 1)
                        elif l == 5:
                            decay_exps(n + 1)
                        elif l == 6:
                            values_in(n + 1, 1 - g, at_next)
                    x_turned(n, 0, l)
                x_turned(n, 1, LEVELS)
                for d, sc in enumerate(scans):
                    done("gu_mm", d, n, 2)
                    copy(sc.u, u_view(d), "gu", d)
                    if nxt is not None:
                        scores_out(n + 1, d)

            se.wait_ge(s["bd_clean"], 2)
            all_turns(se, prepare, turn)

            for d in range(2):
                se.wait_ge(s[f"y_out{d}"], NCX)
            act_f(g_lo, g_lo, ACT.Sigmoid).then_inc(s["g_sig"], 1)
            se.wait_ge(s["conv_ready"], 1)
            for j in range(4):
                act_f(ycv[0][:, j, :], y_conv[:, j, :], ACT.Copy).then_inc(s["h_hi"], 1)
            for j in range(NJ):
                se.wait_ge(s["centred_bonus"], 2 * j + 1)
                act_f(ysq[:, j, :], yc[:, j, :], ACT.Square).then_inc(s["head_sq"], 1)
            for j in range(NJ):
                se.wait_ge(s["head_rec"], NJ + j + 1)
                act_f(yr[:, j, :], yr[:, j, :], ACT.Sqrt).then_inc(s["head_root"], 1)
            split_first("W_OUT")
            split_input([yrw[0][:, j, :] for j in range(NJ)], [y_rwkv[:, j, :] for j in range(NJ)], "mixed", 0)
            squares_split("W_OUT", 35)
            split_first("UP1")
            root(rstd[:, :])
            split_normed(mod[:, 3 * KB:4 * KB, 0])

            def ffn(first, up, down, taken, name):
                p0 = DONE[SLOT[up] - 1]

                def act_high(j):
                    se.wait_ge(s["val_free"], first + j + 1)
                    return act_hi[:, bass.ds(j, 1), :].rearrange("p a t -> p (a t)")

                def body(i, u, last=False):
                    start = isinstance(i, int) and i == 0
                    if not (start and first == 0):
                        se.wait_ge(s["conv"], first + 2 * i + u - 1)
                    se.wait_ge(s["product"], p0 + 4 * i + 2 * u + 1)
                    if name == 1:
                        act_f(pad[u][:, 1:1 + GRID_H, 1:1 + GRID_W],
                              banks[2 * u][:, :].rearrange("p (y x) -> p y x", y=GRID_H),
                              ACT.Copy).then_inc(s["gate_in"], 1)
                    else:
                        act_f(pad1[u][:, 2:2 + TX], banks[2 * u][:, :], ACT.Copy).then_inc(s["gate_in"], 1)
                    if not last:
                        split_up(up, i + u, 1 - u, 0)
                    if not (start and u == 0):
                        j = 2 * i + u - 1
                        act_f(act_high(j), silu[1 - u], ACT.Copy).then_inc(s["act_hi"], 1)
                    if not last:
                        split_up(up, i + u, 1 - u, 1)
                    se.wait_ge(s["conv"], first + 2 * i + u + 1)
                    if not start:
                        se.wait_ge(s["act_lo"], first + 2 * i + u - 1)
                    act_f(silu[u], conv[u], ACT.Silu).then_inc(s["silu"], 1)
                    if last:
                        act_f(act_high(FB - 1), silu[u], ACT.Copy).then_inc(s["act_hi"], 1)

                se.wait_ge(s["pads_clean"], 2 * name)
                body(0, 0)
                body(0, 1)
                with se.Fori(1, FB // 2 - 1) as i:
                    body(i, 0)
                    body(i, 1)
                body(FB // 2 - 1, 0)
                body(FB // 2 - 1, 1, last=True)

                def tile(i, m, last=False):
                    if not last:
                        split_down(down, i + m, 1 - m, 0)
                        split_down(down, i + m, 1 - m, 1)
                    se.wait_ge(s["taken"], taken + 2 * i + m + 1)
                    mt = bass.ds(2 * i + m, 1)
                    act_f(hf[:, mt, :], x[:, mt, :], ACT.Square).then_inc(s["squares"], 1)

                split_down(down, 0, 0, 0)
                split_down(down, 0, 0, 1)
                with se.Fori(0, KB // 2 - 1) as i:
                    tile(i, 0)
                    tile(i, 1)
                tile(KB // 2 - 1, 0)
                tile(KB // 2 - 1, 1, last=True)

            ffn(0, "UP1", "DOWN1", 43, 1)
            root(rstd[:, :])

            squares(x, h, ("normed", 4 * KB))
            split_first("W_IN2")
            root(rstd[:, :])
            split_normed(None, h2[0], h)
            se.wait_ge(s["lb"], 1)
            act_f(lbv, lbv, ACT.Sigmoid).then_inc(s["forget"], 1)
            p_in2 = DONE[SLOT["W_IN2"] - 1]

            def take2(i, u):
                for c in range(2):
                    m = 4 * i + 2 * u + c
                    next_high("W_IN2", i, u, c, p_in2 + 2 * u + c + 1, 4)
                    take(pr[:, m, :] if isinstance(i, int) else pr[:, bass.ds(m, 1), :], banks[2 * u + c][:, :],
                         p_in2 + 4 * i + 2 * u + c + 1)

            in_pairs(se, 8, take2)
            bias = vcol("batt")
            for j in range(4):
                next_high("W_IN2", 4, j // 2, j % 2, p_in2 + j + 1, 4)
                act_f(aq[:, j, :], banks[j][:, :], ACT.Identity, bias=bias[:, j:j + 1]).then_inc(s["taken"], 1)
            se.wait_ge(s["pads2"], 4)
            se.wait_ge(s["product"], p_in2 + 21)
            act_f(kz[0][0:64, HC:], banks[0][0:64, :], ACT.Identity, bias=bias[0:64, 4:5]).then_inc(s["act_step"], 1)
            act_f(kz[1][64:128, HC:], banks[0][64:128, :], ACT.Identity,
                  bias=bias[64:128, 4:5]).then_inc(s["taken"], 1)
            se.wait_ge(s["product"], p_in2 + 22)
            act_f(vp[:, HC:], banks[1][:, :], ACT.Identity, bias=bias[:, 5:6]).then_inc(s["taken"], 1)
            for hd in range(NH):
                act_f(pr[:, 4 + hd, :], pr[:, 4 + hd, :], ACT.Sigmoid).then_inc(s["forget"], 1)
            for hd in range(NH):
                act_f(pr[:, 12 + hd, :], pr[:, 12 + hd, :], ACT.Silu).then_inc(s["g_silu"], 1)
            for hd in range(NH):
                se.wait_ge(s["keys_hg"], hd + 1)
                act_f(cumf[:, :, hd, :], cumf[:, :, hd, :], ACT.Ln).then_inc(s["cum_f"], 1)

            def mixer2(i):
                first = isinstance(i, int) and i == 0
                chunk = bass.ds(NH * HC * i, NH * HC)
                cf = cumf.rearrange("p n h t -> p (n h t)")[:, chunk]

                def heads(b):
                    return b[:, :].rearrange("p (h t) -> p h t", h=NH)

                if not first:
                    se.wait_ge(s["h_S"], i)
                act_f(ec.rearrange("p h t -> p (h t)"), cf, ACT.Exp).then_inc(s["h_ec"], 1)
                se.wait_ge(s["h_v_mm"], i + 1)
                act_f(v_tok2, heads(banks[2]), ACT.Copy).then_inc(s["h_v"], 1)

                def level(l):
                    se.wait_ge(s["h_d"], 2 * HLEV * i + 2 * l)
                    act_f(de[l % 2], de[l % 2], ACT.Exp).then_inc(s["h_e"], 1)

                level(1)
                level(2)
                se.wait_ge(s["a_ds"], i + 1)
                for q in range(NQ):
                    act_f(pp[:, q, :], pp[:, q, :], ACT.Exp, bias=nm[:, q:q + 1],
                          accum_out=den[:, q:q + 1]).then_inc(s["a_p"], 1)
                act_f(esk, dsk, ACT.Exp).then_inc(s["a_es"], 1)
                for l in range(3, HLEV + 1):
                    level(l)
                se.wait_ge(s["h_ke"], i + 1)
                act_f(ke, ke, ACT.Exp).then_inc(s["h_ke_e"], 1)
                se.wait_ge(s["h_k_mm"], i + 1)
                act_f(k_tok2, heads(banks[2]), ACT.Copy).then_inc(s["h_k"], 1)
                se.wait_ge(s["h_o_mm"], i + 1)
                act_f(mix[:, 0:4, bass.ds(HC * i, HC)], heads(banks[3]), ACT.Copy).then_inc(s["h_o"], 1)
                for b in range(4):
                    se.wait_ge(s["a_t_mm"], 4 * i + b + 1)
                    act_f(pT[:, 4 * b:4 * b + 4, :], heads(banks[4 + b]), ACT.Copy).then_inc(s["a_t"], 1)
                se.wait_ge(s["a_v_mm"], i + 1)
                for g in range(2):
                    act_f(vz[:, g, :, 64 * g:64 * g + 64],
                          banks[4][:, 0:2 * HC].rearrange("p (c f) -> p c f", c=2)[:, :, 64 * g:64 * g + 64],
                          ACT.Copy).then_inc(s["a_v"], 1)
                se.wait_ge(s["a_o_mm"], i + 1)
                act_f(mix[:, 4:8, bass.ds(HC * i, HC)], heads(banks[5]), ACT.Copy).then_inc(s["a_o"], 1)

            se.wait_ge(s["cum_scan"], 1)
            mixer2(0)
            with se.Fori(1, NB) as i:
                mixer2(i)
            se.wait_ge(s["h_o"], NB)
            for hd in range(NH):
                act_f(sq2[:, hd, :], mix[:, hd, :], ACT.Square).then_inc(s["head_sq"], 1)
            for hd in range(NH):
                se.wait_ge(s["head_rec"], 2 * NJ + hd + 1)
                act_f(yr2[:, hd, :], yr2[:, hd, :], ACT.Sqrt).then_inc(s["head_root"], 1)
            split_first("W_OUT2")
            for k in range(4):
                act_f(mx[0][:, 4 + k, :], mix[:, 4 + k, :], ACT.Copy).then_inc(s["h_hi"], 1)
            split_input([mx[0][:, k, :] for k in range(4)], [mix[:, k, :] for k in range(4)], "mix2", 0)
            squares_split("W_OUT2", 73)
            split_first("UP2")
            root(rstd[:, :])
            split_normed(None)
            ffn(FB, "UP2", "DOWN2", 81, 2)
            root(rstd[:, :])

        @block.gpsimd
        def _(pool):
            pool.wait_ge(s["head_sum"], NJ)
            for sc in scans:
                nc.gpsimd.memset(sc.S, 0.0).then_inc(s["bd_clean"], 1)

            def done(name, d, n, per=1, at=0):
                pool.wait_ge(s[f"{name}{d}"], per * n + (at or per))

            def apart(to, src, name, w):
                nc.gpsimd.tensor_tensor(to, src.unsqueeze(2).broadcast_to([P, GP, 2, w]),
                                        headones[:, ::HD].unsqueeze(1).unsqueeze(3).broadcast_to([P, GP, 2, w]),
                                        ALU.mult).then_inc(s[name], 1)

            def heads_apart(n):
                for k in range(3):
                    for d, sc in enumerate(scans):
                        done("keys", d, n, 3, k + 1)
                        if k == 0 and not (isinstance(n, int) and n == 0):
                            done("gu_mm", d, n - 1, 2, 1)
                        a, b = ((sc.kt_z, sc.kt), (sc.bh_z, sc.bh), (sc.kh_z, sc.kh))[k]
                        apart(a, b, f"z{d}", L)

            def prepare():
                heads_apart(0)

            def turn(n, c, g, cur, nxt):
                if nxt is not None:
                    heads_apart(n + 1)
                if nxt:
                    for d, sc in enumerate(scans):
                        done("S_in", d, n + 1)
                        if cur:
                            pool.wait_ge(s[f"early_mm{d}"], n - NCC + 1)
                        apart(sc.S_bd.rearrange("p j (q f) -> p j q f", q=2), sc.S_in, f"S_bd{d}", HD)

            all_turns(pool, prepare, turn)
            pool.wait_ge(s["mixed"], NJ)
            for a in pad:
                nc.gpsimd.memset(a, 0.0).then_inc(s["pads_clean"], 1)

            def act_low(first):
                with nc.gpsimd.Fori(0, FB // 2) as i:
                    for u in range(2):
                        j = 2 * i + u
                        pool.wait_ge(s["act_hi"], first + 1 + j)
                        nc.gpsimd.tensor_tensor(act_lo[:, bass.ds(j, 1), :].rearrange("p a t -> p (a t)"), silu[u], act_hi[:, bass.ds(j, 1), :].rearrange("p a t -> p (a t)"),
                            ALU.subtract).then_inc(s["act_lo"], 1)

            act_low(0)
            pool.wait_ge(s["taken"], 51)
            pool.wait_ge(s["square_sum"], 4)
            nc.gpsimd.memset(hreset, 1.0).then_inc(s["pool_step"], 1)
            pool.wait_ge(s["pool_step"], 1)
            nc.gpsimd.memset(hreset[:, :, :, 0:1], 0.0).then_inc(s["pads2"], 1)
            for a in (kz[0], kz[1], vp[:, 0:HC]):
                nc.gpsimd.memset(a, 0.0).then_inc(s["pads2"], 1)
            nc.gpsimd.memset(vz, 0.0).then_inc(s["pads2"], 1)
            nc.gpsimd.memset(S2, 0.0).then_inc(s["pads2"], 1)

            def mixer2(i):
                first = isinstance(i, int) and i == 0
                if not first:
                    pool.wait_ge(s["a_s_mm"], i)
                nc.gpsimd.tensor_copy(q_ch, aq[:, :, bass.ds(HC * i, HC)]).then_inc(s["a_in"], 1)
                if not first:
                    pool.wait_ge(s["h_mm"], 8 * i)
                    pool.wait_ge(s["h_v_mm"], i)
                nc.gpsimd.tensor_copy(v_ch, pr[:, 8:12, bass.ds(HC * i, HC)]).then_inc(s["h_in"], 1)
                nc.gpsimd.tensor_copy(k_ch.rearrange("p h t -> p (h t)"),
                                      kh.rearrange("p n h t -> p (n h t)")[:, bass.ds(NH * HC * i, NH * HC)]
                                      ).then_inc(s["h_in"], 1)
                if not first:
                    pool.wait_ge(s["a_v_mm"], i)
                nc.gpsimd.tensor_copy(v_st.rearrange("p c t -> p (c t)"),
                                      vp[:, bass.ds(HC * i, 2 * HC)]).then_inc(s["a_in"], 1)

            pool.wait_ge(s["taken"], 73)
            pool.wait_ge(s["keys_hg"], NH)
            mixer2(0)
            with pool.Fori(1, NB) as i:
                mixer2(i)
            pool.wait_ge(s["taken"], 81)
            for a in pad1:
                nc.gpsimd.memset(a[:, 0:2], 0.0).then_inc(s["pads_clean"], 1)
            act_low(FB)

        @block.vector
        def _(dve):
            V = nc.vector
            steps = Steps(dve, "dve_step")
            norms = [0]

            def mean_square(r, bank, t):
                norms[0] += 1
                dve.wait_ge(s["square_sum"], norms[0])
                steps.do(V.tensor_scalar(r, bank[:, 0:t], 1.0 / D, EPS, ALU.mult, ALU.add))
                steps.last()
                V.reciprocal(r, r).then_inc(s["mean_sq"], 1)

            def norm(to, src, r, gain):
                rooted()
                for k in range(KB):
                    V.scalar_tensor_tensor(to[:, k, :], src[:, k, :], gain[:, k:k + 1], r, ALU.mult,
                                           ALU.mult).then_inc(s["normed"], 1)

            split_n = [0]

            split_n = [0]

            def low_input(low, whole, high):
                split_n[0] += 1
                dve.wait_ge(s["h_hi"], split_n[0])
                V.tensor_tensor(low, whole, high, ALU.subtract).then_inc(s["normed"], 1)

            def norm_split(gain, shift=None, to=hf, src=x, r=rstd[:, :], parts=(hf_hi, hf_lo)):
                for k in range(KB + 1):
                    if k < KB:
                        V.scalar_tensor_tensor(to[:, k, :], src[:, k, :], gain[:, k:k + 1], r, ALU.mult,
                                               ALU.mult).then_inc(s["h_f"], 1)
                    if k > 0:
                        high, low, whole = parts[0][:, k - 1, :], parts[1][:, k - 1, :], to[:, k - 1, :]
                        if shift is None:
                            low_input(low, whole, high)
                        else:
                            split_n[0] += 1
                            dve.wait_ge(s["h_hi"], split_n[0])
                            V.scalar_tensor_tensor(low, whole, shift[:, k - 1:k], high, ALU.add,
                                                   ALU.subtract).then_inc(s["normed"], 1)

            def rooted():
                norms_done[0] += 1
                dve.wait_ge(s["root"], norms_done[0])

            def low_up(name, i, u, c):
                dve.wait_ge(s["w_hi"], 4 * i + PIECE[name] + 2 * u + c + 1)
                w = w_of[name][c]
                V.tensor_tensor(w[:, 1], slot_view(SLOT[name] + u)[:, c * KB:c * KB + KB, :], w[:, 0],
                                ALU.subtract).then_inc(s["w_lo"], 1)

            def low_down(name, i, m, half):
                dve.wait_ge(s["w_hi"], 4 * i + PIECE[name] + 2 * m + half + 1)
                w = w_down[half]
                V.tensor_tensor(w[:, 1], slot_view(SLOT[name] + half, HALF), w[:, 0],
                                ALU.subtract).then_inc(s["w_lo"], 1)

            norms_done = [0]
            dve.wait_ge(s["vec_in"], 16)
            mean_square(rstd_c[:, :], banks[0], TC)
            mean_square(rstd[:, :], banks[1], TX)
            dve.wait_ge(s["ada_turned"], 1)
            V.tensor_tensor(mod[:, 0:16, :], banks[3][:, 0:32].rearrange("p (m c) -> p m c", c=2),
                            spread(vcol("adab")[:, 0:16], 16, 2), ALU.add).then_inc(s["mod"], 1)
            dve.wait_ge(s["mod"], 1)
            for c in range(2):
                steps.do(V.scalar_tensor_tensor(gains[:, c, :], mod[:, 8:16, c], 1.0, vcol("n1"), ALU.add,
                                                ALU.mult))
            steps.last()
            for c in range(2):
                low_up("W_IN", 0, 0, c)
            rooted()
            rooted()
            norm_split(gains[:, 0], mod[:, 0:8, 0], h, x, rstd[:, :], hx)
            norm_split(gains[:, 1], mod[:, 0:8, 1], hc, ctx_sb, rstd_c[:, :], hc_)

            def low_pieces(name, n):
                def slot(i, u):
                    for c in range(2):
                        low_up(name, i, u, c)

                slot(0, 1)
                with dve.Fori(1, n // 2) as i:
                    slot(i, 0)
                    slot(i, 1)
                slot(n // 2, 0)

            low_pieces("W_IN", 13)

            for j in range(NJ):
                dve.wait_ge(s["head_sum"], j + 1)
                steps.do(V.tensor_scalar(kk[:, j, TC:TT], banks[2 * j][:, 0:TX], 1e-24, None, ALU.max))
                steps.do(V.tensor_scalar(kk[:, j, 0:TC], banks[2 * j + 1][:, 0:TC], 1e-24, None, ALU.max))
                steps.last()
                V.reciprocal(kk[:, j, :], kk[:, j, :]).then_inc(s["head_rec"], 1)
            for j in range(NJ):
                dve.wait_ge(s["head_root"], j + 1)
                V.scalar_tensor_tensor(kk[:, j, :], kT[:, j, :], vcol("kk")[:, j:j + 1], kk[:, j, :], ALU.mult,
                                       ALU.mult).then_inc(s["kk_ready"], 1)
            cw = vcol("conva", 3, 4)
            cb, u_, t_ = px[:, 0:4], px[:, 4:8], px[:, 8:12]
            steps.do(V.tensor_tensor(u_, u_, t_, ALU.mult))
            steps.last()
            for j in range(4):
                steps.do(V.tensor_scalar(t_[:, j, :], u_[:, j, :], cw[:, 1, j:j + 1], None, ALU.mult))
            steps.last()
            for j in range(4):
                steps.do(V.scalar_tensor_tensor(t_[:, j, 1:TX], u_[:, j, 0:TX - 1], cw[:, 0, j:j + 1],
                                                t_[:, j, 1:TX], ALU.mult, ALU.add))
            steps.last()
            for j in range(4):
                steps.do(V.scalar_tensor_tensor(t_[:, j, 0:TX - 1], u_[:, j, 1:TX], cw[:, 2, j:j + 1],
                                                t_[:, j, 0:TX - 1], ALU.mult, ALU.add))
            steps.last()
            V.tensor_tensor(cb, cb, t_, ALU.mult).then_inc(s["conv_ready"], 1)
            dve.wait_ge(s["conv_ready"], 1)

            bank = [banks[0:4], banks[4:8]]

            def heads(b):
                return b[:, :].rearrange("p (h t) -> p h t", h=GH)

            def flat(a):
                return a.rearrange("p a b -> p (a b)")

            def over(mask):
                return mask.unsqueeze(1).broadcast_to([P, GH, L])

            def done(name, d, n, per=1, at=0):
                dve.wait_ge(s[f"{name}{d}"], per * n + (at or per))

            def group(a, g):
                return a[:, GP * g:GP * g + GP]

            def last_of(a, d):
                return a[:, :, L - 1 if d == 0 else 0]

            def gate_bias(n, g):
                for d, sc in enumerate(scans):
                    done("z_mm", d, n)
                    for k in range(2):
                        bias = spread(vcol("wa0", 2, 2, NJ)[:, d, k, GP * g:GP * g + GP], GP, L)
                        ins = V.tensor_tensor(sc.gate[:, k], heads(bank[d][0])[:, GP * k:GP * k + GP, :], bias,
                                              ALU.add)
                    ins.then_inc(s[f"z_biased{d}"], 1)

            def gates(n, g):
                for d, sc in enumerate(scans):
                    done("z_tanh", d, n)
                    steps.do(V.tensor_scalar(sc.gate[:, 0], sc.gate[:, 0], -DECAY / 2, -DECAY / 2, ALU.mult, ALU.add))
                    steps.do(V.tensor_scalar(sc.gate[:, 1], sc.gate[:, 1], 0.5, 0.5, ALU.mult, ALU.add))

            def running_sums(n, g):
                steps.last()
                for d, sc in enumerate(scans):
                    if not (isinstance(n, int) and n == 0):
                        done("tok_mm", d, n - 1, 2, 1)
                    to, gate, r = flat(sc.cum), flat(sc.gate[:, 0]), reset[:, d, :]
                    if d == 1:
                        to, gate, r = to[:, ::-1], gate[:, ::-1], r[:, ::-1]
                    steps.do(V.tensor_tensor_scan(to, r, gate, 0.0, ALU.mult, ALU.add))
                    steps.do(V.scalar_tensor_tensor(sc.kh, sc.gate[:, 1], -1.0,
                                                    spread(group(vcol("ka"), g), GP, L), ALU.add, ALU.mult))

            def centre(n, g):
                steps.last()
                for d, sc in enumerate(scans):
                    at = bass.ds(chunk_at(d, n_place[0], n_place[1]), L)
                    steps.do(V.tensor_scalar(sc.half, last_of(sc.cum, d), -0.5, None, ALU.mult))
                    steps.do(V.scalar_tensor_tensor(sc.kh, sc.kh, 1.0, group(kT, g)[:, :, at], ALU.add, ALU.mult))
                    steps.do(V.tensor_tensor(sc.gate[:, 1], sc.gate[:, 1], group(kk, g)[:, :, at], ALU.mult))
                steps.last()
                for d, sc in enumerate(scans):
                    steps.do(V.tensor_tensor(sc.cum, sc.cum, spread(sc.half, GP, L), ALU.add))
                steps.last()
                for d, sc in enumerate(scans):
                    V.tensor_tensor(sc.gate[:, 0], sc.cum, sc.gate[:, 0], ALU.subtract).then_inc(s[f"decays{d}"], 1)

            def keys(n, g):
                for d, sc in enumerate(scans):
                    at = bass.ds(chunk_at(d, n_place[0], n_place[1]), L)
                    done("exps", d, n, 3)
                    V.tensor_tensor(sc.kt, group(kk, g)[:, :, at], sc.gate[:, 0], ALU.mult).then_inc(s[f"keys{d}"], 1)
                    V.tensor_tensor(sc.bh, sc.gate[:, 1], sc.cum, ALU.mult).then_inc(s[f"keys{d}"], 1)
                    V.tensor_tensor(sc.kh, sc.kh, sc.cum, ALU.mult).then_inc(s[f"keys{d}"], 1)

            def keys_r(n, g, cur):
                for d, sc in enumerate(scans):
                    ax = bass.ds(chunk_at(d, n_place[0], True) - TC, L)
                    if cur:
                        dve.wait_ge(s[f"early_mm{d}"], n - NCC)
                    V.tensor_tensor(sc.rt, group(rT, g)[:, :, ax], sc.pin, ALU.mult).then_inc(s[f"rt{d}"], 1)

            def first_level(n, d):
                sc = scans[d]
                done("a_mm", d, n)
                steps.do(V.scalar_tensor_tensor(sc.X, heads(bank[d][3]), -1.0, over(level[:, d, 0]), ALU.mult,
                                                ALU.mult))
                steps.last()
                V.tensor_tensor(sc.X, sc.X, over(ident), ALU.add).then_inc(s[f"X{d}"], 1)

            def k_scores(n, d):
                done("m_mm", d, n, 2)
                V.tensor_tensor(scans[d].ak, heads(bank[d][0]), over(strict[:, d]), ALU.mult).then_inc(s[f"ak{d}"], 1)

            def r_scores(n, d, k):
                sc = scans[d]
                dve.wait_ge(s[f"r_mm{d}"], 2 * (n - NCC) + k + 1)
                V.tensor_tensor((sc.rb, sc.rk)[k], heads(bank[d][2]), over(incl[:, d]),
                                ALU.mult).then_inc(s[f"r_out{d}"], 1)

            def state_decayed(g):
                for d, sc in enumerate(scans):
                    steps.do(V.tensor_copy(sc.decay, last_of(sc.pin, d)))
                    V.tensor_tensor(sc.S_in, sc.S[:, g], spread(last_of(sc.pin, d), GP, HD),
                                    ALU.mult).then_inc(s[f"S_in{d}"], 1)

            def w_out(n, d, l):
                done("nx_mm", d, n, LEVELS - 1, l - 1)
                V.tensor_tensor(scans[d].w, heads(bank[d][3]), over(level[:, d, l - 1]),
                                ALU.mult).then_inc(s[f"w{d}"], 1)

            def x_out(n, d, l):
                done("dx_mm", d, n, LEVELS - 1, l - 1)
                V.tensor_tensor(scans[d].X, heads(bank[d][3]), scans[d].X, ALU.add).then_inc(s[f"X{d}"], 1)

            n_place = [0, False]

            def prepare():
                for step in (gate_bias, gates, running_sums, centre, keys):
                    step(0, 0)
                state_decayed(0)
                for d in range(2):
                    first_level(0, d)
                for d in range(2):
                    k_scores(0, d)

            def turn(n, c, g, cur, nxt):
                n_place[:] = c + g, nxt
                for l in range(2, LEVELS + 1):
                    w_out(n, 0, l)
                    if nxt is not None:
                        if l == 2:
                            gate_bias(n + 1, 1 - g)
                        elif l == 4:
                            running_sums(n + 1, 1 - g)
                        elif l == 6:
                            keys(n + 1, 1 - g)
                    x_out(n, 0, l)
                    w_out(n, 1, l)
                    if nxt is not None:
                        if l == 3:
                            gates(n + 1, 1 - g)
                        elif l == 4:
                            centre(n + 1, 1 - g)
                        elif l == 6 and nxt:
                            keys_r(n + 1, 1 - g, cur)
                    x_out(n, 1, l)
                if nxt is not None:
                    for d in range(2):
                        first_level(n + 1, d)
                if not cur:
                    dve.wait_ge(s["ada_turned"], 2 + n)
                    V.tensor_tensor(mod[:, 16 + 8 * n:24 + 8 * n, :],
                                    banks[2][:, 0:16].rearrange("p (m c) -> p m c", c=2),
                                    spread(vcol("adab")[:, 16 + 8 * n:24 + 8 * n], 8, 2),
                                    ALU.add).then_inc(s["mod"], 1)
                for d, sc in enumerate(scans):
                    done("ds_mm", d, n)
                    if cur:
                        y = group(y_dir[d], g)[:, :, bass.ds(chunk_at(d, c, True) - TC, L)]
                        V.tensor_tensor(y, heads(bank[d][2])[:, 0:GP, :], y, ALU.add).then_inc(s[f"y_out{d}"], 1)
                    if nxt is not None:
                        steps.do(V.tensor_tensor(sc.S[:, g], bank[d][2][:, 256:256 + GP * HD].rearrange(
                            "p (j f) -> p j f", j=GP), sc.S_in, ALU.add))
                        steps.last()
                        V.tensor_tensor(sc.S[:, g], sc.S[:, g], spread(sc.decay, GP, HD),
                                        ALU.mult).then_inc(s[f"S{d}"], 1)
                        k_scores(n + 1, d)
                if nxt is not None:
                    for d in range(2):
                        done("S", d, n)
                    state_decayed(1 - g)
                if nxt:
                    for k in range(2):
                        for d in range(2):
                            r_scores(n + 1, d, k)

            dve.wait_ge(s["bd_clean"], 2)
            all_turns(dve, prepare, turn, steps, 44)

            for d in range(2):
                dve.wait_ge(s[f"y_out{d}"], NCX)
            for j in range(NJ):
                V.tensor_tensor(ys[:, j, :], y_dir[0][:, j, :], y_dir[1][:, j, :], ALU.add).then_inc(s["y_rkr"], 1)
                V.scalar_tensor_tensor(rkr[:, j, :], rT[:, j, :], vcol("rk")[:, j:j + 1], kT[:, j, TC:TT], ALU.mult,
                                       ALU.mult).then_inc(s["y_rkr"], 1)
            for j in range(NJ):
                dve.wait_ge(s["y_rkr_mm"], 2 * j + 1)
                V.scalar_tensor_tensor(yc[:, j, :], banks[j][:, :], -1.0 / HD, ys[:, j, :], ALU.mult,
                                       ALU.add).then_inc(s["centred_bonus"], 1)
                dve.wait_ge(s["y_rkr_mm"], 2 * j + 2)
                V.tensor_tensor(bonus[:, j, :], banks[4 + j][:, :], vT[:, j, TC:TT], ALU.mult).then_inc(s["centred_bonus"], 1)
            for j in range(NJ):
                dve.wait_ge(s["head_sum"], NJ + j + 1)
                steps.do(V.tensor_scalar(yr[:, j, :], banks[j][:, :], 1.0 / HD, GN_EPS, ALU.mult, ALU.add))
                steps.last()
                V.reciprocal(yr[:, j, :], yr[:, j, :]).then_inc(s["head_rec"], 1)
            for j in range(NJ):
                dve.wait_ge(s["head_root"], NJ + j + 1)
                steps.do(V.scalar_tensor_tensor(yc[:, j, :], yc[:, j, :], vcol("lng")[:, j:j + 1], yr[:, j, :],
                                                ALU.mult, ALU.mult))
                steps.last()
                steps.do(V.scalar_tensor_tensor(yc[:, j, :], yc[:, j, :], vcol("lnb")[:, j:j + 1], bonus[:, j, :],
                                                ALU.add, ALU.add))
                steps.last()
                dve.wait_ge(s["gate_mm"], j + 1)
                V.tensor_tensor(y_rwkv[:, j, :], banks[4 + j][:, :], yc[:, j, :], ALU.mult).then_inc(s["mixed"], 1)
            for c in range(2):
                low_up("W_OUT", 0, 0, c)
            for j in range(4):
                low_input(ycv[1][:, j, :], y_conv[:, j, :], ycv[0][:, j, :])
            for j in range(NJ):
                low_input(yrw[1][:, j, :], y_rwkv[:, j, :], yrw[0][:, j, :])

            def residual_tile(p0, p, m, bank, gate):
                dve.wait_ge(s["product"], p0 + p)
                xm = x[:, m, :] if isinstance(m, int) else x[:, bass.ds(m, 1), :].rearrange("p a t -> p (a t)")
                if gate is None:
                    V.tensor_tensor(xm, bank[:, :], xm, ALU.add).then_inc(s["taken"], 1)
                else:
                    V.scalar_tensor_tensor(xm, bank[:, :], mod[:, bass.ds(gate + m, 1), 0], xm, ALU.mult,
                                           ALU.add).then_inc(s["taken"], 1)

            def residual(name, gate=None):
                p0 = DONE[SLOT[name] - 1]
                for j in range(4):
                    for c in range(2):
                        if j < 3:
                            low_up(name, (j + 1) // 2, (j + 1) % 2, c)
                        residual_tile(p0 + 2 * j + c + 1, 0, 2 * j + c, banks[(2 * j + c) % 4], gate)

            residual("W_OUT", gate=2 * KB)
            steps.do(V.scalar_tensor_tensor(gain2[:, :], mod[:, 4 * KB:5 * KB, 0], 1.0, vcol("n2"), ALU.add,
                                            ALU.mult))
            steps.last()
            mean_square(rstd[:, :], banks[6], TX)
            for c in range(2):
                low_up("UP1", 0, 0, c)
            rooted()
            norm_split(gain2, mod[:, 3 * KB:4 * KB, 0])

            def ffn(first, up, down, taps, per, gate=None):
                p0 = DONE[SLOT[up] - 1]

                def body(i, u, last=False):
                    if not last:
                        low_up(up, i + u, 1 - u, 0)
                    dve.wait_ge(s["gate_in"], first + 2 * i + u + 1)
                    if not (isinstance(i, int) and i == 0 and first == 0):
                        dve.wait_ge(s["silu"], first + 2 * i + u - 1)
                    taps(i, u)
                    if not last:
                        low_up(up, i + u, 1 - u, 1)
                    dve.wait_ge(s["silu"], first + 2 * i + u + 1)
                    dve.wait_ge(s["product"], p0 + 4 * i + 2 * u + 2)
                    V.tensor_tensor(silu[u], silu[u], banks[2 * u + 1][:, :], ALU.mult).then_inc(s["val_free"], 1)

                body(0, 0)
                body(0, 1)
                turns = FB // 2 - 2
                with dve.Fori(1, FB // 2 - 1) as i:
                    steps.loop(i - 1, 2 * per)
                    body(i, 0)
                    body(i, 1)
                    steps.end(turns)
                body(FB // 2 - 1, 0)
                body(FB // 2 - 1, 1, last=True)

                p1 = DONE[SLOT[down] - 1]

                def tile(i, m, last=False):
                    if not last:
                        low_down(down, i + m, 1 - m, 0)
                    residual_tile(p1 + 2 * m + 2, 4 * i, 2 * i + m, banks[m], gate)
                    if not last:
                        low_down(down, i + m, 1 - m, 1)

                low_down(down, 0, 0, 0)
                low_down(down, 0, 0, 1)
                with dve.Fori(0, KB // 2 - 1) as i:
                    tile(i, 0)
                    tile(i, 1)
                tile(KB // 2 - 1, 0)
                tile(KB // 2 - 1, 1, last=True)

            def taps_grid(i, u):
                f0 = VEC["fcw"][0] + 10 * (2 * i + u)
                to = conv[u].rearrange("p (y x) -> p y x", y=GRID_H)
                steps.do(V.tensor_scalar(to, pad[u][:, 0:GRID_H, 0:GRID_W], v[:, bass.ds(f0, 1)],
                                         v[:, bass.ds(f0 + 9, 1)], ALU.mult, ALU.add))
                for n in range(1, 9):
                    steps.last()
                    ins = V.scalar_tensor_tensor(to, pad[u][:, n // 3:n // 3 + GRID_H, n % 3:n % 3 + GRID_W],
                                                 v[:, bass.ds(f0 + n, 1)], to, ALU.mult, ALU.add)
                    if n < 8:
                        steps.do(ins)
                ins.then_inc(s["conv"], 1)

            def taps_causal(i, u):
                f0 = VEC["cw2"][0] + 4 * (2 * i + u)
                steps.do(V.tensor_scalar(conv[u], pad1[u][:, 0:TX], v[:, bass.ds(f0, 1)], v[:, bass.ds(f0 + 3, 1)],
                                         ALU.mult, ALU.add))
                for n in range(1, 3):
                    steps.last()
                    ins = V.scalar_tensor_tensor(conv[u], pad1[u][:, n:n + TX], v[:, bass.ds(f0 + n, 1)], conv[u],
                                                 ALU.mult, ALU.add)
                    if n < 2:
                        steps.do(ins)
                ins.then_inc(s["conv"], 1)

            ffn(0, "UP1", "DOWN1", taps_grid, 8, gate=5 * KB)
            mean_square(rstd[:, :], banks[6], TX)
            norm(x, x, rstd[:, :], vcol("fin"))

            lb = vcol("lb", 2, 4)
            V.tensor_tensor(lbv, lb[:, 0], lb[:, 1], ALU.subtract).then_inc(s["lb"], 1)
            mean_square(rstd[:, :], banks[7], TX)
            for c in range(2):
                low_up("W_IN2", 0, 0, c)
            rooted()
            norm_split(vcol("nmix"), to=h, parts=h2)
            low_pieces("W_IN2", 11)
            dve.wait_ge(s["forget"], 1)
            steps.do(V.tensor_scalar(oml, lbv, -1.0, 1.0, ALU.mult, ALU.add))
            steps.last()
            dve.wait_ge(s["taken"], 73)
            for hd in range(NH):
                dve.wait_ge(s["forget"], hd + 2)
                src = pr[:, 4 + hd, :].rearrange("p (n t) -> p n t", n=NB)
                V.tensor_scalar(cumf[:, :, hd, :], src, oml[:, hd:hd + 1], lbv[:, hd:hd + 1], ALU.mult,
                                ALU.add).then_inc(s["f"], 1)
            for hd in range(NH):
                dve.wait_ge(s["f"], hd + 1)
                V.tensor_scalar(kh[:, :, hd, :], cumf[:, :, hd, :], -1.0, 1.0, ALU.mult,
                                ALU.add).then_inc(s["keys_hg"], 1)
                V.tensor_scalar(qh[:, :, hd, :], pr[:, hd, :].rearrange("p (n t) -> p n t", n=NB), HC ** -0.5, None,
                                ALU.mult).then_inc(s["q_hg"], 1)
            cf2 = cumf.rearrange("p n h t -> p (n h t)")
            dve.wait_ge(s["cum_f"], NH)
            dve.wait_ge(s["pads2"], 5)
            V.tensor_tensor_scan(cf2, hreset.rearrange("p n h t -> p (n h t)"), cf2, 0.0, ALU.mult,
                                 ALU.add).then_inc(s["cum_scan"], 1)
            dve.wait_ge(s["cum_scan"], 1)
            dve.wait_ge(s["masks_in"], 16)

            def mixer2(i):
                first = isinstance(i, int) and i == 0
                chunk = bass.ds(NH * HC * i, NH * HC)
                cf, kf, qf = (a.rearrange("p n h t -> p (n h t)")[:, chunk] for a in (cumf, kh, qh))
                dve.wait_ge(s["a_s_mm"], i + 1)
                if not first:
                    dve.wait_ge(s["a_t_mm"], 4 * i)
                mask = band_sb[:, bass.ds(i, 1), :].broadcast_to([P, 2, 2 * HC])
                for j in range(4):
                    steps.do(V.scalar_tensor_tensor(pp[:, 2 * j:2 * j + 2, :],
                                                    banks[4 + j][:, :].rearrange("p (g k) -> p g k", g=2), 0.125,
                                                    mask, ALU.mult, ALU.add))
                steps.last()
                steps.do(V.tensor_reduce(hi, pp, AX.X, ALU.max))
                steps.last()
                steps.do(V.tensor_tensor(hi, hi, sink_order, ALU.max))
                steps.last()
                V.tensor_scalar(nm, hi, -1.0, None, ALU.mult).then_inc(s["a_nm"], 1)
                V.tensor_tensor(dsk, sink_order, hi, ALU.subtract).then_inc(s["a_ds"], 1)

                def halves(a, l):
                    w = a.rearrange("p (b t) -> p b t", t=1 << l)
                    return w[:, :, 0:1 << l - 1], w[:, :, 1 << l - 1:1 << l]

                def decay(l):
                    nb = NH * HC >> l
                    early, late = halves(cf, l)
                    mid = early[:, :, (1 << l - 1) - 1:1 << l - 1].broadcast_to([P, nb, 1 << l - 1])
                    de_early, de_late = halves(de[l % 2], l)
                    V.tensor_tensor(de_early, mid, early, ALU.subtract).then_inc(s["h_d"], 1)
                    V.tensor_tensor(de_late, late, mid, ALU.subtract).then_inc(s["h_d"], 1)

                def scale(l):
                    dve.wait_ge(s["h_e"], HLEV * i + l)
                    if not first or l > 2:
                        dve.wait_ge(s["h_mm"], 8 * i + l - 2)
                    z, e = halves(zz[l % 2], l), halves(de[l % 2], l)
                    V.tensor_tensor(z[0], e[0], halves(kf, l)[0], ALU.mult).then_inc(s["h_z"], 1)
                    if l > 1:
                        dve.wait_ge(s["h_mm"], 8 * i + l - 1)
                    V.tensor_tensor(z[1], e[1], halves(qf, l)[1], ALU.mult).then_inc(s["h_z"], 1)

                def pick(l):
                    mask = (level[:, 1, l - 1] if l <= HLEV else ident).unsqueeze(1).broadcast_to([P, NH, HC])
                    bank = banks[l % 2][:, :].rearrange("p (h t) -> p h t", h=NH)
                    if l == 1:
                        if not first:
                            dve.wait_ge(s["h_o_mm"], i)
                        V.tensor_tensor(sT, bank, mask, ALU.mult).then_inc(s["h_s"], 1)
                    else:
                        V.copy_predicated(sT, mask.bitcast(U32), bank).then_inc(s["h_s"], 1)

                decay(1)
                decay(2)
                dve.wait_ge(s["h_ec"], i + 1)
                V.tensor_tensor(qe.rearrange("p h t -> p (h t)"), ec.rearrange("p h t -> p (h t)"), qf,
                                ALU.mult).then_inc(s["h_qe"], 1)
                cw_ = cf.rearrange("p (h t) -> p h t", h=NH)
                V.tensor_tensor(ke, cw_[:, :, HC - 1:HC].broadcast_to([P, NH, HC]), cw_,
                                ALU.subtract).then_inc(s["h_ke"], 1)
                for l in range(1, HLEV + 1):
                    if l > 2:
                        dve.wait_ge(s["h_s"], 8 * i + l - 2)
                    scale(l)
                    if l > 1:
                        pick(l - 1)
                    if l + 2 <= HLEV:
                        dve.wait_ge(s["h_z"], 2 * HLEV * i + 2 * l)
                        decay(l + 2)
                dve.wait_ge(s["h_ke_e"], i + 1)
                dve.wait_ge(s["h_mm"], 8 * i + HLEV)
                dve.wait_ge(s["h_s"], 8 * i + HLEV - 1)
                V.tensor_tensor(ke.rearrange("p h t -> p (h t)"), ke.rearrange("p h t -> p (h t)"), kf,
                                ALU.mult).then_inc(s["h_kend"], 1)
                pick(HLEV)
                dve.wait_ge(s["a_es"], i + 1)
                dve.wait_ge(s["a_p"], NQ * i + NQ)
                dve.wait_ge(s["h_mm"], 8 * i + HLEV + 1)
                dve.wait_ge(s["h_s"], 8 * i + HLEV)
                steps.do(V.tensor_tensor(den, den, esk, ALU.add))
                pick(HLEV + 1)
                steps.last()
                steps.do(V.reciprocal(den, den))
                steps.last()
                V.tensor_tensor(pp, pp, spread(den, NQ, 2 * HC), ALU.mult).then_inc(s["a_pn"], 1)
                dve.wait_ge(s["h_o_mm"], i + 1)
                steps.do(V.tensor_tensor(S2, S2, ec[:, :, HC - 1:HC].broadcast_to([P, NH, HC]), ALU.mult))
                steps.last()
                dve.wait_ge(s["h_ds"], i + 1)
                V.tensor_tensor(S2, banks[3][:, :].rearrange("p (h t) -> p h t", h=NH), S2,
                                ALU.add).then_inc(s["h_S"], 1)

            sink_order = vcol("sinks")
            dve.wait_ge(s["pads2"], 6)
            mixer2(0)
            with dve.Fori(1, NB) as i:
                steps.loop(i - 1, 9)
                mixer2(i)
                steps.end(NB - 1)
            for hd in range(NH):
                dve.wait_ge(s["head_sum"], 2 * NJ + hd + 1)
                steps.do(V.tensor_scalar(yr2[:, hd, :], banks[hd][:, :], 1.0 / HC, EPS, ALU.mult, ALU.add))
                steps.last()
                V.reciprocal(yr2[:, hd, :], yr2[:, hd, :]).then_inc(s["head_rec"], 1)
            for hd in range(NH):
                dve.wait_ge(s["head_root"], 2 * NJ + hd + 1)
                steps.do(V.scalar_tensor_tensor(mix[:, hd, :], mix[:, hd, :], vcol("hgn"), yr2[:, hd, :], ALU.mult,
                                                ALU.mult))
            steps.last()
            for hd in range(NH):
                V.tensor_tensor(mix[:, hd, :], mix[:, hd, :], pr[:, 12 + hd, :], ALU.mult).then_inc(s["mix2"], 1)
            for c in range(2):
                low_up("W_OUT2", 0, 0, c)
            for k in (4, 5, 6, 7, 0, 1, 2, 3):
                low_input(mx[1][:, k, :], mix[:, k, :], mx[0][:, k, :])
            residual("W_OUT2")
            mean_square(rstd[:, :], banks[6], TX)
            for c in range(2):
                low_up("UP2", 0, 0, c)
            rooted()
            norm_split(vcol("nffn"))
            ffn(FB, "UP2", "DOWN2", taps_causal, 2)
            mean_square(rstd[:, :], banks[6], TX)
            norm(x, x, rstd[:, :], vcol("fin2"))


def _tiles(w, blocks=KB):
    k, m = w.shape
    t = w.reshape(k // P, P, m // P, P).transpose(2, 1, 0, 3)
    return t.reshape(m // P, P, k)


def _halves(w):
    t = _tiles(w).reshape(D // P, P, 2, HALF * P)
    return t.transpose(0, 2, 1, 3).reshape(2 * D // P, P, HALF * P)


def _columns(v):
    return v.reshape(-1, P).T


def _arrange(a):
    g = {n: np.asarray(v) for n, v in a.items()}
    dc = D // 2
    w_in = g["w_in"][0]
    w_in = np.concatenate([w_in[:, :4 * dc], w_in[:, 6 * dc + 128:], w_in[:, 4 * dc:6 * dc + 128]], axis=1)
    up1 = g["ffn_w_up"][0].reshape(D, 2, FB, P).transpose(0, 2, 1, 3).reshape(D, 2 * DFF)
    up2 = np.stack([g["w_gate_2"][0].reshape(D, FB, P), g["w_up_2"][0].reshape(D, FB, P)], axis=2).reshape(D, 2 * DFF)
    head = np.concatenate([np.arange(64) + 64 * h for j in range(4) for h in (j, j + 4)])
    w_in2 = g["w_in_2"][0]
    w_in2 = np.concatenate([w_in2[:, :2048], w_in2[:, 2048 + head], w_in2[:, 2560:]], axis=1)
    w_out2 = g["w_out_2"][0]
    w_out2 = np.concatenate([w_out2[:512], w_out2[512 + head]], axis=0)
    batt = g["b_attn_2"][0]
    batt = np.concatenate([batt[head], batt[512:]])
    ada = _tiles(g["ada_w"][0])
    w8 = np.concatenate([ada[:16], _tiles(w_in), ada[16:], _tiles(g["w_out"][0]), _tiles(up1),
                         _tiles(w_in2), _tiles(w_out2), _tiles(up2)])
    w11 = np.concatenate([_halves(g["ffn_w_down"][0]), _halves(g["w_down_2"][0])])
    lora = np.zeros((P, 2, 2, 4, P), np.float32)
    for d in range(2):
        lora[:64, d, 0] = g["rw_w_up"][0, d].reshape(64, 4, P)
        lora[64:, d, 1] = g["rw_a_up"][0, d].reshape(64, 4, P)
    vec = np.zeros((P, NVEC), np.float32)

    def put(name, v):
        o, w = VEC[name]
        vec[:, o:o + w] = v.reshape(P, w)

    put("n1", _columns(g["norm1_g"]))
    put("n2", _columns(g["norm2_g"]))
    put("fin", _columns(g["final_g"]))
    put("cs", np.stack([_columns(g["c"]), _columns(g["c_ctx"])], axis=2))
    put("adab", _columns(g["ada_b"]))
    put("conva", _columns(g["conv_a_w"]))
    put("wa0", np.concatenate([_columns(g[n][0, d]) for d in range(2) for n in ("rw_w0", "rw_a0")], axis=1))
    put("kk", _columns(g["rw_k_k"]))
    put("ka", _columns(g["rw_k_a"]))
    put("rk", _columns(g["rw_r_k"]))
    put("lng", _columns(g["rw_ln_g"]))
    put("lnb", _columns(g["rw_ln_b"]))
    fcw = np.concatenate([g["ffn_conv_w"].reshape(9, FB, P), g["ffn_conv_b"].reshape(1, FB, P)])
    put("fcw", fcw.transpose(2, 1, 0))
    put("nmix", _columns(g["norm_mix_w_2"]))
    put("nffn", _columns(g["norm_ffn_w_2"]))
    put("batt", _columns(batt))
    put("lb", _columns(g["lb_logits_2"]))
    put("hgn", _columns(g["hg_norm_w_2"]))
    sinks = g["sinks_2"][0][[h for j in range(4) for h in (j, j + 4)]]
    put("sinks", np.broadcast_to(sinks, (P, NQ)))
    cw2 = np.concatenate([g["conv_w_2"].reshape(3, FB, P), g["conv_b_2"].reshape(1, FB, P)])
    put("cw2", cw2.transpose(2, 1, 0))
    put("fin2", _columns(g["final_norm_w_2"]))

    def features(x):
        return np.ascontiguousarray(x.T.reshape(KB, P, -1).transpose(1, 0, 2))

    return {
        "xT": features(g["x"][0]), "ctxT": features(g["ctx"][0]), "vec": vec, "con": constants(),
        "band": band_masks(), "w8": w8, "w11": w11,
        "lora": lora.reshape(P, 16 * P), "gup": np.ascontiguousarray(g["rw_g_up"][0]),
    }


def kernel(**inputs):
    import concourse.bacc as _bacc
    from concourse.bass_utils import run_bass_kernel_spmd as _run

    nc = _bacc.Bacc("TRN2", target_bir_lowering=False, num_devices=1)
    arrays = {n: np.ascontiguousarray(a) for n, a in _arrange(inputs).items()}
    args = {n: nc.dram_tensor(n, a.shape, mybir.dt.from_np(a.dtype), kind="ExternalInput").ap()
            for n, a in arrays.items()}
    out = nc.dram_tensor("outT", (P, KB, TX), F32, kind="ExternalOutput").ap()
    two_blocks(nc, outT=out, **args)
    r = _run(nc, [arrays], core_ids=[0])
    got = r.results[0]["outT"]
    return got.transpose(2, 1, 0).reshape(1, TX, D)
```
